# Optimizing a Trainium2 kernel written in Bass

```python
import math
import jax
import jax.numpy as jnp
from jax import lax
import numpy as np
import jax, jax.numpy as jnp

D_MODEL = 2048
BATCH = 1
SEQ = 256
DEPTH = 1

GRID_W = 64
CTX_LEN = 256
HEAD_DIM = 128
N_GROUPS = 4
HEADS_PER_GROUP = D_MODEL // (N_GROUPS * HEAD_DIM)
D_MIX = N_GROUPS * HEADS_PER_GROUP * HEAD_DIM
Q_BLOCK = 128
ROPE_THETA = 10000.0
EPS = 1e-6
NA_KH_MAX = 8
NA_KW = 16
GQA_KV_HEADS = 2
MLA_Q_RANK = 512
MLA_KV_RANK = 256
MLA_NOPE = 128
MLA_ROPE = 64
MLA_V = 128
DIFF_D = 64
D_FF = -(-8 * D_MODEL // (3 * 256)) * 256

IN_SPLITS = (
    HEADS_PER_GROUP * HEAD_DIM, HEADS_PER_GROUP * HEAD_DIM, HEADS_PER_GROUP * HEAD_DIM,
    HEADS_PER_GROUP * HEAD_DIM, GQA_KV_HEADS * HEAD_DIM, GQA_KV_HEADS * HEAD_DIM,
    MLA_Q_RANK, MLA_KV_RANK, MLA_ROPE,
    HEADS_PER_GROUP * 2 * DIFF_D, HEADS_PER_GROUP * 2 * DIFF_D, HEADS_PER_GROUP * 2 * DIFF_D,
)
D_IN = sum(IN_SPLITS)


def rms_norm(x, g):
    xf = x.astype(jnp.float32)
    y = xf * lax.rsqrt(jnp.mean(xf * xf, axis=-1, keepdims=True) + EPS)
    return y.astype(x.dtype) * g

def axial_rope(n_tokens, dim):
    t = jnp.arange(n_tokens, dtype=jnp.int32)
    row = (t // GRID_W).astype(jnp.float32)
    col = (t % GRID_W).astype(jnp.float32)
    d_axis = dim // 2
    inv = 1.0 / (ROPE_THETA ** (jnp.arange(0, d_axis, 2, dtype=jnp.float32) / d_axis))
    ang = jnp.concatenate([row[:, None] * inv, col[:, None] * inv], axis=-1)
    return jnp.cos(ang), jnp.sin(ang)

def apply_rope(x, cos, sin):
    x1, x2 = jnp.split(x, 2, axis=-1)
    return jnp.concatenate([x1 * cos - x2 * sin, x1 * sin + x2 * cos], axis=-1).astype(x.dtype)

def to_heads(a, n_heads):
    b, t, _ = a.shape
    return a.reshape(b, t, n_heads, -1).transpose(0, 2, 1, 3)

def over_query_blocks(fn, q):
    *lead, s, d = q.shape
    nb = s // Q_BLOCK
    qb = jnp.moveaxis(q.reshape(*lead, nb, Q_BLOCK, d), -3, 0)
    out = lax.map(fn, qb)
    out = jnp.moveaxis(out, 0, -3)
    return out.reshape(*out.shape[:-3], s, out.shape[-1])

def softmax_attend(q, k, v, scale):
    s = jnp.einsum('bkgqd,bktd->bkgqt', q, k).astype(jnp.float32) * scale
    p = jax.nn.softmax(s, axis=-1).astype(v.dtype)
    return jnp.einsum('bkgqt,bktd->bkgqd', p, v)

def neighbourhood_attention(q, k, v, k_ctx, v_ctx, rpb):
    b, h, s, d = q.shape
    rows = s // GRID_W
    kh = min(NA_KH_MAX, rows)
    scale = d ** -0.5
    qg = q.reshape(b, h, rows, GRID_W, d)
    kg = k.reshape(b, h, rows, GRID_W, d)
    vg = v.reshape(b, h, rows, GRID_W, d)
    cols = np.arange(GRID_W)
    c_start = np.clip(cols - NA_KW // 2, 0, GRID_W - NA_KW)
    col_idx = c_start[:, None] + np.arange(NA_KW)[None, :]
    dc_idx = col_idx - cols[:, None] + (NA_KW - 1)
    col_bias = rpb[:, :, dc_idx]
    n_win = kh * NA_KW

    def row_block(r):
        r_start = jnp.clip(r - kh // 2, 0, rows - kh)
        q_r = lax.dynamic_index_in_dim(qg, r, axis=2, keepdims=False)
        k_win = lax.dynamic_slice_in_dim(kg, r_start, kh, axis=2)[:, :, :, col_idx]
        v_win = lax.dynamic_slice_in_dim(vg, r_start, kh, axis=2)[:, :, :, col_idx]
        dr_idx = r_start + jnp.arange(kh) - r + (NA_KH_MAX - 1)
        bias = jnp.take(col_bias, dr_idx, axis=1).transpose(0, 2, 1, 3)
        s_win = jnp.einsum('bhcd,bhicjd->bhcij', q_r, k_win).astype(jnp.float32) * scale + bias.astype(jnp.float32)
        s_ctx = jnp.einsum('bhcd,bhtd->bhct', q_r, k_ctx).astype(jnp.float32) * scale
        p = jax.nn.softmax(jnp.concatenate([s_win.reshape(b, h, GRID_W, n_win), s_ctx], axis=-1), axis=-1).astype(v.dtype)
        p_win = p[..., :n_win].reshape(b, h, GRID_W, kh, NA_KW)
        p_ctx = p[..., n_win:]
        return jnp.einsum('bhcij,bhicjd->bhcd', p_win, v_win) + jnp.einsum('bhct,bhtd->bhcd', p_ctx, v_ctx)

    out = lax.map(row_block, jnp.arange(rows))
    return jnp.moveaxis(out, 0, 2).reshape(b, h, s, d)

def na_mixer(q_l, k_l, v_l, q_c, k_c, v_c, rpb, ctx_out):
    H = HEADS_PER_GROUP
    kc, vc = to_heads(k_c, H), to_heads(v_c, H)
    ol = neighbourhood_attention(to_heads(q_l, H), to_heads(k_l, H), to_heads(v_l, H), kc, vc, rpb)
    oc = None
    if ctx_out:
        oc = softmax_attend(to_heads(q_c, H)[:, :, None], kc, vc, HEAD_DIM ** -0.5)[:, :, 0]
    return ol, oc

def gqa_mixer(q_l, k_l, v_l, q_c, k_c, v_c, g_q, g_k, rope, ctx_out):
    H, KV = HEADS_PER_GROUP, GQA_KV_HEADS
    G = H // KV
    cos, sin = rope
    scale = HEAD_DIM ** -0.5

    def grouped(q):
        b, _, t, d = q.shape
        return q.reshape(b, KV, G, t, d)

    ql = grouped(apply_rope(rms_norm(to_heads(q_l, H), g_q), cos, sin))
    kl = apply_rope(rms_norm(to_heads(k_l, KV), g_k), cos, sin)
    kc = rms_norm(to_heads(k_c, KV), g_k)
    vc = to_heads(v_c, KV)
    k_all = jnp.concatenate([kc, kl], axis=2)
    v_all = jnp.concatenate([vc, to_heads(v_l, KV)], axis=2)
    ol = over_query_blocks(lambda qb: softmax_attend(qb, k_all, v_all, scale), ql)
    b, _, _, s, d = ol.shape
    ol = ol.reshape(b, H, s, d)
    oc = None
    if ctx_out:
        qc = grouped(rms_norm(to_heads(q_c, H), g_q))
        oc = softmax_attend(qc, kc, vc, scale).reshape(b, H, -1, d)
    return ol, oc

def mla_mixer(cq_l, ckv_l, kpe_l, cq_c, ckv_c, kpe_c, g_q, g_kv, w_uq, w_ukv, rope, ctx_out):
    H = HEADS_PER_GROUP
    cos, sin = rope
    scale = (MLA_NOPE + MLA_ROPE) ** -0.5

    def queries(cq, rot):
        q = to_heads(rms_norm(cq, g_q) @ w_uq, H)
        q_nope, q_pe = q[..., :MLA_NOPE], q[..., MLA_NOPE:]
        if rot:
            q_pe = apply_rope(q_pe, cos, sin)
        return jnp.concatenate([q_nope, q_pe], axis=-1)[:, :, None]

    def keys_values(ckv, kpe, rot):
        kv = to_heads(rms_norm(ckv, g_kv) @ w_ukv, H)
        k_nope, v = kv[..., :MLA_NOPE], kv[..., MLA_NOPE:]
        k_pe = kpe[:, None]
        if rot:
            k_pe = apply_rope(k_pe, cos, sin)
        k_pe = jnp.broadcast_to(k_pe, k_nope.shape[:-1] + (MLA_ROPE,))
        return jnp.concatenate([k_nope, k_pe], axis=-1), v

    kl, vl = keys_values(ckv_l, kpe_l, True)
    kc, vc = keys_values(ckv_c, kpe_c, False)
    k_all = jnp.concatenate([kc, kl], axis=2)
    v_all = jnp.concatenate([vc, vl], axis=2)
    ol = over_query_blocks(lambda qb: softmax_attend(qb, k_all, v_all, scale), queries(cq_l, True))[:, :, 0]
    oc = None
    if ctx_out:
        oc = softmax_attend(queries(cq_c, False), kc, vc, scale)[:, :, 0]
    return ol, oc

def diff_mixer(q_l, k_l, v_l, q_c, k_c, v_c, lq1, lk1, lq2, lk2, g_sub, lam_init, rope, ctx_out):
    H = HEADS_PER_GROUP
    cos, sin = rope
    scale = DIFF_D ** -0.5
    f32 = jnp.float32
    lam = (jnp.exp(jnp.sum(lq1.astype(f32) * lk1.astype(f32)))
           - jnp.exp(jnp.sum(lq2.astype(f32) * lk2.astype(f32))) + lam_init)

    def pair_heads(a):
        b, t, _ = a.shape
        return a.reshape(b, t, H, 2, DIFF_D).transpose(0, 2, 3, 1, 4)

    def attend(q, k, v):
        s = jnp.einsum('bhiqd,bhitd->bhiqt', q, k).astype(f32) * scale
        p = jax.nn.softmax(s, axis=-1)
        w = (p[:, :, 0] - lam * p[:, :, 1]).astype(v.dtype)
        return jnp.einsum('bhqt,bhtd->bhqd', w, v)

    def finish(o):
        return rms_norm(o, g_sub) * (1.0 - lam_init)

    ql = apply_rope(pair_heads(q_l), cos, sin)
    kl = apply_rope(pair_heads(k_l), cos, sin)
    kc = pair_heads(k_c)
    vc = to_heads(v_c, H)
    k_all = jnp.concatenate([kc, kl], axis=3)
    v_all = jnp.concatenate([vc, to_heads(v_l, H)], axis=2)
    ol = finish(over_query_blocks(lambda qb: attend(qb, k_all, v_all), ql))
    oc = None
    if ctx_out:
        oc = finish(attend(pair_heads(q_c), kc, vc))
    return ol, oc

def hybrid_mixer(h, hc, w_in, w_out, rpb, gqa_gq, gqa_gk, mla_gq, mla_gkv, mla_wuq, mla_wukv,
                 lq1, lk1, lq2, lk2, g_sub, lam_init, rope128, rope64, ctx_out):
    offsets = np.cumsum(IN_SPLITS)[:-1].tolist()
    pl = jnp.split(h @ w_in, offsets, axis=-1)
    pc = jnp.split(hc @ w_in, offsets, axis=-1)
    oa, oac = na_mixer(*pl[0:3], *pc[0:3], rpb, ctx_out)
    ob, obc = gqa_mixer(*pl[3:6], *pc[3:6], gqa_gq, gqa_gk, rope128, ctx_out)
    oc, occ = mla_mixer(*pl[6:9], *pc[6:9], mla_gq, mla_gkv, mla_wuq, mla_wukv, rope64, ctx_out)
    od, odc = diff_mixer(*pl[9:12], *pc[9:12], lq1, lk1, lq2, lk2, g_sub, lam_init, rope64, ctx_out)

    def merge(parts):
        o = jnp.concatenate(parts, axis=1)
        b, n, t, d = o.shape
        return o.transpose(0, 2, 1, 3).reshape(b, t, n * d) @ w_out

    out_c = merge([oac, obc, occ, odc]) if ctx_out else None
    return merge([oa, ob, oc, od]), out_c

def swiglu(h, wg, wu, wd):
    return (jax.nn.silu(h @ wg) * (h @ wu)) @ wd

def first_inputs(seed: int = 0) -> dict:
    key = jax.random.key(seed)
    ks = iter(jax.random.split(key, 32))
    L, D, H = DEPTH, D_MODEL, HEADS_PER_GROUP

    def nrm(shape, scale):
        return jax.random.normal(next(ks), shape, jnp.float32) * scale

    def gain(shape):
        return 1.0 + 0.02 * jax.random.normal(next(ks), shape, jnp.float32)

    return {
        'x': nrm((BATCH, SEQ, D), 1.0),
        'c': nrm((BATCH, D), 1.0),
        'ctx': nrm((BATCH, CTX_LEN, D), 1.0),
        'c_ctx': nrm((D,), 1.0),
        'w_ada': nrm((L, D, 6 * D), D ** -0.5),
        'b_ada': nrm((L, 6 * D), 0.02),
        'g_attn': gain((L, D)),
        'g_ffn': gain((L, D)),
        'w_in': nrm((L, D, D_IN), D ** -0.5),
        'w_out': nrm((L, D_MIX, D), D_MIX ** -0.5),
        'na_rpb': nrm((L, H, 2 * NA_KH_MAX - 1, 2 * NA_KW - 1), 0.1),
        'gqa_gq': gain((L, HEAD_DIM)),
        'gqa_gk': gain((L, HEAD_DIM)),
        'mla_gq': gain((L, MLA_Q_RANK)),
        'mla_gkv': gain((L, MLA_KV_RANK)),
        'mla_wuq': nrm((L, MLA_Q_RANK, H * (MLA_NOPE + MLA_ROPE)), MLA_Q_RANK ** -0.5),
        'mla_wukv': nrm((L, MLA_KV_RANK, H * (MLA_NOPE + MLA_V)), MLA_KV_RANK ** -0.5),
        'diff_lq1': nrm((L, DIFF_D), 0.1),
        'diff_lk1': nrm((L, DIFF_D), 0.1),
        'diff_lq2': nrm((L, DIFF_D), 0.1),
        'diff_lk2': nrm((L, DIFF_D), 0.1),
        'diff_gsub': gain((L, 2 * DIFF_D)),
        'ffn_wg': nrm((L, D, D_FF), D ** -0.5),
        'ffn_wu': nrm((L, D, D_FF), D ** -0.5),
        'ffn_wd': nrm((L, D_FF, D), D_FF ** -0.5),
        'g_final': gain((D,)),
    }

def first_block(x, c, ctx, c_ctx, w_ada, b_ada, g_attn, g_ffn, w_in, w_out, na_rpb, gqa_gq, gqa_gk,
              mla_gq, mla_gkv, mla_wuq, mla_wukv, diff_lq1, diff_lk1, diff_lq2, diff_lk2, diff_gsub,
              ffn_wg, ffn_wu, ffn_wd, g_final):
    s = x.shape[1]
    rope128 = axial_rope(s, HEAD_DIM)
    rope64 = axial_rope(s, MLA_ROPE)
    silu_c = jax.nn.silu(c)
    silu_cc = jax.nn.silu(c_ctx)
    xc = ctx
    for l in range(DEPTH):
        ctx_out = l < DEPTH - 1
        lam_init = 0.8 - 0.6 * math.exp(-0.3 * l)
        mod = (silu_c @ w_ada[l] + b_ada[l])[:, None, :]
        mod_c = silu_cc @ w_ada[l] + b_ada[l]
        sh_a, sc_a, gt_a, sh_f, sc_f, gt_f = jnp.split(mod, 6, axis=-1)
        csh_a, csc_a, cgt_a, csh_f, csc_f, cgt_f = jnp.split(mod_c, 6, axis=-1)
        h = rms_norm(x, g_attn[l]) * (1.0 + sc_a) + sh_a
        hc = rms_norm(xc, g_attn[l]) * (1.0 + csc_a) + csh_a
        o_l, o_c = hybrid_mixer(h, hc, w_in[l], w_out[l], na_rpb[l], gqa_gq[l], gqa_gk[l],
                                mla_gq[l], mla_gkv[l], mla_wuq[l], mla_wukv[l],
                                diff_lq1[l], diff_lk1[l], diff_lq2[l], diff_lk2[l], diff_gsub[l],
                                lam_init, rope128, rope64, ctx_out)
        x = x + gt_a * o_l
        h = rms_norm(x, g_ffn[l]) * (1.0 + sc_f) + sh_f
        x = x + gt_f * swiglu(h, ffn_wg[l], ffn_wu[l], ffn_wd[l])
        if ctx_out:
            xc = xc + cgt_a * o_c
            hc = rms_norm(xc, g_ffn[l]) * (1.0 + csc_f) + csh_f
            xc = xc + cgt_f * swiglu(hc, ffn_wg[l], ffn_wu[l], ffn_wd[l])
    return rms_norm(x, g_final)


N_HEADS_MOBA = D_MODEL // (2 * HEAD_DIM)
N_HEADS_FOX = D_MODEL // (2 * HEAD_DIM)
MOBA_WIDTH = N_HEADS_MOBA * HEAD_DIM
FOX_WIDTH = N_HEADS_FOX * HEAD_DIM
MOBA_BLOCK = 256
MOBA_TOPK = 3
MOBA_Q_CHUNK = 64
FOX_Q_BLOCK = 128
D_FF_2 = 4 * D_MODEL
RMS_EPS = 1e-6
IN_WIDTHS = (MOBA_WIDTH, MOBA_WIDTH, MOBA_WIDTH,
             FOX_WIDTH, FOX_WIDTH, FOX_WIDTH,
             N_HEADS_FOX,
             D_MODEL, D_MODEL)
D_IN_2 = sum(IN_WIDTHS)


def rms_norm_2(x, g):
    xf = x.astype(jnp.float32)
    y = xf * lax.rsqrt(jnp.mean(xf * xf, axis=-1, keepdims=True) + RMS_EPS)
    return (y * g.astype(jnp.float32)).astype(x.dtype)

def split_heads(t, n_heads):
    b, s, _ = t.shape
    return t.reshape(b, s, n_heads, HEAD_DIM).transpose(0, 2, 1, 3)

def merge_heads(t):
    b, h, s, d = t.shape
    return t.transpose(0, 2, 1, 3).reshape(b, s, h * d)

def to_chunks(a, c):
    a = a.reshape(a.shape[:2] + (a.shape[2] // c, c) + a.shape[3:])
    return jnp.moveaxis(a, 2, 0)

def from_chunks(a):
    a = jnp.moveaxis(a, 0, 2)
    return a.reshape(a.shape[:2] + (a.shape[2] * a.shape[3],) + a.shape[4:])

def alibi_slopes(n_heads):
    return jnp.exp2(-8.0 * jnp.arange(1, n_heads + 1, dtype=jnp.float32) / n_heads)

def moba_attention(q, k, v):
    b, h, s, d = q.shape
    s_pad = -(-s // MOBA_BLOCK) * MOBA_BLOCK
    pad = ((0, 0), (0, 0), (0, s_pad - s), (0, 0))
    q, k, v = jnp.pad(q, pad), jnp.pad(k, pad), jnp.pad(v, pad)
    nb = s_pad // MOBA_BLOCK
    n_sel = min(MOBA_TOPK, nb)
    scale = HEAD_DIM ** -0.5
    slopes = alibi_slopes(h)[None, :, None]
    kb = k.reshape(b, h, nb, MOBA_BLOCK, d)
    vb = v.reshape(b, h, nb, MOBA_BLOCK, d)
    kmean = jnp.mean(kb.astype(jnp.float32), axis=3)
    gate = jnp.einsum('bhtd,bhnd->bhtn', q.astype(jnp.float32), kmean)
    q_blk = jnp.arange(s_pad) // MOBA_BLOCK
    past = jnp.arange(nb)[None, :] < q_blk[:, None]
    gate = jnp.where(past, gate, -jnp.inf)
    top_vals, sel = lax.top_k(gate, n_sel)
    valid = jnp.isfinite(top_vals)
    bi = jnp.arange(b)[:, None, None, None]
    hi = jnp.arange(h)[None, :, None, None]
    blk_off = jnp.arange(MOBA_BLOCK)

    def chunk(args):
        ci, qc, selc, validc = args
        q_pos = ci * MOBA_Q_CHUNK + jnp.arange(MOBA_Q_CHUNK)
        own = (ci * MOBA_Q_CHUNK) // MOBA_BLOCK
        k_own = lax.dynamic_index_in_dim(kb, own, axis=2, keepdims=False)
        v_own = lax.dynamic_index_in_dim(vb, own, axis=2, keepdims=False)
        dist_own = (q_pos[:, None] - (own * MOBA_BLOCK + blk_off)[None, :])
        s_own = jnp.einsum('bhcd,bhsd->bhcs', qc, k_own).astype(jnp.float32) * scale
        s_own = s_own - slopes[..., None] * jnp.abs(dist_own).astype(jnp.float32)
        s_own = jnp.where(dist_own >= 0, s_own, -jnp.inf)
        k_sel = kb[bi, hi, selc]
        v_sel = vb[bi, hi, selc]
        s_sel = jnp.einsum('bhcd,bhcjsd->bhcjs', qc, k_sel).astype(jnp.float32) * scale
        sel_pos = selc[..., None] * MOBA_BLOCK + blk_off
        dist_sel = jnp.abs(q_pos[None, None, :, None, None] - sel_pos).astype(jnp.float32)
        s_sel = s_sel - slopes[..., None, None] * dist_sel
        s_sel = jnp.where(validc[..., None], s_sel, -jnp.inf)
        c, j = selc.shape[2], selc.shape[3]
        scores = jnp.concatenate([s_sel.reshape(b, h, c, j * MOBA_BLOCK), s_own], axis=-1)
        p = jax.nn.softmax(scores, axis=-1).astype(v.dtype)
        p_sel = p[..., :j * MOBA_BLOCK].reshape(b, h, c, j, MOBA_BLOCK)
        p_own = p[..., j * MOBA_BLOCK:]
        return (jnp.einsum('bhcjs,bhcjsd->bhcd', p_sel, v_sel)
                + jnp.einsum('bhcs,bhsd->bhcd', p_own, v_own))

    nc = s_pad // MOBA_Q_CHUNK
    out = lax.map(chunk, (jnp.arange(nc), to_chunks(q, MOBA_Q_CHUNK),
                          to_chunks(sel, MOBA_Q_CHUNK), to_chunks(valid, MOBA_Q_CHUNK)))
    return from_chunks(out)[:, :, :s]

def forgetting_attention(q, k, v, f_logit, b_forget):
    b, h, s, d = q.shape
    scale = HEAD_DIM ** -0.5
    log_f = jax.nn.log_sigmoid(f_logit.astype(jnp.float32) + b_forget.astype(jnp.float32))
    c = jnp.cumsum(log_f, axis=1).transpose(0, 2, 1)
    key_pos = jnp.arange(s)

    def chunk(args):
        ci, qc, cq = args
        sc = jnp.einsum('bhcd,bhsd->bhcs', qc, k).astype(jnp.float32) * scale
        sc = sc + cq[..., None] - c[:, :, None, :]
        q_pos = ci * FOX_Q_BLOCK + jnp.arange(FOX_Q_BLOCK)
        sc = jnp.where(q_pos[:, None] >= key_pos[None, :], sc, -jnp.inf)
        p = jax.nn.softmax(sc, axis=-1).astype(v.dtype)
        return jnp.einsum('bhcs,bhsd->bhcd', p, v)

    nc = s // FOX_Q_BLOCK
    cq = c.reshape(b, h, nc, FOX_Q_BLOCK).transpose(2, 0, 1, 3)
    out = lax.map(chunk, (jnp.arange(nc), to_chunks(q, FOX_Q_BLOCK), cq))
    return from_chunks(out)

def second_inputs(seed: int = 0) -> dict:
    key = jax.random.key(seed)
    ks = jax.random.split(key, 11)
    f32 = jnp.float32
    def normal(k, shape, scale):
        return jax.random.normal(k, shape, f32) * scale
    return {
        "x": normal(ks[0], (BATCH, SEQ, D_MODEL), 1.0),
        "norm_mix_g": 1.0 + normal(ks[1], (D_MODEL,), 0.02),
        "w_in": normal(ks[2], (D_MODEL, D_IN_2), D_MODEL ** -0.5),
        "b_forget": 2.0 + normal(ks[3], (N_HEADS_FOX,), 0.5),
        "w_proj_a": normal(ks[4], (MOBA_WIDTH, D_MODEL), MOBA_WIDTH ** -0.5),
        "w_proj_b": normal(ks[5], (FOX_WIDTH, D_MODEL), FOX_WIDTH ** -0.5),
        "w_out": normal(ks[6], (D_MODEL, D_MODEL), D_MODEL ** -0.5),
        "norm_mlp_g": 1.0 + normal(ks[7], (D_MODEL,), 0.02),
        "w_up": normal(ks[8], (D_MODEL, D_FF_2), D_MODEL ** -0.5),
        "w_down": normal(ks[9], (D_FF_2, D_MODEL), D_FF_2 ** -0.5),
        "norm_final_g": 1.0 + normal(ks[10], (D_MODEL,), 0.02),
    }

def second_block(x, norm_mix_g, w_in, b_forget, w_proj_a, w_proj_b, w_out,
              norm_mlp_g, w_up, w_down, norm_final_g):
    split_idx = list(np.cumsum(IN_WIDTHS)[:-1])
    for _ in range(DEPTH):
        hn = rms_norm_2(x, norm_mix_g)
        z = hn @ w_in
        q_a, k_a, v_a, q_b, k_b, v_b, f_logit, g_a, g_b = jnp.split(z, split_idx, axis=-1)
        a = moba_attention(split_heads(q_a, N_HEADS_MOBA), split_heads(k_a, N_HEADS_MOBA),
                           split_heads(v_a, N_HEADS_MOBA))
        bfx = forgetting_attention(split_heads(q_b, N_HEADS_FOX), split_heads(k_b, N_HEADS_FOX),
                                   split_heads(v_b, N_HEADS_FOX), f_logit, b_forget)
        a = merge_heads(a) @ w_proj_a
        bfx = merge_heads(bfx) @ w_proj_b
        merged = jax.nn.sigmoid(g_a) * a + jax.nn.sigmoid(g_b) * bfx
        x = x + merged @ w_out
        hm = rms_norm_2(x, norm_mlp_g)
        x = x + jnp.square(jax.nn.relu(hm @ w_up)) @ w_down
    return rms_norm_2(x, norm_final_g)


def setup_inputs(seed=0):
    out = dict(first_inputs(seed))
    for name, value in second_inputs(seed + 1).items():
        if name != "x":
            out[name + "_2"] = value
    return out


def reference(
    x, c, ctx, c_ctx, w_ada, b_ada, g_attn, g_ffn, w_in, w_out, na_rpb, gqa_gq, gqa_gk, mla_gq,
    mla_gkv, mla_wuq, mla_wukv, diff_lq1, diff_lk1, diff_lq2, diff_lk2, diff_gsub, ffn_wg,
    ffn_wu, ffn_wd, g_final, norm_mix_g_2, w_in_2, b_forget_2, w_proj_a_2, w_proj_b_2, w_out_2,
    norm_mlp_g_2, w_up_2, w_down_2, norm_final_g_2,
):
    x = first_block(
        x, c, ctx, c_ctx, w_ada, b_ada, g_attn, g_ffn, w_in, w_out, na_rpb, gqa_gq, gqa_gk,
        mla_gq, mla_gkv, mla_wuq, mla_wukv, diff_lq1, diff_lk1, diff_lq2, diff_lk2, diff_gsub,
        ffn_wg, ffn_wu, ffn_wd, g_final,
    )
    return second_block(
        x, norm_mix_g_2, w_in_2, b_forget_2, w_proj_a_2, w_proj_b_2, w_out_2, norm_mlp_g_2,
        w_up_2, w_down_2, norm_final_g_2,
    )


_drawn_inputs = setup_inputs


def setup_inputs(seed=0):
    import zlib

    import numpy as np

    out = dict(_drawn_inputs(seed))
    spreads = {}
    factors = {'g_attn': 8.0,
     'g_ffn': 3.464,
     'na_rpb': 8.0,
     'gqa_gq': 8.0,
     'gqa_gk': 8.0,
     'mla_gq': 8.0,
     'mla_gkv': 8.0,
     'diff_lq1': 4.43,
     'diff_lk1': 8.0,
     'diff_lq2': 8.0,
     'diff_lk2': 8.0,
     'diff_gsub': 8.0,
     'norm_mix_g_2': 5.462,
     'norm_mlp_g_2': 3.236,
     'norm_final_g_2': 2.76}
    for name, (base, spread) in spreads.items():
        noise = np.random.default_rng([zlib.crc32(name.encode()), seed]).standard_normal(out[name].shape)
        drawn = base * np.exp(spread * noise) if base else spread * noise
        out[name] = jnp.asarray(drawn.astype(out[name].dtype))
    for name, factor in factors.items():
        out[name] = (out[name] * factor).astype(out[name].dtype)
    return out
```

```python
from contextlib import ExitStack
import math

import numpy as np

import concourse.bass as bass
from concourse import mybir
from concourse.alu_op_type import AluOpType as ALU

F32 = mybir.dt.float32
F32R = mybir.dt.float32r
ACT = mybir.ActivationFunctionType
AX = mybir.AxisListType

P = 128
D = 2048
SEQ = 256
NCH = 512
KQ = 4
HD = 128
EPS = 1e-6
D_IN = 4928
D_FF = 5632
D_IN_2 = 10248
D_FF_2 = 8192
KB = 1024
BASE = 16512

NA_Q, NA_K, NA_V, GQ_Q, GQ_K, GQ_V = 0, 512, 1024, 1536, 2048, 2304
ML_Q, ML_KV, ML_PE, DF_Q, DF_K, DF_V = 2560, 3072, 3328, 3392, 3904, 4416
CX_ML, CX_DK, CX_DV, CX_GK, CX_NK, CX_NV, CX_W = 0, 320, 832, 1344, 1856, 2368, 2880
WIN = [(ML_Q, 512, None), (ML_KV, 320, CX_ML), (DF_Q, 512, None), (DF_K, 512, CX_DK), (DF_V, 512, CX_DV),
       (GQ_Q, 512, None), (GQ_K, 512, CX_GK), (NA_Q, 512, None), (NA_K, 512, CX_NK), (NA_V, 512, CX_NV)]

N_ADA = 6 * D // NCH
U_ADA = 0
U_WIN = U_ADA + 4 * N_ADA
U_MLA = U_WIN + 4 * len(WIN)
U_OUT = U_MLA + 4
U_FFN = U_OUT + 4 * (D // NCH)
N_FF = D_FF // NCH
U_WIN2 = U_FFN + 12 * N_FF
N_QKV2 = 12
U_MRG = U_WIN2 + 4 * N_QKV2
U_OUT2 = U_MRG + 12 * (D // NCH)
U_FFN2 = U_OUT2 + 4 * (D // NCH)
N_FF2 = D_FF_2 // NCH
LAM0 = 0.8 - 0.6 * math.exp(-0.3 * 0)


def head_steps():
    steps, a, d = [], 0, 0
    for kind, n in (("mla", 4), ("diff", 8), ("gqa", 4), ("na", 4)):
        for m in range(n):
            half = m % 2 if kind == "diff" else 0
            head = m // 2 if kind == "diff" else m
            turn, value = half == 0, kind != "diff" or half == 1
            steps.append(dict(kind=kind, head=head, half=half, a=a if turn else a - 1, turn=turn,
                              d=d if value else None))
            a += turn
            d += value
    return steps


def head_steps_2():
    return [dict(kind=k, head=h, half=0, a=n, turn=True, d=n)
            for n, (k, h) in enumerate([("moba", h) for h in range(8)] + [("fox", h) for h in range(8)])]


def build(nc, t):
    ctx = ExitStack()
    with ctx:
        sems = {}

        def sem(name):
            if name not in sems:
                sems[name] = ctx.enter_context(nc.semaphore(name))
            return sems[name]

        def at(name, shape, dt, kb):
            return nc.alloc_sbuf_tensor_at(name, shape, dt, offset=BASE + int(kb * KB))

        def wait(eng, name, value):
            if isinstance(value, int) and value <= 0:
                return
            eng.wait_ge(sem(name), value)

        ps = [ctx.enter_context(nc.psum_tensor(f"bank{b}", [P, 512], F32)) for b in range(8)]

        raw = at("w_raw", [P, 4, KQ, NCH], F32, 0)
        whi = at("w_hi", [P, 2, KQ, NCH], F32R, 32)
        wlo = at("w_lo", [P, 2, KQ, NCH], F32R, 48)
        XA = (at("xa_hi", [P, 16, SEQ], F32R, 64), at("xa_lo", [P, 16, SEQ], F32R, 80))
        XB = (at("xb_hi", [P, 16, SEQ], F32R, 96), at("xb_lo", [P, 16, SEQ], F32R, 112))
        brow = at("b_ada_rows", [2, 6 * D], F32, 64)
        cst = at("c_stationary", [P, 16, 128], F32R, 112)
        rows = at("ada_rows", [P, 2, NCH], F32, 120)
        modsb = at("mod_rows", [2, 2, NCH], F32, 124)
        xin = at("x_in", [P, 4, D], F32, 128)
        crow = at("c_rows", [32, 128], F32, 160)
        csig = at("c_silu", [32, 128], F32, 161)
        ccol = at("c_cols", [P, 32], F32, 162)
        esel = at("row_select", [P, 2], F32, 163)
        junk = at("squares", [P, D], F32, 164)
        mods = at("mods_a", [P, 4, D], F32, 160)
        PL = at("proj_x", [P, 2, D_IN], F32, 128)
        PC = at("proj_ctx", [P, 2, CX_W], F32, 128 + 38.5)
        kpeT = at("mla_kpe_T", [64, 512], F32, 128 + 61)
        XQ = (at("mla_cq_hi", [P, 4, SEQ], F32R, 96), at("mla_cq_lo", [P, 4, SEQ], F32R, 100))
        XKV = (at("mla_ckv_hi", [P, 2, 512], F32R, 104), at("mla_ckv_lo", [P, 2, 512], F32R, 108))
        mkv = at("mla_kv", [P, 4, 1024], F32, 112)
        kT = at("k_T", [P, 2, 512], F32, 96)
        qT = at("q_T", [P, 2, 512], F32, 100)
        probs = at("probs", [P, 2, 2, 512], F32, 104)
        probsT = at("probs_T", [P, 2, 4, SEQ], F32, 192 + 7.75)
        nabias = at("na_bias", [P, 4, 2, 256], F32, 112)
        nasel = at("na_select", [31, 16, 128], F32, 120)
        od = at("diff_out", [P, 2, 2, 128], F32, 112)
        ident = at("identity", [P, P], F32, 192)
        small = at("small", [P, 64], F32, 192.5)
        cos128 = at("cos128", [P, 2, 64], F32, 192.75)
        sin128 = at("sin128", [P, 2, 64], F32, 193.25)
        cos64 = at("cos64", [P, 2, 32], F32, 193.75)
        sin64 = at("sin64", [P, 2, 32], F32, 194)
        g_gq = at("gqa_gq_row", [P, 128], F32, 194.25)
        g_gk = at("gqa_gk_row", [P, 128], F32, 194.75)
        g_sub = at("diff_gsub_row", [P, 128], F32, 195.25)
        g_mq = at("mla_gq_row", [P, 512], F32, 195.75)
        g_mkv = at("mla_gkv_row", [P, 256], F32, 197.75)
        lamv = at("diff_lambdas", [P, 4, 64], F32, 198.75)
        gvec = at("g_row", [P, D], F32, 192 + 7.75)
        ropeA = at("rope_a", [P, 512], F32, 192 + 7.75)
        ropeB = at("rope_b", [P, 512], F32, 192 + 9.75)
        psq = at("win_squares", [P, 512], F32, 192 + 11.75)
        pstat = at("pool_stats", [P, 24], F32, 192 + 15.75)
        namask = at("na_mask", [P, 64], F32, 198.75)
        narpb = at("na_rpb_T", [31, 28], F32, 199)
        xres = at("x_res", [P, 2, D], F32, 128)
        gt_a = at("gt_a", [P, D], F32, 144)
        sc_f = at("sc_f", [P, D], F32, 152)
        sh_f = at("sh_f", [P, D], F32, 160)
        gt_f = at("gt_f", [P, D], F32, 168)
        ybuf = at("y_sum", [P, 2, D], F32, 176)
        tmp = at("gated", [P, 2, NCH], F32, 112)
        act_g = at("ffn_gate", [P, 2, NCH], F32, 116)
        act_a = at("ffn_act", [P, 2, NCH], F32, 120)
        XF = (at("ffn_act_hi", [P, 4, SEQ], F32R, 96), at("ffn_act_lo", [P, 4, SEQ], F32R, 100))
        h3 = at("h_mix", [P, 2, D], F32, 176)
        P2 = at("proj_2", [P, 2, 6144], F32, 144)
        wf = at("w_forget", [P, 16, 8], F32, 124)
        wfh = at("w_forget_hi", [P, 16, 8], F32R, 124.5)
        wfl = at("w_forget_lo", [P, 16, 8], F32R, 125)
        bf = at("b_forget", [P, 8], F32, 125.5)
        fz = at("forget_work", [P, 6, 2, 8], F32, 126)
        nlf = at("neg_log_forget", [P, 2, 8], F32, 192 + 15.75)
        distm = at("distance", [P, 2, 256], F32, 192.75)
        causal = at("causal_mask", [P, 2, 256], F32, 194.75)
        tri = at("triangle", [P, 2, 256], F32, 196.75)
        kT2 = at("k_T_2", [P, 2, 256], F32, 128)
        qT2 = at("q_T_2", [P, 2, 256], F32, 130)
        probs2 = at("probs_2", [P, 2, 2, 256], F32, 132)
        probsT2 = at("probs_T_2", [P, 2, 2, SEQ], F32, 136)
        sig = at("gate_sig", [P, 4, NCH], F32, 160)
        mrg = at("merged", [P, 2, D], F32, 144)

        def stat(n, w=1):
            return small[:, n:n + w]

        SS, RSTD = 0, 4
        MX, NM, SUM, RIN = 8, 12, 16, 20
        OSS, ORS = 24, 28
        LAM, LAMW = 32, 34
        NCQ, NCKV, NGQ, NGK = 36, 38, 42, 50
        WIN_SQ = {0: (NCQ, 512, 1, 2), 1: (NCKV, 256, 1, 4), 5: (NGQ, HD, 4, 2), 6: (NGK, HD, 2, 4)}

        w_in_v = t["w_in"][0].rearrange("(q k p) n -> p q k n", p=P, k=KQ)
        w_ada_v = t["w_ada"][0].rearrange("(q k p) n -> p q k n", p=P, k=KQ)
        w_out_v = t["w_out"][0].rearrange("(q k p) n -> p q k n", p=P, k=KQ)
        wg_v = t["ffn_wg"][0].rearrange("(q k p) n -> p q k n", p=P, k=KQ)
        wu_v = t["ffn_wu"][0].rearrange("(q k p) n -> p q k n", p=P, k=KQ)
        wd_v = t["ffn_wd"][0].rearrange("(q k p) n -> p q k n", p=P, k=KQ)
        wuq_v = t["mla_wuq"][0].rearrange("(k p) n -> p k n", p=P)
        wukv_v = t["mla_wukv"][0].rearrange("(k p) n -> p k n", p=P)
        w_in2_v = t["w_in_2"].rearrange("(q k p) n -> p q k n", p=P, k=KQ)
        wpa_v = t["w_proj_a_2"].rearrange("(q k p) n -> p q k n", p=P, k=KQ)
        wpb_v = t["w_proj_b_2"].rearrange("(q k p) n -> p q k n", p=P, k=KQ)
        w_out2_v = t["w_out_2"].rearrange("(q k p) n -> p q k n", p=P, k=KQ)
        w_up_v = t["w_up_2"].rearrange("(q k p) n -> p q k n", p=P, k=KQ)
        w_down_v = t["w_down_2"].rearrange("(q k p) n -> p q k n", p=P, k=KQ)
        x_v = t["x"][0].rearrange("(t p) n -> p t n", p=P)
        ctx_v = t["ctx"][0].rearrange("(t p) n -> p t n", p=P)
        out_v = t["out"][0].rearrange("(t p) n -> p t n", p=P)
        mod_d = nc.dram_tensor("mods_scratch", (2, 6 * D), F32).ap()
        x2_d = nc.dram_tensor("x2_scratch", (P, 2, D), F32).ap()

        def bcast(row, n):
            return row.to_broadcast([P, n])

        STEPS, STEPS2 = head_steps(), head_steps_2()
        N1 = 12

        def load(sp, u4, q, src, k=KQ, w=NCH):
            if isinstance(src, tuple):
                v, off, axis = src
                off = sp.snap(off)
                src = v[:, :, bass.ds(off, NCH)] if axis == "col" else v[:, bass.ds(off, KQ), :]
            wait(sp, "lo_made", 4 * u4 + q - 3)
            sp.dma_start(raw[:, q, 0:k, 0:w], src).then_inc(sem(f"landed{q}"), 16)

        def at_col(v, col):
            return v[:, :, col:col + NCH] if isinstance(col, int) else (v, col, "col")

        def hi(act, u4, q, k=KQ, w=NCH):
            act.wait_ge(sem(f"landed{q}"), 16 * u4 + 16)
            wait(act, "unit_used", 4 * u4 + q - 1)
            act.activation(whi[:, q % 2, 0:k, 0:w], raw[:, q, 0:k, 0:w], ACT.Copy).then_inc(sem("hi_made"), 1)

        def lo(dve, u4, q, k=KQ, w=NCH):
            dve.wait_ge(sem("hi_made"), 4 * u4 + q + 1)
            wait(dve, "unit_used", 4 * u4 + q - 1)
            dve.tensor_tensor(wlo[:, q % 2, 0:k, 0:w], raw[:, q, 0:k, 0:w],
                              whi[:, q % 2, 0:k, 0:w].bitcast(F32), ALU.subtract).then_inc(sem("lo_made"), 1)

        def mm3(pe, out, xh, xl, wh, wl, first, last):
            pe.matmul(out, xh, wh, start=first, stop=False)
            pe.matmul(out, xh, wl, start=False, stop=False)
            return pe.matmul(out, xl, wh, start=False, stop=last)

        def unit(pe, u4, q, outs, X, k0, first, last, k=KQ, w=NCH, toks=(0, 1)):
            pe.wait_ge(sem("lo_made"), 4 * u4 + q + 1)
            for j in range(k):
                for out, tk in zip(outs, toks):
                    Xt = X[tk // 2] if isinstance(X, list) else X
                    c = slice((tk % 2) * P, (tk % 2) * P + P) if isinstance(X, list) else slice(tk * P, tk * P + P)
                    m = mm3(pe, out[:, 0:w], Xt[0][:, k0 + j, c], Xt[1][:, k0 + j, c],
                            whi[:, q % 2, j, 0:w], wlo[:, q % 2, j, 0:w],
                            first and j == 0, last and j == k - 1)
            m.then_inc(sem("unit_used"), 1)

        def turn_pe(pe, tag, srcs, n, ready):
            b = 0
            for i, src in enumerate(srcs):
                wait(pe, ready, i + 1)
                for g in range(n):
                    wait(pe, tag + "_lo", b - 7)
                    for j in range(4):
                        m = pe.transpose(ps[b % 8][:, j * P:j * P + P],
                                         src[:, (4 * g + j) * P:(4 * g + j + 1) * P], ident[:, :])
                    m.then_inc(sem(tag + "_turned"), 1)
                    b += 1

        def turn_act(act, tag, i, X, n, c):
            for g in range(n):
                act.wait_ge(sem(tag + "_turned"), n * i + g + 1)
                act.activation(X[0][:, 4 * g:4 * g + 4, c:c + P],
                               ps[(n * i + g) % 8][:, :].rearrange("p (j t) -> p j t", j=4),
                               ACT.Copy).then_inc(sem(tag + "_hi"), 1)

        def turn_dve(dve, tag, i, X, n, c):
            for g in range(n):
                dve.wait_ge(sem(tag + "_hi"), n * i + g + 1)
                dve.tensor_tensor(X[1][:, 4 * g:4 * g + 4, c:c + P],
                                  ps[(n * i + g) % 8][:, :].rearrange("p (j t) -> p j t", j=4),
                                  X[0][:, 4 * g:4 * g + 4, c:c + P].bitcast(F32),
                                  ALU.subtract).then_inc(sem(tag + "_lo"), 1)

        def pool_rstd(pool, out, sums, width, n):
            pool.tensor_scalar(out, sums, 1.0 / n, EPS, ALU.mult, ALU.add)
            pool.drain()
            return pool.tensor_tensor(out, out, pstat[:, 16:16 + width], ALU.pow)

        def srcs_of(s):
            h, kind = s["head"], s["kind"]
            c = h * HD

            def lc(lat, cx):
                return [PL[:, 0, lat:lat + HD], PL[:, 1, lat:lat + HD],
                        PC[:, 0, cx:cx + HD], PC[:, 1, cx:cx + HD]]
            if kind == "mla":
                q0 = ML_Q + h * 192
                return dict(q=[PL[:, i, q0:q0 + HD] for i in range(2)],
                            qpe=[PL[:, i, q0 + HD:q0 + 192] for i in range(2)],
                            k=[mkv[:, i, h * 256:h * 256 + HD] for i in range(4)],
                            v=[mkv[:, i, h * 256 + HD:h * 256 + 256] for i in range(4)],
                            o=8 + h, scale=192 ** -0.5)
            if kind == "diff":
                return dict(q=[PL[:, i, DF_Q + c:DF_Q + c + HD] for i in range(2)],
                            k=lc(DF_K + c, CX_DK + c), v=lc(DF_V + c, CX_DV + c), o=12 + h, scale=64 ** -0.5)
            if kind == "gqa":
                e = (h // 2) * HD
                return dict(q=[PL[:, i, GQ_Q + c:GQ_Q + c + HD] for i in range(2)],
                            k=lc(GQ_K + e, CX_GK + e), v=lc(GQ_V + e, CX_GK + 256 + e), o=4 + h, scale=HD ** -0.5)
            if kind == "na":
                return dict(q=[PL[:, i, NA_Q + c:NA_Q + c + HD] for i in range(2)],
                            k=lc(NA_K + c, CX_NK + c), v=lc(NA_V + c, CX_NV + c), o=h, scale=HD ** -0.5)
            o = 0 if kind == "moba" else 3072
            return dict(q=[P2[:, i, o + c:o + c + HD] for i in range(2)],
                        k=[P2[:, i, o + 1024 + c:o + 1024 + c + HD] for i in range(2)],
                        v=[P2[:, i, o + 2048 + c:o + 2048 + c + HD] for i in range(2)],
                        o=h + (0 if kind == "moba" else 8), scale=HD ** -0.5)

        class Attn:

            def __init__(self, tag, steps, nkt, kT, qT, pr, prT, X):
                self.tag, self.steps, self.nkt = tag, steps, nkt
                self.kT, self.qT, self.pr, self.prT, self.X = kT, qT, pr, prT, X

            def get(self, n, lo_, hi_):
                return self.steps[n] if lo_ <= n < hi_ else None

            def last_step_of_turn(self, a):
                return max(i for i, s in enumerate(self.steps) if s["a"] == a)

            def d_before(self, n):
                return sum(1 for s in self.steps[:max(n, 0)] if s["d"] is not None)

        def attn_pe(pe, A, lo_, hi_):
            T, nkt = A.tag, A.nkt
            for n in range(lo_, hi_ + 4):
                s = A.get(n, lo_, hi_)
                if s and s["turn"]:
                    src = srcs_of(s)
                    wait(pe, T + "_qk_copied", s["a"])
                    for i, k in enumerate(src["k"]):
                        pe.transpose(ps[0][:, i * P:i * P + P], k, ident[:, :])
                    for i, q in enumerate(src["q"]):
                        m = pe.transpose(ps[1][:, i * P:i * P + P], q, ident[:, :])
                    for i, q in enumerate(src.get("qpe", ())):
                        m = pe.transpose(ps[1][0:64, 256 + i * P:256 + i * P + P], q, ident[:, :])
                    m.then_inc(sem(T + "_qk_turned"), 1)
                s = A.get(n - 1, lo_, hi_)
                if s:
                    pe.wait_ge(sem(T + "_qk_copied"), s["a"] + 1)
                    wait(pe, T + "_exp_done", n - 1)
                    r, w = s["a"] % 2, nkt * P
                    rs = slice(64 * s["half"], 64 * s["half"] + 64) if s["kind"] == "diff" else slice(0, P)
                    for i in range(2):
                        extra = s["kind"] in ("mla", "fox")
                        m = pe.matmul(ps[2 + i][:, 0:w], A.qT[rs, r, i * P:i * P + P], A.kT[rs, r, 0:w],
                                      start=True, stop=not extra)
                        if s["kind"] == "mla":
                            m = pe.matmul(ps[2 + i][:, 0:w], A.qT[0:64, r, 256 + i * P:256 + i * P + P],
                                          kpeT[:, :], start=False, stop=True)
                        if s["kind"] == "fox":
                            for j in range(2):
                                m = pe.matmul(ps[2 + i][:, 0:w],
                                              nlf[:, j, s["head"]:s["head"] + 1].to_broadcast([P, P]),
                                              tri[:, j, :], start=False, stop=j == 1)
                    m.then_inc(sem(T + "_scores"), 1)
                s = A.get(n - 2, lo_, hi_)
                if s and s["d"] is not None:
                    pe.wait_ge(sem(T + "_probs"), n - 1)
                    wait(pe, T + "_pt_copied", s["d"])
                    for i in range(2):
                        for j in range(nkt):
                            m = pe.transpose(ps[4 + i][:, j * P:j * P + P],
                                             A.pr[:, (n - 2) % 2, i, j * P:j * P + P], ident[:, :])
                    m.then_inc(sem(T + "_probs_turned"), 1)
                s = A.get(n - 3, lo_, hi_)
                if s and s["d"] is not None:
                    src, d = srcs_of(s), s["d"]
                    pe.wait_ge(sem(T + "_pt_copied"), d + 1)
                    wait(pe, T + "_out_lo", d - 1)
                    o = ps[6 + d % 2]
                    if s["kind"] == "diff":
                        for i in range(2):
                            for j in range(nkt):
                                m = pe.matmul(o[:, i * P:i * P + P], A.prT[:, d % 2, j, i * P:i * P + P],
                                              src["v"][j], start=j == 0, stop=j == nkt - 1)
                    else:
                        for j in range(nkt):
                            m = pe.matmul(o[:, 0:SEQ], src["v"][j], A.prT[:, d % 2, j, :],
                                          start=j == 0, stop=j == nkt - 1)
                    m.then_inc(sem(T + "_out"), 1)
                s = A.get(n - 4, lo_, hi_)
                if s and s["d"] is not None and s["kind"] == "diff":
                    pe.wait_ge(sem("diff_normed"), s["head"] + 1)
                    for i in range(2):
                        m = pe.transpose(ps[6 + s["d"] % 2][:, 256 + i * P:256 + i * P + P],
                                         od[:, s["head"] % 2, i, :], ident[:, :])
                    m.then_inc(sem("diff_turned"), 1)

        def out_cols(s):
            return slice(256, 512) if s["kind"] == "diff" else slice(0, 256)

        def probs_free(eng, A, n):
            wait(eng, A.tag + "_probs_turned", A.d_before(n - 1))
            if n >= 1 and A.steps[n - 1]["half"] == 1:
                eng.wait_ge(sem(A.tag + "_probs"), n)

        def attn_act(act, A, lo_, hi_):
            T, nkt = A.tag, A.nkt
            for n in range(lo_, hi_ + 4):
                s = A.get(n, lo_, hi_)
                if s and s["turn"]:
                    act.wait_ge(sem(T + "_qk_turned"), s["a"] + 1)
                    if s["a"] >= 2:
                        act.wait_ge(sem(T + "_scores"), A.last_step_of_turn(s["a"] - 2) + 1)
                    r = s["a"] % 2
                    act.activation(A.kT[:, r, 0:nkt * P], ps[0][:, 0:nkt * P], ACT.Copy)
                    m = act.activation(A.qT[:, r, 0:SEQ], ps[1][:, 0:SEQ], ACT.Copy)
                    if s["kind"] == "mla":
                        m = act.activation(A.qT[0:64, r, 256:512], ps[1][0:64, 256:512], ACT.Copy)
                    m.then_inc(sem(T + "_qk_copied"), 1)
                s = A.get(n - 1, lo_, hi_)
                if s:
                    par = (n - 1) % 2
                    probs_free(act, A, n - 1)
                    act.wait_ge(sem(T + "_negmax"), n)
                    biased = s["kind"] in ("na", "moba", "fox")
                    for i in range(2):
                        src = A.pr[:, par, i, :] if biased else ps[2 + i][:, 0:nkt * P]
                        scale = srcs_of(s)["scale"]
                        m = act.activation(A.pr[:, par, i, :], src, ACT.Exp, bias=stat(NM + 2 * par + i),
                                           scale=1.0 if s["kind"] == "na" else scale,
                                           accum_out=stat(SUM + 2 * par + i))
                    m.then_inc(sem(T + "_exp_done"), 1)
                s = A.get(n - 3, lo_, hi_)
                if s and s["d"] is not None and s["kind"] == "diff":
                    act.wait_ge(sem(T + "_out"), s["d"] + 1)
                    wait(act, "diff_normed", s["head"])
                    for i in range(2):
                        m = act.activation(od[:, s["head"] % 2, i, :], ps[6 + s["d"] % 2][:, i * P:i * P + P],
                                           ACT.Square, accum_out=stat(OSS + i))
                    m.then_inc(sem("diff_squares"), 1)
                s = A.get(n - 4, lo_, hi_)
                if s and s["d"] is not None:
                    if s["kind"] == "diff":
                        act.wait_ge(sem("diff_turned"), s["head"] + 1)
                    else:
                        act.wait_ge(sem(T + "_out"), s["d"] + 1)
                    act.activation(A.X[0][:, srcs_of(s)["o"], :], ps[6 + s["d"] % 2][:, out_cols(s)],
                                   ACT.Copy).then_inc(sem(T + "_out_hi"), 1)

        def attn_dve(dve, A, lo_, hi_):
            T, nkt = A.tag, A.nkt
            w = nkt * P
            for n in range(lo_, hi_ + 4):
                s = A.get(n - 3, lo_, hi_)
                if s and s["d"] is not None:
                    d = s["d"]
                    dve.wait_ge(sem(T + "_probs_turned"), d + 1)
                    wait(dve, T + "_out", d - 1)
                    for i in range(2):
                        m = dve.tensor_copy(A.prT[:, d % 2, :, i * P:i * P + P],
                                            ps[4 + i][:, 0:w].rearrange("p (j t) -> p j t", j=nkt))
                    m.then_inc(sem(T + "_pt_copied"), 1)
                s = A.get(n - 2, lo_, hi_)
                if s:
                    par = (n - 2) % 2
                    dve.wait_ge(sem(T + "_exp_done"), n - 1)
                    dve.reciprocal(stat(RIN + 2 * par, 2), stat(SUM + 2 * par, 2))
                    dve.drain()
                    if s["half"] == 1:
                        dve.tensor_scalar(stat(RIN + 2 * par, 2), stat(RIN + 2 * par, 2), stat(LAM), None, ALU.mult)
                        dve.drain()
                    for i in range(2):
                        p = A.pr[:, par, i, :]
                        if s["half"] == 1:
                            m = dve.scalar_tensor_tensor(p, p, stat(RIN + 2 * par + i), A.pr[:, 1 - par, i, :],
                                                         ALU.mult, ALU.add)
                        else:
                            m = dve.tensor_scalar(p, p, stat(RIN + 2 * par + i), None, ALU.mult)
                    m.then_inc(sem(T + "_probs"), 1)
                s = A.get(n - 1, lo_, hi_)
                if s:
                    par = (n - 1) % 2
                    src = srcs_of(s)
                    dve.wait_ge(sem(T + "_scores"), n)
                    if s["kind"] in ("na", "moba", "fox"):
                        probs_free(dve, A, n - 1)
                        for i in range(2):
                            p = A.pr[:, par, i, :]
                            if s["kind"] == "na":
                                dve.scalar_tensor_tensor(p[:, 0:256], ps[2 + i][:, 0:256], src["scale"],
                                                         nabias[:, s["head"], i, :], ALU.mult, ALU.add)
                                dve.tensor_scalar(p[:, 256:512], ps[2 + i][:, 256:512], src["scale"], None, ALU.mult)
                            elif s["kind"] == "moba":
                                slope = 2.0 ** -(s["head"] + 1)
                                dve.scalar_tensor_tensor(p, distm[:, i, :], -slope / src["scale"],
                                                         ps[2 + i][:, 0:w], ALU.mult, ALU.add)
                            else:
                                dve.scalar_tensor_tensor(p, causal[:, i, :], 1.0, ps[2 + i][:, 0:w],
                                                         ALU.mult, ALU.add)
                        dve.drain()
                    for i in range(2):
                        x = A.pr[:, par, i, :] if s["kind"] in ("na", "moba", "fox") else ps[2 + i][:, 0:w]
                        dve.tensor_reduce(stat(MX + 2 * par + i), x, AX.X, ALU.max)
                    dve.drain()
                    dve.tensor_scalar(stat(NM + 2 * par, 2), stat(MX + 2 * par, 2),
                                      -1.0 if s["kind"] == "na" else -src["scale"], None,
                                      ALU.mult).then_inc(sem(T + "_negmax"), 1)
                s = A.get(n - 4, lo_, hi_)
                if s and s["d"] is not None:
                    if s["kind"] == "diff":
                        dve.wait_ge(sem("diff_rstd"), s["head"] + 1)
                        for i in range(2):
                            m = dve.scalar_tensor_tensor(od[:, s["head"] % 2, i, :],
                                                         ps[6 + s["d"] % 2][:, i * P:i * P + P], stat(ORS + i),
                                                         g_sub[:, :], ALU.mult, ALU.mult)
                        m.then_inc(sem("diff_normed"), 1)
                    dve.wait_ge(sem(T + "_out_hi"), s["d"] + 1)
                    o = srcs_of(s)["o"]
                    dve.tensor_tensor(A.X[1][:, o, :], ps[6 + s["d"] % 2][:, out_cols(s)],
                                      A.X[0][:, o, :].bitcast(F32), ALU.subtract).then_inc(sem(T + "_out_lo"), 1)

        A1 = Attn("att", STEPS, 4, kT, qT, probs, probsT, XA)
        A2 = Attn("att2", STEPS2, 2, kT2, qT2, probs2, probsT2, XB)

        def ffn_base(U, i, gated):
            per = 3 if gated else 2
            return U // 4 + (per - 1) + (i - 1) * per

        def ffn_pe(pe, T, U, n, gated):
            def group(u4, banks, done):
                for q in range(4):
                    unit(pe, u4, q, banks, XA, 4 * q, q == 0, q == 3)
                    if q == 3:
                        pe.nop().then_inc(sem(done), 1) if False else None

            def body(i, head=True, tail=True):
                g0 = U // 4 if isinstance(i, int) and i == 0 else ffn_base(U, i, gated)
                k = 0
                if head and gated:
                    wait(pe, T + "_gated", i)
                    for q in range(4):
                        unit(pe, g0, q, ps[0:2], XA, 4 * q, q == 0, q == 3)
                    k = 1
                for q in range(4):
                    if head:
                        if q == 0:
                            wait(pe, T + "_act", i)
                        unit(pe, g0 + k, q, ps[2:4], XA, 4 * q, q == 0, q == 3)
                    if q == 1 and tail:
                        pe.wait_ge(sem(T + "_act"), i)
                        wait(pe, T + "_y", 4 * i - 4)
                        for tk in range(2):
                            for j in range(4):
                                m = pe.transpose(ps[4 + tk][:, j * P:j * P + P],
                                                 act_a[:, tk, j * P:j * P + P], ident[:, :])
                        m.then_inc(sem(T + "_turned"), 1)
                k += head
                if tail:
                    pe.wait_ge(sem(T + "_xlo"), i)
                    for q in range(4):
                        wait(pe, T + "_y", 4 * i - 4 + q - 1)
                        b = 6 if q % 2 == 0 else 4
                        unit(pe, g0 + k, q, ps[b:b + 2], XF, 0, True, True)

            body(0, tail=False)
            body(1)
            with pe.Fori(2, n) as i:
                body(i)
            body_tail(pe, n, body, U, gated)

        def body_tail(eng, n, body, U, gated):
            body(n, head=False)

        def ffn_act(act, T, U, n, gated):
            def body(i, head=True, tail=True):
                g0 = U // 4 if isinstance(i, int) and i == 0 else ffn_base(U, i, gated)
                k = 0
                if head and gated:
                    for q in range(4):
                        hi(act, g0, q)
                    k = 1
                if head:
                    hi(act, g0 + k, 0)
                    hi(act, g0 + k, 1)
                if head and gated:
                    act.wait_ge(sem("unit_used"), 4 * g0 + 4)
                    wait(act, T + "_act", i)
                    for tk in range(2):
                        m = act.activation(act_g[:, tk, :], ps[tk][:, :], ACT.Silu)
                    m.then_inc(sem(T + "_gated"), 1)
                if head:
                    hi(act, g0 + k, 2)
                if tail:
                    act.wait_ge(sem(T + "_turned"), i)
                    for tk in range(2):
                        m = act.activation(XF[0][:, :, tk * P:tk * P + P],
                                           ps[4 + tk][:, :].rearrange("p (j t) -> p j t", j=4), ACT.Copy)
                    m.then_inc(sem(T + "_xhi"), 1)
                if head:
                    hi(act, g0 + k, 3)
                k += head
                if tail:
                    hi(act, g0 + k, 0)
                    hi(act, g0 + k, 1)
                if head and not gated:
                    act.wait_ge(sem("unit_used"), 4 * (g0 + k))
                    wait(act, T + "_act", i)
                    for tk in range(2):
                        m = act.activation(act_g[:, tk, :], ps[2 + tk][:, :], ACT.Relu)
                    m.then_inc(sem(T + "_gated"), 1)
                if tail:
                    hi(act, g0 + k, 2)
                    hi(act, g0 + k, 3)

            body(0, tail=False)
            body(1)
            with act.Fori(2, n) as i:
                body(i)
            body(n, head=False)

        def ffn_dve(dve, T, U, n, gated):
            def add_y(i, q, g):
                dve.wait_ge(sem("unit_used"), 4 * g + q + 1)
                b = 6 if q % 2 == 0 else 4
                for tk in range(2):
                    y = ybuf[:, tk, q * NCH:(q + 1) * NCH]
                    if isinstance(i, int) and i == 1:
                        m = dve.tensor_copy(y, ps[b + tk][:, :])
                    else:
                        m = dve.tensor_tensor(y, y, ps[b + tk][:, :], ALU.add)
                m.then_inc(sem(T + "_y"), 1)

            def body(i, head=True, tail=True, pending=True):
                g0 = U // 4 if isinstance(i, int) and i == 0 else ffn_base(U, i, gated)
                k = 0
                if head and gated:
                    lo(dve, g0, 0)
                    lo(dve, g0, 1)
                    if pending:
                        add_y(i - 1, 3, g0 - 1)
                    lo(dve, g0, 2)
                    lo(dve, g0, 3)
                    k = 1
                if head:
                    lo(dve, g0 + k, 0)
                    lo(dve, g0 + k, 1)
                if pending and not (head and gated):
                    add_y(i - 1, 3, g0 - 1)
                if head:
                    lo(dve, g0 + k, 2)
                if tail:
                    dve.wait_ge(sem(T + "_xhi"), i)
                    for tk in range(2):
                        m = dve.tensor_tensor(XF[1][:, :, tk * P:tk * P + P],
                                              ps[4 + tk][:, :].rearrange("p (j t) -> p j t", j=4),
                                              XF[0][:, :, tk * P:tk * P + P].bitcast(F32), ALU.subtract)
                    m.then_inc(sem(T + "_xlo"), 1)
                if head:
                    lo(dve, g0 + k, 3)
                k += head
                if tail:
                    lo(dve, g0 + k, 0)
                    lo(dve, g0 + k, 1)
                    add_y(i, 0, g0 + k)
                if head:
                    dve.wait_ge(sem(T + "_gated"), i + 1)
                    if gated:
                        dve.wait_ge(sem("unit_used"), 4 * (g0 + k))
                    if tail:
                        dve.wait_ge(sem(T + "_turned"), i)
                    for tk in range(2):
                        m = dve.tensor_tensor(act_a[:, tk, :], act_g[:, tk, :],
                                              ps[2 + tk][:, :] if gated else act_g[:, tk, :], ALU.mult)
                    m.then_inc(sem(T + "_act"), 1)
                if tail:
                    for q in (2, 3):
                        lo(dve, g0 + k, q)
                        add_y(i, q - 1, g0 + k)

            body(0, tail=False, pending=False)
            body(1, pending=False)
            body(2)
            with dve.Fori(3, n) as i:
                body(i)
            body(n, head=False)
            add_y(n, 3, ffn_base(U, n, gated))

        def ffn_sp(sp, U, n, gated, gate_v, up_v, down_flat):
            def body(i, head=True, tail=True):
                g0 = U // 4 if isinstance(i, int) and i == 0 else ffn_base(U, i, gated)
                k = 0
                for v in ([gate_v, up_v] if gated else [up_v]) if head else []:
                    for q in range(4):
                        load(sp, g0 + k, q, at_col(v[:, q], i * NCH))
                    k += 1
                if tail:
                    for q in range(4):
                        v = down_flat[:, :, q * NCH:(q + 1) * NCH]
                        if isinstance(i, int):
                            load(sp, g0 + k, q, v[:, (i - 1) * KQ:i * KQ, :])
                        else:
                            load(sp, g0 + k, q, (v, i * KQ - KQ, "k"))

            body(0, tail=False)
            body(1)
            with sp.Fori(2, n) as i:
                body(i)
            body(n, head=False)

        wd_k = t["ffn_wd"][0].rearrange("(k p) n -> p k n", p=P)
        w_down_k = t["w_down_2"].rearrange("(k p) n -> p k n", p=P)

        def out_sp(sp, U, v):
            for c in range(4):
                for q in range(4):
                    load(sp, U // 4 + c, q, v[:, q, :, c * NCH:(c + 1) * NCH])

        def out_pe(pe, T, U, X):
            for c in range(4):
                wait(pe, T, c - 1)
                for q in range(4):
                    unit(pe, U // 4 + c, q, ps[2 * (c % 2):2 * (c % 2) + 2], X, 4 * q, q == 0, q == 3)

        def out_act(act, U):
            for c in range(4):
                for q in range(4):
                    hi(act, U // 4 + c, q)

        def out_dve(dve, T, U, gate):
            def add(c):
                dve.wait_ge(sem("unit_used"), U + 4 * c + 4)
                cc = slice(c * NCH, (c + 1) * NCH)
                for tk in range(2):
                    src = ps[2 * (c % 2) + tk][:, :]
                    if gate is not None:
                        dve.drain()
                        dve.tensor_tensor(tmp[:, tk, :], src, gate[:, cc], ALU.mult)
                        dve.drain()
                        src = tmp[:, tk, :]
                    m = dve.tensor_tensor(xres[:, tk, cc], xres[:, tk, cc], src, ALU.add)
                m.then_inc(sem(T), 1)
            for c in range(4):
                lo(dve, U // 4 + c, 0)
                lo(dve, U // 4 + c, 1)
                if c == 1:
                    wait(dve, T + "_loaded", 16 * (6 if gate is not None else 1))
                if c:
                    add(c - 1)
                lo(dve, U // 4 + c, 2)
                lo(dve, U // 4 + c, 3)
            add(3)

        def squares_act(act, T, done, n_done, x, tiles, work):
            act.wait_ge(sem(done), n_done)
            for i in range(tiles):
                act.drain()
                m = act.activation(work, x[:, i, :], ACT.Square, accum_out=stat(SS + i))
            m.then_inc(sem(T + "_squares"), 1)

        def rstd_pool(pool, T, tiles):
            pool.wait_ge(sem(T + "_squares"), 1)
            pool_rstd(pool, stat(RSTD, tiles), stat(SS, tiles), tiles, D).then_inc(sem(T + "_rstd"), 1)

        block = ctx.enter_context(nc.Block())

        @block.sync
        def _(sp):
            sp.dma_start(crow[0:16, :], t["c"].rearrange("a (k p) -> (a k) p", p=P)).then_inc(sem("c_loaded"), 16)
            sp.dma_start(crow[16:32, :], t["c_ctx"].rearrange("(k p) -> k p", p=P)).then_inc(sem("c_loaded"), 16)
            sp.dma_start(ident[:, :], t["identity"]).then_inc(sem("ident_loaded"), 16)
            sp.dma_start(esel[:, :], t["row_select"]).then_inc(sem("ident_loaded"), 16)

            def ada(i):
                for b in range(2):
                    for q in range(4):
                        load(sp, 2 * i + b, q, at_col(w_ada_v[:, q], i * (2 * NCH) + b * NCH))
            ada(0)
            sp.dma_start(brow[:, :], t["b_ada"].to_broadcast([2, 6 * D])).then_inc(sem("b_loaded"), 16)
            sp.dma_start(xin[:, 0:2, :], x_v).then_inc(sem("x_loaded"), 16)
            sp.dma_start(xin[:, 2:4, :], ctx_v).then_inc(sem("x_loaded"), 16)
            with sp.Fori(1, N_ADA // 2) as i:
                ada(i)
            for c, (col, w, _) in enumerate(WIN):
                for q in range(4):
                    load(sp, U_WIN // 4 + c, q, w_in_v[:, q, :, col:col + w], w=w)
            load(sp, U_MLA // 4, 0, wuq_v[:, :, 0:512])
            load(sp, U_MLA // 4, 1, wuq_v[:, :, 512:768], w=256)
            load(sp, U_MLA // 4, 2, wukv_v[:, :, 0:512], k=2)
            load(sp, U_MLA // 4, 3, wukv_v[:, :, 512:1024], k=2)
            out_sp(sp, U_OUT, w_out_v)
            ffn_sp(sp, U_FFN, N_FF, True, wg_v, wu_v, wd_k)

            def qkv2(i):
                for b in range(2):
                    for q in range(4):
                        load(sp, U_WIN2 // 4 + 2 * i + b, q, at_col(w_in2_v[:, q], i * (2 * NCH) + b * NCH))
            with sp.Fori(0, N_QKV2 // 2) as i:
                qkv2(i)

            def merge(n):
                for b, first in enumerate((6152, 8200)):
                    for q in range(4):
                        load(sp, U_MRG // 4 + 3 * n + b, q, at_col(w_in2_v[:, q], n * NCH + first))
                for q in range(4):
                    v = wpa_v if q < 2 else wpb_v
                    load(sp, U_MRG // 4 + 3 * n + 2, q, at_col(v[:, q % 2], n * NCH))
            for n in range(4):
                merge(n)
            out_sp(sp, U_OUT2, w_out2_v)
            ffn_sp(sp, U_FFN2, N_FF2, False, None, w_up_v, w_down_k)
            for tk in range(2):
                sp.wait_ge(sem("final"), tk + 1)
                sp.dma_start(out_v[:, tk, :], h3[:, tk, :]).then_inc(sem("stored"), 16)
            sp.wait_ge(sem("stored"), 32)

        @block.scalar
        def _(act):
            act.wait_ge(sem("c_loaded"), 32)
            act.activation(csig[:, :], crow[:, :], ACT.Silu).then_inc(sem("c_silu"), 1)
            act.wait_ge(sem("c_turned"), 1)
            cs4 = cst[:, :, :].rearrange("p k (v h r) -> p k v h r", v=2, h=2)
            for v in range(2):
                m = act.activation(cs4[:, :, v, 0, :], ccol[:, 16 * v:16 * v + 16].rearrange("p (k r) -> p k r", r=1)
                                   .to_broadcast([P, 16, 32]), ACT.Copy)
            m.then_inc(sem("c_hi"), 1)

            def copy_rows(c, b):
                act.wait_ge(sem("unit_used"), 4 * c + 4)
                wait(act, "ada_combined", c - 1)
                act.activation(rows[:, b, :], ps[b][:, :], ACT.Copy).then_inc(sem("ada_rows"), 1)

            def ada(i, first=False):
                for b in range(2):
                    c = 2 * i + b
                    hi(act, c, 0)
                    hi(act, c, 1)
                    if not (first and b == 0):
                        copy_rows(c - 1, 1 - b)
                    hi(act, c, 2)
                    hi(act, c, 3)
            ada(0, True)
            squares_act(act, "x", "x_loaded", 32, xin, 4, junk[:, :])
            ada(1)
            with act.Fori(2, N_ADA // 2) as i:
                ada(i)
            copy_rows(N_ADA - 1, 1)
            for i, (X, c) in enumerate(((XA, 0), (XA, P), (XB, 0), (XB, P))):
                turn_act(act, "h", i, X, 4, c)

            def win_copy(c):
                col, w, cx = WIN[c]
                act.wait_ge(sem("unit_used"), U_WIN + 4 * c + 4)
                b = 4 * (c % 2)
                m = act.activation(PL[:, 0, col:col + w], ps[b][:, 0:w], ACT.Copy)
                if cx is not None:
                    m = act.activation(PC[:, 0, cx:cx + w], ps[b + 2][:, 0:w], ACT.Copy)
                m.then_inc(sem("win_copied_a"), 1)
                if c in WIN_SQ:
                    first, width, n, tiles = WIN_SQ[c]
                    act.wait_ge(sem("win_copied_d"), c + 1)
                    for i in range(tiles):
                        for h in range(n):
                            act.drain()
                            src = PL[:, i, col + h * width:col + (h + 1) * width] if i < 2 else \
                                PC[:, i - 2, cx + h * width:cx + (h + 1) * width]
                            m = act.activation(psq[:, 0:width], src, ACT.Square, accum_out=stat(first + n * i + h))
                    m.then_inc(sem("win_squared"), 1)
            for c, (_, w, _) in enumerate(WIN):
                hi(act, U_WIN // 4 + c, 0, w=w)
                hi(act, U_WIN // 4 + c, 1, w=w)
                if c:
                    win_copy(c - 1)
                hi(act, U_WIN // 4 + c, 2, w=w)
                hi(act, U_WIN // 4 + c, 3, w=w)
            hi(act, U_MLA // 4, 0)
            win_copy(len(WIN) - 1)
            hi(act, U_MLA // 4, 1, w=256)

            act.wait_ge(sem("mla_turned"), 1)
            for i in range(2):
                act.activation(XQ[0][:, :, i * P:i * P + P], ps[i][:, :].rearrange("p (j t) -> p j t", j=4), ACT.Copy)
            for i in range(4):
                m = act.activation(XKV[0][:, :, i * P:i * P + P],
                                   ps[2 + i // 2][:, (i % 2) * 256:(i % 2) * 256 + 256].rearrange("p (j t) -> p j t", j=2),
                                   ACT.Copy)
            m.then_inc(sem("mla_hi"), 1)
            act.activation(kpeT[:, :], ps[4][0:64, :], ACT.Copy).then_inc(sem("kpe_copied"), 1)
            hi(act, U_MLA // 4, 2, k=2)
            hi(act, U_MLA // 4, 3, k=2)
            act.wait_ge(sem("unit_used"), U_MLA + 1)
            act.activation(PL[:, 0, ML_Q:ML_Q + 512], ps[0][:, :], ACT.Copy)
            act.wait_ge(sem("unit_used"), U_MLA + 2)
            act.activation(PL[:, 0, ML_Q + 512:ML_Q + 768], ps[2][:, 0:256], ACT.Copy).then_inc(sem("mla_copied_a"), 1)
            act.wait_ge(sem("unit_used"), U_MLA + 3)
            for i in (0, 1):
                m = act.activation(mkv[:, i, 0:512], ps[4 + i][:, :], ACT.Copy)
            act.wait_ge(sem("unit_used"), U_MLA + 4)
            for i in (0, 1):
                m = act.activation(mkv[:, i, 512:1024], ps[i][:, :], ACT.Copy)
            m.then_inc(sem("mla_copied_a"), 1)
            act.wait_ge(sem("lam_dots"), 1)
            act.activation(stat(LAMW, 2), stat(LAMW, 2), ACT.Exp).then_inc(sem("lam_exp"), 1)

            act.wait_ge(sem("rotated_pe"), 1)
            attn_act(act, A1, 0, N1)
            attn_act(act, A1, N1, len(STEPS))
            out_act(act, U_OUT)

            squares_act(act, "x1", "x1_chunk", 4, xres, 2, ybuf[:, 0, :])
            for i in range(2):
                turn_act(act, "h2", i, XA, 4, i * P)
            ffn_act(act, "ff1", U_FFN, N_FF, True)

            squares_act(act, "xf", "xf_ready", 1, xres, 2, ybuf[:, 0, :])
            squares_act(act, "x2", "x2_ready", 1, xres, 2, ybuf[:, 0, :])
            for i in range(2):
                turn_act(act, "h3", i, XA, 4, i * P)
            act.wait_ge(sem("wf_loaded"), 32)
            act.activation(wfh[:, :, :], wf[:, :, :], ACT.Copy).then_inc(sem("wf_hi"), 1)

            def qkv2(i, first=False):
                for b in range(2):
                    g = U_WIN2 // 4 + 2 * i + b
                    hi(act, g, 0)
                    hi(act, g, 1)
                    if not (first and b == 0):
                        qkv2_copy(i * 2 + (b - 1), 1 - b)
                    hi(act, g, 2)
                    hi(act, g, 3)

            def qkv2_copy(c, b):
                act.wait_ge(sem("unit_used"), c * 4 + (U_WIN2 + 4))
                act.activation(P2[:, 0, bass.ds(c * NCH, NCH)], ps[2 * b][:, :], ACT.Copy).then_inc(sem("qkv2_a"), 1)
            qkv2(0, True)
            with act.Fori(1, N_QKV2 // 2) as i:
                qkv2(i)
            qkv2_copy(N_QKV2 - 1, 1)
            act.wait_ge(sem("fz_abs"), 1)
            act.activation(fz[:, 2], fz[:, 1], ACT.Exp, scale=-1.0).then_inc(sem("fz_exp"), 1)
            act.wait_ge(sem("fz_one"), 1)
            act.activation(fz[:, 4], fz[:, 3], ACT.Ln).then_inc(sem("fz_log"), 1)
            act.wait_ge(sem("x2_stored"), 16)
            attn_act(act, A2, 0, len(STEPS2))

            def sigm(n, b):
                act.wait_ge(sem("unit_used"), n * 12 + (U_MRG + 4 * b + 4))
                wait(act, "merged_chunk", n)
                for tk in range(2):
                    m = act.activation(sig[:, 2 * b + tk, :], ps[2 * b + tk][:, :], ACT.Sigmoid)
                m.then_inc(sem("gate_sigmoid"), 1)

            def merge(n):
                g = 3 * n + U_MRG // 4
                for q in range(4):
                    hi(act, g, q)
                hi(act, g + 1, 0)
                hi(act, g + 1, 1)
                sigm(n, 0)
                hi(act, g + 1, 2)
                hi(act, g + 1, 3)
                hi(act, g + 2, 0)
                hi(act, g + 2, 1)
                sigm(n, 1)
                hi(act, g + 2, 2)
                hi(act, g + 2, 3)
            merge(0)
            with act.Fori(1, 4) as n:
                merge(n)
            for i in range(2):
                turn_act(act, "mrg", i, XA, 4, i * P)
            out_act(act, U_OUT2)
            squares_act(act, "x3", "x3_chunk", 4, xres, 2, ybuf[:, 0, :])
            for i in range(2):
                turn_act(act, "h4", i, XA, 4, i * P)
            ffn_act(act, "ff2", U_FFN2, N_FF2, False)
            squares_act(act, "x4", "x4_ready", 1, xres, 2, gt_a[:, :])

        @block.vector
        def _(dve):
            dve.memset(pstat[:, 16:24], -0.5).then_inc(sem("halves"), 1)
            dve.wait_ge(sem("c_cols"), 1)
            dve.tensor_copy(ccol[:, :], ps[7][:, 0:32]).then_inc(sem("c_turned"), 1)
            dve.wait_ge(sem("c_hi"), 1)
            cs4 = cst[:, :, :].rearrange("p k (v h r) -> p k v h r", v=2, h=2)
            for v in range(2):
                m = dve.tensor_tensor(cs4[:, :, v, 1, :],
                                      ccol[:, 16 * v:16 * v + 16].rearrange("p (k r) -> p k r", r=1).to_broadcast([P, 16, 32]),
                                      cs4[:, :, v, 0, :].bitcast(F32), ALU.subtract)
            m.then_inc(sem("c_lo"), 1)

            def add_b(c, b):
                dve.wait_ge(sem("ada_combined"), c + 1)
                if isinstance(c, int) and c == 0:
                    dve.wait_ge(sem("b_loaded"), 16)
                if isinstance(c, int):
                    if c >= 2:
                        dve.wait_ge(sem(f"mod_stored{b}"), 16 * (c // 2))
                else:
                    dve.wait_ge(sem(f"mod_stored{b}"), c * 8 - 8 * b)
                dve.tensor_tensor(modsb[:, b, :], ps[2 + b][0:2, :], brow[:, bass.ds(c * NCH, NCH)],
                                  ALU.add).then_inc(sem("mod_row"), 1)

            def ada(i, n=0):
                for b in range(2):
                    c = 2 * i + b
                    for q in range(4):
                        lo(dve, c, q)
                    if n >= 2 - b:
                        add_b(c - 1, 1 - b)
            ada(0, 1)
            ada(1, 2)
            with dve.Fori(2, N_ADA // 2) as i:
                ada(i, 2)
            add_b(N_ADA - 1, 1)

            dve.wait_ge(sem("mods_loaded"), 16 * 5)
            for v in range(2):
                dve.scalar_tensor_tensor(mods[:, 2 * v, :], mods[:, 2 * v, :], 1.0, gvec[:, :], ALU.add, ALU.mult)
            dve.wait_ge(sem("x_rstd"), 1)
            dve.drain()

            def modulate(x, out, rstd, scale, shift, done):
                dve.scalar_tensor_tensor(out, x, rstd, scale, ALU.mult, ALU.mult)
                if shift is not None:
                    dve.drain()
                    return dve.tensor_tensor(out, out, shift, ALU.add)
            for i in range(5):
                if i < 4:
                    m = modulate(xin[:, i, :], xin[:, i, :], stat(RSTD + i), mods[:, 2 * (i // 2), :],
                                 mods[:, 2 * (i // 2) + 1, :], None)
                    m.then_inc(sem("h_ready"), 1)
                if i:
                    turn_dve(dve, "h", i - 1, XA if i <= 2 else XB, 4, ((i - 1) % 2) * P)

            def win_copy(c):
                col, w, cx = WIN[c]
                dve.wait_ge(sem("unit_used"), U_WIN + 4 * c + 4)
                b = 4 * (c % 2)
                m = dve.tensor_copy(PL[:, 1, col:col + w], ps[b + 1][:, 0:w])
                if cx is not None:
                    m = dve.tensor_copy(PC[:, 1, cx:cx + w], ps[b + 3][:, 0:w])
                m.then_inc(sem("win_copied_d"), 1)
            for c, (_, w, _) in enumerate(WIN):
                lo(dve, U_WIN // 4 + c, 0, w=w)
                lo(dve, U_WIN // 4 + c, 1, w=w)
                if c:
                    win_copy(c - 1)
                lo(dve, U_WIN // 4 + c, 2, w=w)
                lo(dve, U_WIN // 4 + c, 3, w=w)
            lo(dve, U_MLA // 4, 0)
            win_copy(len(WIN) - 1)
            lo(dve, U_MLA // 4, 1, w=256)
            dve.wait_ge(sem("mla_hi"), 1)
            for i in range(2):
                dve.tensor_tensor(XQ[1][:, :, i * P:i * P + P], ps[i][:, :].rearrange("p (j t) -> p j t", j=4),
                                  XQ[0][:, :, i * P:i * P + P].bitcast(F32), ALU.subtract)
            for i in range(4):
                m = dve.tensor_tensor(XKV[1][:, :, i * P:i * P + P],
                                      ps[2 + i // 2][:, (i % 2) * 256:(i % 2) * 256 + 256].rearrange("p (j t) -> p j t", j=2),
                                      XKV[0][:, :, i * P:i * P + P].bitcast(F32), ALU.subtract)
            m.then_inc(sem("mla_lo"), 1)
            lo(dve, U_MLA // 4, 2, k=2)
            lo(dve, U_MLA // 4, 3, k=2)
            dve.wait_ge(sem("unit_used"), U_MLA + 1)
            dve.tensor_copy(PL[:, 1, ML_Q:ML_Q + 512], ps[1][:, :])
            dve.wait_ge(sem("unit_used"), U_MLA + 2)
            dve.tensor_copy(PL[:, 1, ML_Q + 512:ML_Q + 768], ps[3][:, 0:256]).then_inc(sem("mla_copied_d"), 1)
            dve.wait_ge(sem("unit_used"), U_MLA + 3)
            for i in (2, 3):
                m = dve.tensor_copy(mkv[:, i, 0:512], ps[4 + i][:, :])
            dve.wait_ge(sem("unit_used"), U_MLA + 4)
            for i in (2, 3):
                m = dve.tensor_copy(mkv[:, i, 512:1024], ps[i][:, :])
            m.then_inc(sem("mla_copied_d"), 1)

            dve.wait_ge(sem("small_loaded"), 16 * 13)
            for v in range(2):
                dve.tensor_tensor(lamv[:, 2 * v, :], lamv[:, 2 * v, :], lamv[:, 2 * v + 1, :], ALU.mult)
                dve.drain()
                dve.tensor_reduce(stat(LAMW + v), lamv[:, 2 * v, :], AX.X, ALU.add)
            dve.drain().then_inc(sem("lam_dots"), 1)
            dve.wait_ge(sem("lam_exp"), 1)
            dve.tensor_tensor(stat(LAM), stat(LAMW + 1), stat(LAMW), ALU.subtract)
            dve.drain()
            dve.tensor_scalar(stat(LAM), stat(LAM), -LAM0, None, ALU.add)
            dve.tensor_scalar(g_sub[:, :], g_sub[:, :], 1.0 - LAM0, None, ALU.mult).then_inc(sem("lam_used"), 1)
            dve.drain()

            attn_dve(dve, A1, 0, N1)
            dve.wait_ge(sem("na_loaded"), 16)
            dve.wait_ge(sem("na_bands"), 4)
            for i in range(2):
                for half in range(2):
                    pp = slice(64 * half, 64 * half + 64)
                    d0 = 3 - (2 * i + half)
                    for jb in range(4):
                        bands = ps[jb][pp, 0:448].rearrange("p (j h d) -> p h d j", h=4, d=7)[:, :, d0:d0 + 4, :]
                        mask = namask[pp, jb * 16:jb * 16 + 16].rearrange("p (a b j) -> p a b j", a=1, b=1)
                        m = dve.tensor_tensor(
                            nabias[pp, :, i, :].rearrange("p h (k j) -> p h k j", k=4)[:, :, :, jb * 16:jb * 16 + 16],
                            bands, mask.to_broadcast([64, 4, 4, 16]), ALU.add)
            m.then_inc(sem("na_bias_made"), 1)
            dve.drain()
            attn_dve(dve, A1, N1, len(STEPS))
            out_dve(dve, "x1_chunk", U_OUT, gt_a)

            dve.scalar_tensor_tensor(sc_f[:, :], sc_f[:, :], 1.0, gvec[:, :], ALU.add, ALU.mult)
            dve.wait_ge(sem("x1_rstd"), 1)
            dve.drain()
            for i in range(3):
                if i < 2:
                    modulate(xres[:, i, :], ybuf[:, i, :], stat(RSTD + i), sc_f[:, :], sh_f[:, :],
                             None).then_inc(sem("h2_ready"), 1)
                if i:
                    turn_dve(dve, "h2", i - 1, XA, 4, (i - 1) * P)
            ffn_dve(dve, "ff1", U_FFN, N_FF, True)
            dve.drain()
            for i in range(2):
                dve.tensor_tensor(ybuf[:, i, :], ybuf[:, i, :], gt_f[:, :], ALU.mult)
                dve.drain()
                m = dve.tensor_tensor(xres[:, i, :], xres[:, i, :], ybuf[:, i, :], ALU.add)
            m.then_inc(sem("xf_ready"), 1)
            dve.wait_ge(sem("g_first_loaded"), 16)
            dve.wait_ge(sem("xf_rstd"), 1)
            for i in range(2):
                m = dve.scalar_tensor_tensor(xres[:, i, :], xres[:, i, :], stat(RSTD + i), gt_a[:, :],
                                             ALU.mult, ALU.mult)
            m.then_inc(sem("x2_ready"), 1)

            dve.wait_ge(sem("g_mix_loaded"), 16)
            dve.wait_ge(sem("x2_rstd"), 1)
            for i in range(3):
                if i < 2:
                    dve.scalar_tensor_tensor(h3[:, i, :], xres[:, i, :], stat(RSTD + i), gvec[:, :],
                                             ALU.mult, ALU.mult).then_inc(sem("h3_ready"), 1)
                if i:
                    turn_dve(dve, "h3", i - 1, XA, 4, (i - 1) * P)
            dve.wait_ge(sem("wf_hi"), 1)
            dve.tensor_tensor(wfl[:, :, :], wf[:, :, :], wfh[:, :, :].bitcast(F32), ALU.subtract).then_inc(sem("wf_lo"), 1)
            dve.wait_ge(sem("f_acc"), 1)
            for i in range(2):
                dve.tensor_tensor(fz[:, 0, i, :], ps[4 + i][:, 0:8], bf[:, :], ALU.add)
            dve.drain()
            dve.scalar_tensor_tensor(fz[:, 1], fz[:, 0], -1.0, fz[:, 0], ALU.mult, ALU.max)
            dve.tensor_scalar(fz[:, 5], fz[:, 0], 0.0, None, ALU.min)
            dve.drain().then_inc(sem("fz_abs"), 1)

            def qkv2_copy(c, b):
                dve.wait_ge(sem("unit_used"), c * 4 + (U_WIN2 + 4))
                dve.tensor_copy(P2[:, 1, bass.ds(c * NCH, NCH)], ps[2 * b + 1][:, :]).then_inc(sem("qkv2_d"), 1)

            def qkv2(i, first=False):
                for b in range(2):
                    g = U_WIN2 // 4 + 2 * i + b
                    lo(dve, g, 0)
                    lo(dve, g, 1)
                    if not (first and b == 0):
                        qkv2_copy(i * 2 + (b - 1), 1 - b)
                    lo(dve, g, 2)
                    lo(dve, g, 3)
            qkv2(0, True)
            with dve.Fori(1, N_QKV2 // 2) as i:
                qkv2(i)
            qkv2_copy(N_QKV2 - 1, 1)
            dve.wait_ge(sem("fz_exp"), 1)
            dve.tensor_scalar(fz[:, 3], fz[:, 2], 1.0, None, ALU.add).then_inc(sem("fz_one"), 1)
            dve.wait_ge(sem("fz_log"), 1)
            dve.tensor_tensor(fz[:, 4], fz[:, 4], fz[:, 5], ALU.subtract)
            dve.drain()
            dve.tensor_scalar(nlf[:, :, :], fz[:, 4], float(HD) ** 0.5, None, ALU.mult).then_inc(sem("nlf_made"), 1)
            dve.wait_ge(sem("masks_loaded"), 48)
            dve.wait_ge(sem("x2_stored"), 16)
            attn_dve(dve, A2, 0, len(STEPS2))

            def gate_mul(n):
                cc = bass.ds(n * NCH, NCH)
                dve.wait_ge(sem("unit_used"), n * 12 + (U_MRG + 12))
                dve.wait_ge(sem("gate_sigmoid"), n * 2 + 2)
                for s in range(4):
                    dve.tensor_tensor(sig[:, s, :], sig[:, s, :], ps[4 + s][:, :], ALU.mult)
                dve.drain()
                for tk in range(2):
                    m = dve.tensor_tensor(mrg[:, tk, cc], sig[:, tk, :], sig[:, 2 + tk, :], ALU.add)
                m.then_inc(sem("merged_chunk"), 1)

            def merge(n, first=False):
                g = 3 * n + U_MRG // 4
                lo(dve, g, 0)
                lo(dve, g, 1)
                if not first:
                    gate_mul(n - 1)
                lo(dve, g, 2)
                lo(dve, g, 3)
                for q in range(4):
                    lo(dve, g + 1, q)
                for q in range(4):
                    lo(dve, g + 2, q)
            merge(0, True)
            with dve.Fori(1, 4) as n:
                merge(n)
            gate_mul(3)
            for i in range(2):
                turn_dve(dve, "mrg", i, XA, 4, i * P)
            out_dve(dve, "x3_chunk", U_OUT2, None)
            dve.wait_ge(sem("g_mlp_loaded"), 16)
            dve.wait_ge(sem("x3_rstd"), 1)
            for i in range(3):
                if i < 2:
                    dve.scalar_tensor_tensor(ybuf[:, i, :], xres[:, i, :], stat(RSTD + i), gvec[:, :],
                                             ALU.mult, ALU.mult).then_inc(sem("h4_ready"), 1)
                if i:
                    turn_dve(dve, "h4", i - 1, XA, 4, (i - 1) * P)
            ffn_dve(dve, "ff2", U_FFN2, N_FF2, False)
            dve.drain()
            for i in range(2):
                m = dve.tensor_tensor(xres[:, i, :], xres[:, i, :], ybuf[:, i, :], ALU.add)
            m.then_inc(sem("x4_ready"), 1)
            dve.drain()
            dve.wait_ge(sem("g_final_loaded"), 16)
            dve.wait_ge(sem("x4_rstd"), 1)
            for i in range(2):
                dve.scalar_tensor_tensor(h3[:, i, :], xres[:, i, :], stat(RSTD + i), gvec[:, :],
                                         ALU.mult, ALU.mult).then_inc(sem("final"), 1)

        @block.tensor
        def _(pe):
            pe.wait_ge(sem("ident_loaded"), 32)
            pe.wait_ge(sem("c_silu"), 1)
            pe.transpose(ps[7][:, 0:32], csig[:, :], ident[0:32, 0:32]).then_inc(sem("c_cols"), 1)
            pe.wait_ge(sem("c_lo"), 1)

            def combine(c, b):
                pe.wait_ge(sem("ada_rows"), c + 1)
                wait(pe, "mod_row", c - 1)
                pe.matmul(ps[2 + b][0:2, :], esel[:, :], rows[:, b, :], start=True, stop=True)\
                    .then_inc(sem("ada_combined"), 1)

            def ada(i, first=False):
                for b in range(2):
                    c = 2 * i + b
                    wait(pe, "ada_rows", c - 1)
                    for q in range(4):
                        pe.wait_ge(sem("lo_made"), 4 * c + q + 1)
                        for j in range(KQ):
                            k = 4 * q + j
                            pe.matmul(ps[b][:, :], cst[:, k, :], whi[:, q % 2, j, :], start=k == 0, stop=False)
                            m = pe.matmul(ps[b][:, :], cst[:, k, :], wlo[:, q % 2, j, :], start=False, stop=k == 15)
                        m.then_inc(sem("unit_used"), 1)
                        if q == 1 and not (first and b == 0):
                            combine(c - 1, 1 - b)
            ada(0, True)
            ada(1)
            with pe.Fori(2, N_ADA // 2) as i:
                ada(i)
            combine(N_ADA - 1, 1)

            turn_pe(pe, "h", [xin[:, i, :] for i in range(4)], 4, "h_ready")
            for c, (col, w, cx) in enumerate(WIN):
                if c == 0:
                    pe.wait_ge(sem("h_lo"), 16)
                wait(pe, "win_copied_a", c - 1)
                wait(pe, "win_copied_d", c - 1)
                toks = (0, 1) if cx is None else (0, 1, 2, 3)
                b = 4 * (c % 2)
                for q in range(4):
                    unit(pe, U_WIN // 4 + c, q, ps[b:b + len(toks)], [XA, XB], 4 * q, q == 0, q == 3, w=w, toks=toks)

            pe.wait_ge(sem("mla_normed"), 1)
            pe.wait_ge(sem("win_copied_a"), len(WIN))
            pe.wait_ge(sem("win_copied_d"), len(WIN))
            for i in range(2):
                for j in range(4):
                    pe.transpose(ps[i][:, j * P:j * P + P], PL[:, i, ML_Q + j * P:ML_Q + j * P + P], ident[:, :])
            for i in range(4):
                ckv = PL[:, i, ML_KV:ML_KV + 320] if i < 2 else PC[:, i - 2, CX_ML:CX_ML + 320]
                for j in range(2):
                    b = (i % 2) * 256 + j * P
                    pe.transpose(ps[2 + i // 2][:, b:b + P], ckv[:, j * P:j * P + P], ident[:, :])
                m = pe.transpose(ps[4][0:64, i * P:i * P + P], ckv[:, 256:320], ident[:, :])
            m.then_inc(sem("mla_turned"), 1)
            g = U_MLA // 4
            pe.wait_ge(sem("mla_lo"), 1)
            pe.wait_ge(sem("kpe_copied"), 1)
            unit(pe, g, 0, ps[0:2], XQ, 0, True, True)
            unit(pe, g, 1, ps[2:4], XQ, 0, True, True, w=256)
            unit(pe, g, 2, ps[4:8], XKV, 0, True, True, k=2, toks=(0, 1, 2, 3))
            pe.wait_ge(sem("mla_copied_a"), 1)
            pe.wait_ge(sem("mla_copied_d"), 1)
            unit(pe, g, 3, ps[0:4], XKV, 0, True, True, k=2, toks=(0, 1, 2, 3))
            pe.wait_ge(sem("mla_copied_a"), 2)
            pe.wait_ge(sem("mla_copied_d"), 2)
            pe.wait_ge(sem("rotated_pe"), 1)
            attn_pe(pe, A1, 0, N1)
            for jb in range(4):
                pe.wait_ge(sem("na_rpb_loaded"), 64)
                pe.wait_ge(sem(f"na_select{jb}"), 16)
                if jb == 0:
                    pe.wait_ge(sem("att_qk_copied"), STEPS[N1 - 1]["a"] + 1)
                    pe.wait_ge(sem("att_exp_done"), N1)
                for j in range(16):
                    m = pe.matmul(ps[jb][:, j * 28:j * 28 + 28], nasel[:, j, :], narpb[:, :], start=True, stop=True)
                m.then_inc(sem("na_bands"), 1)
            pe.wait_ge(sem("na_bias_made"), 1)
            attn_pe(pe, A1, N1, len(STEPS))
            pe.wait_ge(sem("att_out_lo"), 16)
            out_pe(pe, "x1_chunk", U_OUT, XA)
            pe.wait_ge(sem("x1_chunk"), 4)
            turn_pe(pe, "h2", [ybuf[:, i, :] for i in range(2)], 4, "h2_ready")
            pe.wait_ge(sem("h2_lo"), 8)
            ffn_pe(pe, "ff1", U_FFN, N_FF, True)
            pe.wait_ge(sem("ff1_y"), 4 * N_FF)
            turn_pe(pe, "h3", [h3[:, i, :] for i in range(2)], 4, "h3_ready")
            pe.wait_ge(sem("h3_lo"), 8)
            pe.wait_ge(sem("wf_lo"), 1)
            for i in range(2):
                for k in range(16):
                    m = mm3(pe, ps[4 + i][:, 0:8], XA[0][:, k, i * P:i * P + P], XA[1][:, k, i * P:i * P + P],
                            wfh[:, k, :], wfl[:, k, :], k == 0, k == 15)
            m.then_inc(sem("f_acc"), 1)

            def qkv2(i):
                for b in range(2):
                    wait(pe, "qkv2_a", 2 * i + (b - 1))
                    wait(pe, "qkv2_d", 2 * i + (b - 1))
                    for q in range(4):
                        unit(pe, U_WIN2 // 4 + 2 * i + b, q, ps[2 * b:2 * b + 2], XA, 4 * q, q == 0, q == 3)
            qkv2(0)
            with pe.Fori(1, N_QKV2 // 2) as i:
                qkv2(i)
            pe.wait_ge(sem("qkv2_a"), N_QKV2)
            pe.wait_ge(sem("qkv2_d"), N_QKV2)
            pe.wait_ge(sem("nlf_made"), 1)
            pe.wait_ge(sem("masks_loaded"), 48)
            attn_pe(pe, A2, 0, len(STEPS2))
            pe.wait_ge(sem("att2_out_lo"), 16)

            def merge(n):
                g = 3 * n + U_MRG // 4
                wait(pe, "gate_sigmoid", n * 2)
                for b in range(2):
                    for q in range(4):
                        unit(pe, g + b, q, ps[2 * b:2 * b + 2], XA, 4 * q, q == 0, q == 3)
                wait(pe, "merged_chunk", n)
                for q in range(4):
                    b = 4 if q < 2 else 6
                    unit(pe, g + 2, q, ps[b:b + 2], XB, 4 * q, q % 2 == 0, q % 2 == 1)
            merge(0)
            with pe.Fori(1, 4) as n:
                merge(n)
            pe.wait_ge(sem("merged_chunk"), 4)
            turn_pe(pe, "mrg", [mrg[:, i, :] for i in range(2)], 4, "merged_chunk")
            pe.wait_ge(sem("mrg_lo"), 8)
            out_pe(pe, "x3_chunk", U_OUT2, XA)
            pe.wait_ge(sem("x3_chunk"), 4)
            turn_pe(pe, "h4", [ybuf[:, i, :] for i in range(2)], 4, "h4_ready")
            pe.wait_ge(sem("h4_lo"), 8)
            ffn_pe(pe, "ff2", U_FFN2, N_FF2, False)

        @block.gpsimd
        def _(pool):
            for dst, src in ((cos128, t["cos128"]), (sin128, t["sin128"]), (cos64, t["cos64"]), (sin64, t["sin64"])):
                pool.dma_start(dst[:, :, :], src).then_inc(sem("small_loaded"), 16)
            for dst, src, n in ((g_gq, t["gqa_gq"], 128), (g_gk, t["gqa_gk"], 128), (g_sub, t["diff_gsub"], 128),
                                (g_mq, t["mla_gq"], 512), (g_mkv, t["mla_gkv"], 256)):
                pool.dma_start(dst[:, :], bcast(src, n)).then_inc(sem("small_loaded"), 16)
            for i, name in enumerate(("diff_lq1", "diff_lk1", "diff_lq2", "diff_lk2")):
                pool.dma_start(lamv[:, i, :], bcast(t[name], 64)).then_inc(sem("small_loaded"), 16)
            pool.dma_start(gvec[:, :], bcast(t["g_attn"], D)).then_inc(sem("mods_loaded"), 16)

            def store(c, b):
                pool.wait_ge(sem("mod_row"), c + 1)
                pool.dma_start(mod_d[:, bass.ds(c * NCH, NCH)], modsb[:, b, :]).then_inc(sem(f"mod_stored{b}"), 16)
            with pool.Fori(0, N_ADA // 2) as i:
                store(2 * i, 0)
                store(2 * i + 1, 1)
            for b in range(2):
                pool.wait_ge(sem(f"mod_stored{b}"), 16 * (N_ADA // 2))
            pool.wait_ge(sem("halves"), 1)
            rstd_pool(pool, "x", 4)
            pool.wait_ge(sem("x_rstd"), 1)
            for v in range(2):
                for s, col in ((0, D), (1, 0)):
                    pool.dma_start(mods[:, 2 * v + s, :], bcast(mod_d[v:v + 1, col:col + D], D))\
                        .then_inc(sem("mods_loaded"), 16)

            def norm(x, g, width, n, col):
                pool_rstd(pool, stat(col, n), stat(col, n), n, width)
                pool.drain()
                pool.tensor_tensor(x, x, stat(col, n).rearrange("p (a b) -> p a b", b=1)
                                   .to_broadcast([P, n, width]), ALU.mult)
                pool.drain()
                pool.tensor_tensor(x, x, g[:, 0:width].rearrange("p (a b) -> p a b", a=1)
                                   .to_broadcast([P, n, width]), ALU.mult)
                pool.drain()

            def rope(x, cos, sin, half, n):
                a = ropeA[:, 0:2 * n * half].rearrange("p (n s h) -> p n s h", n=n, s=2)
                b = ropeB[:, 0:2 * n * half].rearrange("p (n s h) -> p n s h", n=n, s=2)
                for s in range(2):
                    c3 = cos.rearrange("p (a h) -> p a h", a=1).to_broadcast([P, n, half])
                    s3 = sin.rearrange("p (a h) -> p a h", a=1).to_broadcast([P, n, half])
                    pool.tensor_tensor(a[:, :, s, :], x[:, :, s, :], c3, ALU.mult)
                    pool.tensor_tensor(b[:, :, s, :], x[:, :, s, :], s3, ALU.mult)
                pool.drain()
                pool.tensor_tensor(x[:, :, 0, :], a[:, :, 0, :], b[:, :, 1, :], ALU.subtract)
                m = pool.tensor_tensor(x[:, :, 1, :], b[:, :, 0, :], a[:, :, 1, :], ALU.add)
                pool.drain()
                return m

            def copied(c):
                if c in WIN_SQ:
                    pool.wait_ge(sem("win_squared"), sorted(WIN_SQ).index(c) + 1)
                pool.wait_ge(sem("win_copied_a"), c + 1)
                pool.wait_ge(sem("win_copied_d"), c + 1)

            pool.wait_ge(sem("h_ready"), 4)
            pool.wait_ge(sem("small_loaded"), 16 * 13)
            copied(0)
            for i in range(2):
                norm(PL[:, i:i + 1, ML_Q:ML_Q + 512], g_mq, 512, 1, NCQ + i)
            copied(1)
            for i in range(2):
                norm(PL[:, i:i + 1, ML_KV:ML_KV + 256], g_mkv, 256, 1, NCKV + i)
                norm(PC[:, i:i + 1, CX_ML:CX_ML + 256], g_mkv, 256, 1, NCKV + 2 + i)
                rope(PL[:, i, ML_PE:ML_PE + 64].rearrange("p (n s h) -> p n s h", n=1, s=2), cos64[:, i, :],
                     sin64[:, i, :], 32, 1)
            pool.drain().then_inc(sem("mla_normed"), 1)
            for c, col in ((2, DF_Q), (3, DF_K)):
                copied(c)
                for i in range(2):
                    rope(PL[:, i, col:col + 512].rearrange("p (n s h) -> p n s h", s=2, h=32), cos64[:, i, :],
                         sin64[:, i, :], 32, 8)
            copied(5)
            for i in range(2):
                norm(PL[:, i, GQ_Q:GQ_Q + 512].rearrange("p (n d) -> p n d", d=HD), g_gq, HD, 4, NGQ + 4 * i)
                rope(PL[:, i, GQ_Q:GQ_Q + 512].rearrange("p (n s h) -> p n s h", s=2, h=64), cos128[:, i, :],
                     sin128[:, i, :], 64, 4)
            copied(6)
            for i in range(2):
                norm(PL[:, i, GQ_K:GQ_K + 256].rearrange("p (n d) -> p n d", d=HD), g_gk, HD, 2, NGK + 2 * i)
                norm(PC[:, i, CX_GK:CX_GK + 256].rearrange("p (n d) -> p n d", d=HD), g_gk, HD, 2, NGK + 4 + 2 * i)
                rope(PL[:, i, GQ_K:GQ_K + 256].rearrange("p (n s h) -> p n s h", s=2, h=64), cos128[:, i, :],
                     sin128[:, i, :], 64, 2)
            pool.wait_ge(sem("mla_copied_a"), 1)
            pool.wait_ge(sem("mla_copied_d"), 1)
            for i in range(2):
                q = PL[:, i, ML_Q:ML_Q + 768].rearrange("p (n d) -> p n d", d=192)[:, :, 128:192]
                rope(q.rearrange("p n (s h) -> p n s h", s=2), cos64[:, i, :], sin64[:, i, :], 32, 4)
            pool.drain().then_inc(sem("rotated_pe"), 1)

            pool.wait_ge(sem("lam_used"), 1)
            with nc.allow_non_contiguous_dma(reason="31 x 28 table, once"):
                for h in range(4):
                    pool.dma_start(narpb[:, h * 7:h * 7 + 7],
                                   t["na_rpb"][0, h, 4:11, :].rearrange("r m -> m r")).then_inc(sem("na_rpb_loaded"), 16)
            pool.dma_start(namask[:, :], t["na_mask"]).then_inc(sem("na_loaded"), 16)
            for h in range(4):
                if h == 0:
                    pool.wait_ge(sem("att_out"), 4)
                    pool.dma_start(nasel[:, :, :], t["na_select"][:, 0:16, :]).then_inc(sem("na_select0"), 16)
                pool.wait_ge(sem("diff_squares"), h + 1)
                pool_rstd(pool, stat(ORS, 2), stat(OSS, 2), 2, HD).then_inc(sem("diff_rstd"), 1)
            for jb in range(1, 4):
                pool.wait_ge(sem("na_bands"), jb)
                pool.dma_start(nasel[:, :, :], t["na_select"][:, 16 * jb:16 * jb + 16, :]).then_inc(sem(f"na_select{jb}"), 16)

            pool.wait_ge(sem("att_out_lo"), 16)
            pool.dma_start(xres[:, :, :], x_v).then_inc(sem("x1_chunk_loaded"), 16)
            for dst, n in ((gt_a, 2), (sh_f, 3), (sc_f, 4), (gt_f, 5)):
                pool.dma_start(dst[:, :], bcast(mod_d[0:1, n * D:n * D + D], D)).then_inc(sem("x1_chunk_loaded"), 16)
            pool.dma_start(gvec[:, :], bcast(t["g_ffn"], D)).then_inc(sem("x1_chunk_loaded"), 16)
            rstd_pool(pool, "x1", 2)
            pool.wait_ge(sem("x1_chunk"), 4)
            pool.dma_start(gt_a[:, :], bcast(t["g_final"].rearrange("(a n) -> a n", a=1), D))\
                .then_inc(sem("g_first_loaded"), 16)
            pool.wait_ge(sem("h2_ready"), 2)
            pool.dma_start(gvec[:, :], bcast(t["norm_mix_g_2"].rearrange("(a n) -> a n", a=1), D))\
                .then_inc(sem("g_mix_loaded"), 16)
            with nc.allow_non_contiguous_dma(reason="eight columns of w_in_2"):
                pool.dma_start(wf[:, :, :], t["w_in_2"].rearrange("(k p) n -> p k n", p=P)[:, :, 6144:6152])\
                    .then_inc(sem("wf_loaded"), 16)
            pool.dma_start(bf[:, :], bcast(t["b_forget_2"].rearrange("(a n) -> a n", a=1), 8)).then_inc(sem("wf_loaded"), 16)
            for dst, src in ((distm, t["distance"]), (causal, t["causal"]), (tri, t["triangle"])):
                pool.dma_start(dst[:, :, :], src).then_inc(sem("masks_loaded"), 16)
            rstd_pool(pool, "xf", 2)
            rstd_pool(pool, "x2", 2)
            pool.wait_ge(sem("x2_ready"), 1)
            pool.dma_start(x2_d, xres[:, :, :]).then_inc(sem("x2_stored"), 16)
            pool.wait_ge(sem("h3_ready"), 2)
            pool.dma_start(gvec[:, :], bcast(t["norm_mlp_g_2"].rearrange("(a n) -> a n", a=1), D))\
                .then_inc(sem("g_mlp_loaded"), 16)
            pool.wait_ge(sem("x2_stored"), 16)
            pool.wait_ge(sem("att2_out_lo"), 16)
            pool.dma_start(xres[:, :, :], x2_d).then_inc(sem("x3_chunk_loaded"), 16)
            rstd_pool(pool, "x3", 2)
            pool.wait_ge(sem("h4_ready"), 2)
            pool.dma_start(gvec[:, :], bcast(t["norm_final_g_2"].rearrange("(a n) -> a n", a=1), D))\
                .then_inc(sem("g_final_loaded"), 16)
            rstd_pool(pool, "x4", 2)


_INS = ["x", "c", "ctx", "c_ctx", "w_ada", "b_ada", "g_attn", "g_ffn", "w_in", "w_out", "na_rpb", "gqa_gq",
        "gqa_gk", "mla_gq", "mla_gkv", "mla_wuq", "mla_wukv", "diff_lq1", "diff_lk1", "diff_lq2", "diff_lk2",
        "diff_gsub", "ffn_wg", "ffn_wu", "ffn_wd", "g_final", "norm_mix_g_2", "w_in_2", "b_forget_2", "w_proj_a_2",
        "w_proj_b_2", "w_out_2", "norm_mlp_g_2", "w_up_2", "w_down_2", "norm_final_g_2"]


def constants():
    tok = np.arange(SEQ)
    row, col = (tok // 64).astype(np.float32), (tok % 64).astype(np.float32)

    def rope(dim):
        axis = dim // 2
        inv = (1.0 / (np.float32(10000.0) ** (np.arange(0, axis, 2, dtype=np.float32) / np.float32(axis)))).astype(np.float32)
        ang = np.concatenate([row[:, None] * inv, col[:, None] * inv], axis=-1).astype(np.float32)
        tile = lambda a: np.ascontiguousarray(a.reshape(2, P, -1).transpose(1, 0, 2).astype(np.float32))
        return tile(np.cos(ang)), tile(np.sin(ang))
    cos128, sin128 = rope(128)
    cos64, sin64 = rope(64)
    select = np.zeros((P, 2), np.float32)
    select[[0, 32], 0] = 1
    select[[64, 96], 1] = 1
    c, j = np.arange(P) % 64, np.arange(64)
    start = np.clip(c - 8, 0, 48)
    inside = (j[None] >= start[:, None]) & (j[None] < start[:, None] + 16)
    na_mask = np.where(inside, 0.0, -1e30).astype(np.float32)
    na_select = (np.arange(31)[:, None, None] == (j[None, :, None] - c[None, None, :] + 15)).astype(np.float32)
    q = np.arange(SEQ)
    dist = (q[:, None] - q[None, :]).astype(np.float32)
    tiles = lambda a: np.ascontiguousarray(a.astype(np.float32).reshape(2, P, SEQ).transpose(1, 0, 2))
    return {"identity": np.eye(P, dtype=np.float32), "row_select": select, "cos128": cos128, "sin128": sin128,
            "cos64": cos64, "sin64": sin64, "na_mask": na_mask, "na_select": np.ascontiguousarray(na_select),
            "distance": tiles(np.where(dist >= 0, dist, 1e30)), "causal": tiles(np.where(dist >= 0, 0.0, -1e30)),
            "triangle": tiles(q[:, None] <= q[None, :])}


def kernel(**inputs):
    import concourse.bacc as bacc
    from concourse.bass_utils import run_bass_kernel_spmd

    nc = bacc.Bacc("TRN2", target_bir_lowering=False, num_devices=1)
    arrays, t = {}, {}
    for name, a in [(n, inputs[n]) for n in _INS] + list(constants().items()):
        a = np.ascontiguousarray(a)
        arrays[f"in_{name}"] = a
        t[name] = nc.dram_tensor(f"in_{name}", a.shape, mybir.dt.from_np(a.dtype), kind="ExternalInput").ap()
    t["out"] = nc.dram_tensor("out_x", (1, SEQ, D), F32, kind="ExternalOutput").ap()
    build(nc, t)
    r = run_bass_kernel_spmd(nc, [arrays], core_ids=[0])
    return r.results[0]["out_x"]
```

```python
from contextlib import ExitStack
import math

import numpy as np

import concourse.bass as bass
from concourse import mybir
from concourse.alu_op_type import AluOpType as ALU

F32 = mybir.dt.float32
F32R = mybir.dt.float32r
ACT = mybir.ActivationFunctionType
AX = mybir.AxisListType

P = 128
D = 2048
SEQ = 256
NCH = 512
KQ = 4
HD = 128
EPS = 1e-6
D_IN = 4928
D_FF = 5632
D_IN_2 = 10248
D_FF_2 = 8192
KB = 1024
BASE = 16512

NA_Q, NA_K, NA_V, GQ_Q, GQ_K, GQ_V = 0, 512, 1024, 1536, 2048, 2304
ML_Q, ML_KV, ML_PE, DF_Q, DF_K, DF_V = 2560, 3072, 3328, 3392, 3904, 4416
CX_ML, CX_DK, CX_DV, CX_GK, CX_NK, CX_NV, CX_W = 0, 320, 832, 1344, 1856, 2368, 2880
WIN = [(ML_Q, 512, None), (ML_KV, 320, CX_ML), (DF_Q, 512, None), (DF_K, 512, CX_DK), (DF_V, 512, CX_DV),
       (GQ_Q, 512, None), (GQ_K, 512, CX_GK), (NA_Q, 512, None), (NA_K, 512, CX_NK), (NA_V, 512, CX_NV)]

N_ADA = 6 * D // NCH
N_ADA_1 = 2 * D // NCH
U_MIX = 4 * N_ADA_1
U_MLA = U_MIX + 4 * len(WIN) + 4 * (N_ADA - N_ADA_1)
U_OUT = U_MLA + 4
U_FFN = U_OUT + 4 * (D // NCH)
N_FF = D_FF // NCH
U_WIN2 = U_FFN + 12 * N_FF
N_QKV2 = 12
U_MRG = U_WIN2 + 4 * N_QKV2
U_OUT2 = U_MRG + 12 * (D // NCH)
U_FFN2 = U_OUT2 + 4 * (D // NCH)
N_FF2 = D_FF_2 // NCH
LAM0 = 0.8 - 0.6 * math.exp(-0.3 * 0)


def mixed_units():
    units, a = [], N_ADA_1
    for c in range(len(WIN)):
        for q in range(4):
            if c not in (4, 9):
                units += [("ada", a + q // 2, 2 * (q % 2)), ("ada", a + q // 2, 2 * (q % 2) + 1)]
            units.append(("win", c, q))
        a += 0 if c in (4, 9) else 2
    return units


MIX = mixed_units()
LAST = {(kind, c): n for n, (kind, c, q) in enumerate(MIX) if q == 3}


def ada_banks(c):
    return (2, 3) if c < N_ADA_1 + 8 else (6, 7)


def head_steps():
    steps, a, d = [], 0, 0
    for kind, n in (("mla", 4), ("diff", 8), ("gqa", 4), ("na", 4)):
        for m in range(n):
            half = m % 2 if kind == "diff" else 0
            head = m // 2 if kind == "diff" else m
            turn, value = half == 0, kind != "diff" or half == 1
            steps.append(dict(kind=kind, head=head, half=half, a=a if turn else a - 1, turn=turn,
                              d=d if value else None))
            a += turn
            d += value
    return steps


def head_steps_2():
    return [dict(kind=k, head=h, half=0, a=n, turn=True, d=n)
            for n, (k, h) in enumerate([("moba", h) for h in range(8)] + [("fox", h) for h in range(8)])]


def build(nc, t):
    ctx = ExitStack()
    with ctx:
        sems = {}

        def sem(name):
            if name not in sems:
                sems[name] = ctx.enter_context(nc.semaphore(name))
            return sems[name]

        def at(name, shape, dt, kb):
            return nc.alloc_sbuf_tensor_at(name, shape, dt, offset=BASE + int(kb * KB))

        def wait(eng, name, value):
            if isinstance(value, int) and value <= 0:
                return
            eng.wait_ge(sem(name), value)

        ps = [ctx.enter_context(nc.psum_tensor(f"bank{b}", [P, 512], F32)) for b in range(8)]

        raw = at("w_raw", [P, 4, KQ, NCH], F32, 0)
        whi = at("w_hi", [P, 2, KQ, NCH], F32R, 32)
        wlo = at("w_lo", [P, 2, KQ, NCH], F32R, 48)
        XA = (at("xa_hi", [P, 16, SEQ], F32R, 64), at("xa_lo", [P, 16, SEQ], F32R, 80))
        XB = (at("xb_hi", [P, 16, SEQ], F32R, 96), at("xb_lo", [P, 16, SEQ], F32R, 112))
        cst = at("c_stationary", [P, 16, 4], F32R, 198.75)
        rows_1 = at("ada_rows", [5, 2, NCH], F32, 160)
        scale_g = at("scale_g", [P, 2, NCH], F32, 164)
        spread = at("row_spread", [5, 2, 128], F32, 180)
        nab_1 = at("na_bias_early", [P, 4, 2, 256], F32, 64)
        band = at("na_band", [63, 191], F32, 72)
        bandr = at("na_band_r", [63, 191], F32R, 73)
        narpbr = at("na_rpb_hi_lo", [63, 28], F32R, 74)
        namask = at("na_mask", [P, 64], F32, 104)
        narpb = at("na_rpb_T", [63, 28], F32, 104.25)
        xin = at("x_in", [P, 4, D], F32, 128)
        crow = at("c_rows", [32, 128], F32, 178)
        csig = at("c_silu", [32, 128], F32, 178.5)
        ccol = at("c_cols", [P, 32], F32, 179)
        esel = at("row_select", [5, 2], F32, 199)
        junk = at("squares", [P, D], F32, 168)
        PL = at("proj_x", [P, 2, D_IN], F32, 128)
        PC = at("proj_ctx", [P, 2, CX_W], F32, 128 + 38.5)
        kpeT = at("mla_kpe_T", [64, 512], F32, 128 + 61)

        def rows_of(c, b):
            return rows_1[:, b, :] if c < N_ADA_1 else PC[0:5, b, CX_NV:CX_NV + NCH]

        def late_row(b):
            return PL[0:1, b, NA_V:NA_V + NCH]
        XQ = (at("mla_cq_hi", [P, 4, SEQ], F32R, 96), at("mla_cq_lo", [P, 4, SEQ], F32R, 100))
        XKV = (at("mla_ckv_hi", [P, 2, 512], F32R, 104), at("mla_ckv_lo", [P, 2, 512], F32R, 108))
        mkv = at("mla_kv", [P, 4, 1024], F32, 112)
        kT = at("k_T", [P, 2, 512], F32, 96)
        qT = at("q_T", [P, 2, 512], F32, 100)
        probs = at("probs", [P, 2, 2, 512], F32, 104)
        probsT = at("probs_T", [P, 2, 4, SEQ], F32, 192 + 7.75)
        nabias = at("na_bias", [P, 4, 2, 256], F32, 112)
        od = at("diff_out", [P, 2, 2, 128], F32, 120)
        ident = at("identity", [P, P], F32, 192)
        small = at("small", [P, 64], F32, 192.5)
        cos128 = at("cos128", [P, 2, 64], F32, 192.75)
        sin128 = at("sin128", [P, 2, 64], F32, 193.25)
        cos64 = at("cos64", [P, 2, 32], F32, 193.75)
        sin64 = at("sin64", [P, 2, 32], F32, 194)
        g_gq = at("gqa_gq_row", [P, 128], F32, 194.25)
        g_gk = at("gqa_gk_row", [P, 128], F32, 194.75)
        g_sub = at("diff_gsub_row", [P, 128], F32, 195.25)
        g_mq = at("mla_gq_row", [P, 512], F32, 195.75)
        g_mkv = at("mla_gkv_row", [P, 256], F32, 197.75)
        lamv = at("diff_lambdas", [P, 4, 64], F32, 191)
        gvec = at("g_row", [P, D], F32, 192 + 7.75)
        ropeA = at("rope_a", [P, 512], F32, 192 + 7.75)
        ropeB = at("rope_b", [P, 512], F32, 192 + 9.75)
        psq = at("win_squares", [P, 512], F32, 192 + 11.75)
        pstat = at("pool_stats", [P, 24], F32, 192 + 15.75)
        xres = at("x_res", [P, 2, D], F32, 128)
        gt_a = at("gt_a", [P, D], F32, 144)
        sc_f = at("sc_f", [P, D], F32, 152)
        sh_f = at("sh_f", [P, D], F32, 160)
        gt_f = at("gt_f", [P, D], F32, 168)
        ybuf = at("y_sum", [P, 2, D], F32, 176)
        tmp = at("gated", [P, 2, NCH], F32, 112)
        squared = at("squared", [P, 2, NCH], F32, 104)
        act_g = at("ffn_gate", [P, 2, NCH], F32, 116)
        act_a = at("ffn_act", [P, 2, NCH], F32, 120)
        XF = (at("ffn_act_hi", [P, 4, SEQ], F32R, 96), at("ffn_act_lo", [P, 4, SEQ], F32R, 100))
        h3 = at("h_mix", [P, 2, D], F32, 160)
        P2 = at("proj_2", [P, 2, 6144], F32, 144)
        wf = at("w_forget", [P, 16, 8], F32, 124)
        wfh = at("w_forget_hi", [P, 16, 8], F32R, 124.5)
        wfl = at("w_forget_lo", [P, 16, 8], F32R, 125)
        bf = at("b_forget", [P, 8], F32, 125.5)
        fz = at("forget_work", [P, 6, 2, 8], F32, 126)
        zT = at("forget_z_T", [8, SEQ], F32, 108)
        nlf = at("neg_log_forget", [P, 2, 8], F32, 192 + 15.75)
        distm = at("distance", [P, 2, 256], F32, 192.75)
        causal = at("causal_mask", [P, 2, 256], F32, 194.75)
        tri = at("triangle", [P, 2, 256], F32, 196.75)
        kT2 = at("k_T_2", [P, 2, 256], F32, 128)
        qT2 = at("q_T_2", [P, 2, 256], F32, 130)
        probs2 = at("probs_2", [P, 2, 2, 256], F32, 132)
        probsT2 = at("probs_T_2", [P, 2, 2, SEQ], F32, 136)
        sig = at("gate_sig", [P, 4, NCH], F32, 160)
        mrg = at("merged", [P, 2, D], F32, 144)

        def stat(n, w=1):
            return small[:, n:n + w]

        SS, RSTD = 0, 4
        MX, NM, SUM, RIN = 8, 12, 16, 20
        OSS, ORS = 24, 28
        LAM, LAMW = 32, 34
        NCQ, NCKV, NGQ, NGK = 36, 38, 42, 50
        SQ1, SQ2 = 36, 44
        WIN_SQ = {0: (NCQ, 512, 1, 2), 1: (NCKV, 256, 1, 4), 5: (NGQ, HD, 4, 2), 6: (NGK, HD, 2, 4)}

        w_in_v = t["w_in"][0].rearrange("(q k p) n -> p q k n", p=P, k=KQ)
        w_ada_v = t["w_ada"][0].rearrange("(q k p) n -> p q k n", p=P, k=KQ)
        w_out_v = t["w_out"][0].rearrange("(q k p) n -> p q k n", p=P, k=KQ)
        wg_v = t["ffn_wg"][0].rearrange("(q k p) n -> p q k n", p=P, k=KQ)
        wu_v = t["ffn_wu"][0].rearrange("(q k p) n -> p q k n", p=P, k=KQ)
        wd_v = t["ffn_wd"][0].rearrange("(q k p) n -> p q k n", p=P, k=KQ)
        wuq_v = t["mla_wuq"][0].rearrange("(k p) n -> p k n", p=P)
        wukv_v = t["mla_wukv"][0].rearrange("(k p) n -> p k n", p=P)
        w_in2_v = t["w_in_2"].rearrange("(q k p) n -> p q k n", p=P, k=KQ)
        wpa_v = t["w_proj_a_2"].rearrange("(q k p) n -> p q k n", p=P, k=KQ)
        wpb_v = t["w_proj_b_2"].rearrange("(q k p) n -> p q k n", p=P, k=KQ)
        w_out2_v = t["w_out_2"].rearrange("(q k p) n -> p q k n", p=P, k=KQ)
        w_up_v = t["w_up_2"].rearrange("(q k p) n -> p q k n", p=P, k=KQ)
        w_down_v = t["w_down_2"].rearrange("(q k p) n -> p q k n", p=P, k=KQ)
        x_v = t["x"][0].rearrange("(t p) n -> p t n", p=P)
        ctx_v = t["ctx"][0].rearrange("(t p) n -> p t n", p=P)
        out_v = t["out"][0].rearrange("(t p) n -> p t n", p=P)
        mod_d = nc.dram_tensor("mods_scratch", (1, 4 * D), F32).ap()
        nab_d = nc.dram_tensor("na_bias_scratch", (P, 4, 2, 256), F32).ap()
        x2_d = nc.dram_tensor("x2_scratch", (P, 2, D), F32).ap()

        def bcast(row, n):
            return row.to_broadcast([P, n])

        STEPS, STEPS2 = head_steps(), head_steps_2()

        def load(sp, u4, q, src, k=KQ, w=NCH):
            if isinstance(src, tuple):
                v, off, axis = src
                off = sp.snap(off)
                src = v[:, :, bass.ds(off, NCH)] if axis == "col" else v[:, bass.ds(off, KQ), :]
            wait(sp, "lo_made", 8 * u4 + (2 * q - 6))
            sp.dma_start(raw[:, q, 0:k, 0:w], src).then_inc(sem(f"landed{q}"), 16)

        def at_col(v, col):
            return v[:, :, col:col + NCH] if isinstance(col, int) else (v, col, "col")

        def used(eng, units):
            eng.wait_ge(sem("unit_used"), units * 2)

        def hi(act, u4, q, k=KQ, w=NCH):
            act.wait_ge(sem(f"landed{q}"), 16 * u4 + 16)
            for h in range(2):
                ks = slice(h * k // 2, (h + 1) * k // 2)
                wait(act, "unit_used", 8 * u4 + (2 * q - 3 + h))
                act.activation(whi[:, q % 2, ks, 0:w], raw[:, q, ks, 0:w], ACT.Copy).then_inc(sem("hi_made"), 1)

        def lo(dve, u4, q, k=KQ, w=NCH):
            for h in range(2):
                ks = slice(h * k // 2, (h + 1) * k // 2)
                dve.wait_ge(sem("hi_made"), 8 * u4 + (2 * q + 1 + h))
                dve.tensor_tensor(wlo[:, q % 2, ks, 0:w], raw[:, q, ks, 0:w],
                                  whi[:, q % 2, ks, 0:w].bitcast(F32), ALU.subtract).then_inc(sem("lo_made"), 1)

        def mm3(pe, out, xh, xl, wh, wl, first, last):
            pe.matmul(out, xh, wh, start=first, stop=False)
            pe.matmul(out, xh, wl, start=False, stop=False)
            return pe.matmul(out, xl, wh, start=False, stop=last)

        def unit(pe, u4, q, outs, X, k0, first, last, k=KQ, w=NCH, toks=(0, 1)):
            for j in range(k):
                if j % (k // 2) == 0:
                    pe.wait_ge(sem("lo_made"), 8 * u4 + (2 * q + 1 + 2 * j // k))
                for out, tk in zip(outs, toks):
                    Xt = X[tk // 2] if isinstance(X, list) else X
                    c = slice((tk % 2) * P, (tk % 2) * P + P) if isinstance(X, list) else slice(tk * P, tk * P + P)
                    m = mm3(pe, out[:, 0:w], Xt[0][:, k0 + j, c], Xt[1][:, k0 + j, c],
                            whi[:, q % 2, j, 0:w], wlo[:, q % 2, j, 0:w],
                            first and j == 0, last and j == k - 1)
                if (j + 1) % (k // 2) == 0:
                    m.then_inc(sem("unit_used"), 1)

        def turn_h_pe(pe, g):
            for i in range(4):
                pe.wait_ge(sem("h_ready"), 4 * g + i + 1)
                wait(pe, "h_lo", 4 * g + i - 3)
                for j in range(4):
                    m = pe.transpose(ps[4 + i][:, j * P:j * P + P], xin[:, i, (4 * g + j) * P:(4 * g + j + 1) * P],
                                     ident[:, :])
                m.then_inc(sem("h_turned"), 1)

        def turn_h_act(act, g):
            if g == 0:
                act.wait_ge(sem("na_bias_stored"), 16)
            for i in range(4):
                act.wait_ge(sem("h_turned"), 4 * g + i + 1)
                act.activation((XA, XB)[i // 2][0][:, 4 * g:4 * g + 4, (i % 2) * P:(i % 2) * P + P],
                               ps[4 + i][:, :].rearrange("p (j t) -> p j t", j=4), ACT.Copy).then_inc(sem("h_hi"), 1)

        def turn_h_dve(dve, g):
            for i in range(4):
                X, c = (XA, XB)[i // 2], (i % 2) * P
                dve.wait_ge(sem("h_hi"), 4 * g + i + 1)
                dve.tensor_tensor(X[1][:, 4 * g:4 * g + 4, c:c + P], ps[4 + i][:, :].rearrange("p (j t) -> p j t", j=4),
                                  X[0][:, 4 * g:4 * g + 4, c:c + P].bitcast(F32), ALU.subtract).then_inc(sem("h_lo"), 1)

        def piece_bank(n, first):
            return ps[(n + first) % 8]

        def start_pe(pe, T, srcs, U, first, ready):
            def turn(g):
                for i, src in enumerate(srcs):
                    ready(g, i)
                    for j in range(4):
                        m = pe.transpose(piece_bank(2 * g + i, first)[:, j * P:j * P + P],
                                         src[:, (4 * g + j) * P:(4 * g + j + 1) * P], ident[:, :])
                    m.then_inc(sem(T + "_turned"), 1)
            for g in range(3):
                turn(g)
            for q in range(4):
                pe.wait_ge(sem(T + "_lo"), 2 * q + 2)
                unit(pe, U // 4, q, ps[first:first + 2], XA, 4 * q, q == 0, q == 3)
                if q == 0:
                    turn(3)

        def start_act(act, T, U, first):
            for g in range(4):
                for i in range(2):
                    n = 2 * g + i
                    act.wait_ge(sem(T + "_turned"), n + 1)
                    act.activation(XA[0][:, 4 * g:4 * g + 4, i * P:i * P + P],
                                   piece_bank(n, first)[:, :].rearrange("p (j t) -> p j t", j=4),
                                   ACT.Copy).then_inc(sem(T + "_hi"), 1)
                if g >= 2:
                    hi(act, U // 4, g)

        def start_dve(dve, T, U, first, make):
            def split(g):
                for i in range(2):
                    n = 2 * g + i
                    dve.wait_ge(sem(T + "_hi"), n + 1)
                    dve.tensor_tensor(XA[1][:, 4 * g:4 * g + 4, i * P:i * P + P],
                                      piece_bank(n, first)[:, :].rearrange("p (j t) -> p j t", j=4),
                                      XA[0][:, 4 * g:4 * g + 4, i * P:i * P + P].bitcast(F32),
                                      ALU.subtract).then_inc(sem(T + "_lo"), 1)
            make(0)
            make(1)
            split(0)
            make(2)
            split(1)
            make(3)
            split(2)
            lo(dve, U // 4, 2)
            split(3)
            lo(dve, U // 4, 3)

        def squares_of(act, T, c, done, x, col):
            act.wait_ge(sem(done), c + 1)
            act.drain()
            for i in range(2):
                m = act.activation(squared[:, i, :], x[:, i, c * NCH:(c + 1) * NCH], ACT.Square,
                                   accum_out=stat(col + 4 * i + c))
            m.then_inc(sem(T + "_squares"), 1)

        def sum_squares(dve, T, count, groups):
            dve.wait_ge(sem(T + "_squares"), count)
            for col, out in groups:
                m = dve.tensor_reduce(stat(out, 2), stat(col, 8).rearrange("p (i c) -> p i c", i=2), AX.X, ALU.add)
            m.then_inc(sem(T + "_summed"), 1)

        def pool_rstd(pool, out, sums, width, n):
            pool.tensor_scalar(out, sums, 1.0 / n, EPS, ALU.mult, ALU.add)
            pool.drain()
            return pool.tensor_tensor(out, out, pstat[:, 16:16 + width], ALU.pow)

        def srcs_of(s):
            h, kind = s["head"], s["kind"]
            c = h * HD

            def lc(lat, cx):
                return [PL[:, 0, lat:lat + HD], PL[:, 1, lat:lat + HD],
                        PC[:, 0, cx:cx + HD], PC[:, 1, cx:cx + HD]]
            if kind == "mla":
                q0 = ML_Q + h * 192
                return dict(q=[PL[:, i, q0:q0 + HD] for i in range(2)],
                            qpe=[PL[:, i, q0 + HD:q0 + 192] for i in range(2)],
                            k=[mkv[:, i, h * 256:h * 256 + HD] for i in range(4)],
                            v=[mkv[:, i, h * 256 + HD:h * 256 + 256] for i in range(4)],
                            o=8 + h, scale=192 ** -0.5)
            if kind == "diff":
                return dict(q=[PL[:, i, DF_Q + c:DF_Q + c + HD] for i in range(2)],
                            k=lc(DF_K + c, CX_DK + c), v=lc(DF_V + c, CX_DV + c), o=12 + h, scale=64 ** -0.5)
            if kind == "gqa":
                e = (h // 2) * HD
                return dict(q=[PL[:, i, GQ_Q + c:GQ_Q + c + HD] for i in range(2)],
                            k=lc(GQ_K + e, CX_GK + e), v=lc(GQ_V + e, CX_GK + 256 + e), o=4 + h, scale=HD ** -0.5)
            if kind == "na":
                return dict(q=[PL[:, i, NA_Q + c:NA_Q + c + HD] for i in range(2)],
                            k=lc(NA_K + c, CX_NK + c), v=lc(NA_V + c, CX_NV + c), o=h, scale=HD ** -0.5)
            o = 0 if kind == "moba" else 3072
            return dict(q=[P2[:, i, o + c:o + c + HD] for i in range(2)],
                        k=[P2[:, i, o + 1024 + c:o + 1024 + c + HD] for i in range(2)],
                        v=[P2[:, i, o + 2048 + c:o + 2048 + c + HD] for i in range(2)],
                        o=h + (0 if kind == "moba" else 8), scale=HD ** -0.5)

        class Attn:

            def __init__(self, tag, steps, nkt, kT, qT, pr, prT, X):
                self.tag, self.steps, self.nkt = tag, steps, nkt
                self.kT, self.qT, self.pr, self.prT, self.X = kT, qT, pr, prT, X

            def get(self, n, lo_, hi_):
                return self.steps[n] if lo_ <= n < hi_ else None

            def last_step_of_turn(self, a):
                return max(i for i, s in enumerate(self.steps) if s["a"] == a)

            def d_before(self, n):
                return sum(1 for s in self.steps[:max(n, 0)] if s["d"] is not None)

        def attn_pe(pe, A, lo_, hi_):
            T, nkt = A.tag, A.nkt
            for n in range(lo_, hi_ + 4):
                s = A.get(n, lo_, hi_)
                if s and s["turn"]:
                    src = srcs_of(s)
                    wait(pe, T + "_qk_copied", s["a"])
                    for i, k in enumerate(src["k"]):
                        pe.transpose(ps[0][:, i * P:i * P + P], k, ident[:, :])
                    for i, q in enumerate(src["q"]):
                        m = pe.transpose(ps[1][:, i * P:i * P + P], q, ident[:, :])
                    for i, q in enumerate(src.get("qpe", ())):
                        m = pe.transpose(ps[1][0:64, 256 + i * P:256 + i * P + P], q, ident[:, :])
                    m.then_inc(sem(T + "_qk_turned"), 1)
                s = A.get(n - 1, lo_, hi_)
                if s:
                    pe.wait_ge(sem(T + "_qk_copied"), s["a"] + 1)
                    wait(pe, T + "_exp_done", n - 1)
                    r, w = s["a"] % 2, nkt * P
                    rs = slice(64 * s["half"], 64 * s["half"] + 64) if s["kind"] == "diff" else slice(0, P)
                    for i in range(2):
                        extra = s["kind"] in ("mla", "fox")
                        m = pe.matmul(ps[2 + i][:, 0:w], A.qT[rs, r, i * P:i * P + P], A.kT[rs, r, 0:w],
                                      start=True, stop=not extra)
                        if s["kind"] == "mla":
                            m = pe.matmul(ps[2 + i][:, 0:w], A.qT[0:64, r, 256 + i * P:256 + i * P + P],
                                          kpeT[:, :], start=False, stop=True)
                        if s["kind"] == "fox":
                            for j in range(2):
                                m = pe.matmul(ps[2 + i][:, 0:w],
                                              nlf[:, j, s["head"]:s["head"] + 1].to_broadcast([P, P]),
                                              tri[:, j, :], start=False, stop=j == 1)
                    m.then_inc(sem(T + "_scores"), 1)
                s = A.get(n - 2, lo_, hi_)
                if s and s["d"] is not None:
                    pe.wait_ge(sem(T + "_probs"), n - 1)
                    wait(pe, T + "_pt_copied", s["d"])
                    for i in range(2):
                        for j in range(nkt):
                            m = pe.transpose(ps[4 + i][:, j * P:j * P + P],
                                             A.pr[:, (n - 2) % 2, i, j * P:j * P + P], ident[:, :])
                    m.then_inc(sem(T + "_probs_turned"), 1)
                s = A.get(n - 3, lo_, hi_)
                if s and s["d"] is not None:
                    src, d = srcs_of(s), s["d"]
                    pe.wait_ge(sem(T + "_pt_copied"), d + 1)
                    wait(pe, T + "_out_lo", d - 1)
                    o = ps[6 + d % 2]
                    if s["kind"] == "diff":
                        for i in range(2):
                            for j in range(nkt):
                                m = pe.matmul(o[:, i * P:i * P + P], A.prT[:, d % 2, j, i * P:i * P + P],
                                              src["v"][j], start=j == 0, stop=j == nkt - 1)
                    else:
                        for j in range(nkt):
                            m = pe.matmul(o[:, 0:SEQ], src["v"][j], A.prT[:, d % 2, j, :],
                                          start=j == 0, stop=j == nkt - 1)
                    m.then_inc(sem(T + "_out"), 1)
                s = A.get(n - 4, lo_, hi_)
                if s and s["d"] is not None and s["kind"] == "diff":
                    pe.wait_ge(sem("diff_normed"), s["head"] + 1)
                    for i in range(2):
                        m = pe.transpose(ps[6 + s["d"] % 2][:, 256 + i * P:256 + i * P + P],
                                         od[:, s["head"] % 2, i, :], ident[:, :])
                    m.then_inc(sem("diff_turned"), 1)

        def out_cols(s):
            return slice(256, 512) if s["kind"] == "diff" else slice(0, 256)

        def probs_free(eng, A, n):
            wait(eng, A.tag + "_probs_turned", A.d_before(n - 1))
            if n >= 1 and A.steps[n - 1]["half"] == 1:
                eng.wait_ge(sem(A.tag + "_probs"), n)

        def attn_act(act, A, lo_, hi_):
            T, nkt = A.tag, A.nkt
            for n in range(lo_, hi_ + 4):
                s = A.get(n, lo_, hi_)
                if s and s["turn"]:
                    act.wait_ge(sem(T + "_qk_turned"), s["a"] + 1)
                    if s["a"] >= 2:
                        act.wait_ge(sem(T + "_scores"), A.last_step_of_turn(s["a"] - 2) + 1)
                    r = s["a"] % 2
                    act.activation(A.kT[:, r, 0:nkt * P], ps[0][:, 0:nkt * P], ACT.Copy)
                    m = act.activation(A.qT[:, r, 0:SEQ], ps[1][:, 0:SEQ], ACT.Copy)
                    if s["kind"] == "mla":
                        m = act.activation(A.qT[0:64, r, 256:512], ps[1][0:64, 256:512], ACT.Copy)
                    m.then_inc(sem(T + "_qk_copied"), 1)
                s = A.get(n - 1, lo_, hi_)
                if s:
                    par = (n - 1) % 2
                    probs_free(act, A, n - 1)
                    act.wait_ge(sem(T + "_negmax"), n)
                    biased = s["kind"] in ("na", "moba", "fox")
                    for i in range(2):
                        src = A.pr[:, par, i, :] if biased else ps[2 + i][:, 0:nkt * P]
                        scale = srcs_of(s)["scale"]
                        m = act.activation(A.pr[:, par, i, :], src, ACT.Exp, bias=stat(NM + 2 * par + i),
                                           scale=1.0 if s["kind"] == "na" else scale,
                                           accum_out=stat(SUM + 2 * par + i))
                    m.then_inc(sem(T + "_exp_done"), 1)
                s = A.get(n - 3, lo_, hi_)
                if s and s["d"] is not None and s["kind"] == "diff":
                    act.wait_ge(sem(T + "_out"), s["d"] + 1)
                    wait(act, "diff_normed", s["head"])
                    for i in range(2):
                        m = act.activation(od[:, s["head"] % 2, i, :], ps[6 + s["d"] % 2][:, i * P:i * P + P],
                                           ACT.Square, accum_out=stat(OSS + i))
                    m.then_inc(sem("diff_squares"), 1)
                s = A.get(n - 4, lo_, hi_)
                if s and s["d"] is not None:
                    if s["kind"] == "diff":
                        act.wait_ge(sem("diff_turned"), s["head"] + 1)
                    else:
                        act.wait_ge(sem(T + "_out"), s["d"] + 1)
                    act.activation(A.X[0][:, srcs_of(s)["o"], :], ps[6 + s["d"] % 2][:, out_cols(s)],
                                   ACT.Copy).then_inc(sem(T + "_out_hi"), 1)

        def attn_dve(dve, A, lo_, hi_):
            T, nkt = A.tag, A.nkt
            w = nkt * P
            for n in range(lo_, hi_ + 4):
                s = A.get(n - 3, lo_, hi_)
                if s and s["d"] is not None:
                    d = s["d"]
                    dve.wait_ge(sem(T + "_probs_turned"), d + 1)
                    wait(dve, T + "_out", d - 1)
                    for i in range(2):
                        m = dve.tensor_copy(A.prT[:, d % 2, :, i * P:i * P + P],
                                            ps[4 + i][:, 0:w].rearrange("p (j t) -> p j t", j=nkt))
                    m.then_inc(sem(T + "_pt_copied"), 1)
                s = A.get(n - 2, lo_, hi_)
                if s:
                    par = (n - 2) % 2
                    dve.wait_ge(sem(T + "_exp_done"), n - 1)
                    dve.reciprocal(stat(RIN + 2 * par, 2), stat(SUM + 2 * par, 2))
                    dve.drain()
                    if s["half"] == 1:
                        dve.tensor_scalar(stat(RIN + 2 * par, 2), stat(RIN + 2 * par, 2), stat(LAM), None, ALU.mult)
                        dve.drain()
                    for i in range(2):
                        p = A.pr[:, par, i, :]
                        if s["half"] == 1:
                            m = dve.scalar_tensor_tensor(p, p, stat(RIN + 2 * par + i), A.pr[:, 1 - par, i, :],
                                                         ALU.mult, ALU.add)
                        else:
                            m = dve.tensor_scalar(p, p, stat(RIN + 2 * par + i), None, ALU.mult)
                    m.then_inc(sem(T + "_probs"), 1)
                s = A.get(n - 1, lo_, hi_)
                if s:
                    par = (n - 1) % 2
                    src = srcs_of(s)
                    dve.wait_ge(sem(T + "_scores"), n)
                    if s["kind"] in ("na", "moba", "fox"):
                        probs_free(dve, A, n - 1)
                        if s["kind"] == "na" and s["head"] == 0:
                            dve.wait_ge(sem("na_bias_loaded"), 16)
                        for i in range(2):
                            p = A.pr[:, par, i, :]
                            if s["kind"] == "na":
                                dve.scalar_tensor_tensor(p[:, 0:256], ps[2 + i][:, 0:256], src["scale"],
                                                         nabias[:, s["head"], i, :], ALU.mult, ALU.add)
                                dve.tensor_scalar(p[:, 256:512], ps[2 + i][:, 256:512], src["scale"], None, ALU.mult)
                            elif s["kind"] == "moba":
                                slope = 2.0 ** -(s["head"] + 1)
                                dve.scalar_tensor_tensor(p, distm[:, i, :], -slope / src["scale"],
                                                         ps[2 + i][:, 0:w], ALU.mult, ALU.add)
                            else:
                                dve.scalar_tensor_tensor(p, causal[:, i, :], 1.0, ps[2 + i][:, 0:w],
                                                         ALU.mult, ALU.add)
                        dve.drain()
                    for i in range(2):
                        x = A.pr[:, par, i, :] if s["kind"] in ("na", "moba", "fox") else ps[2 + i][:, 0:w]
                        dve.tensor_reduce(stat(MX + 2 * par + i), x, AX.X, ALU.max)
                    dve.drain()
                    dve.tensor_scalar(stat(NM + 2 * par, 2), stat(MX + 2 * par, 2),
                                      -1.0 if s["kind"] == "na" else -src["scale"], None,
                                      ALU.mult).then_inc(sem(T + "_negmax"), 1)
                s = A.get(n - 4, lo_, hi_)
                if s and s["d"] is not None:
                    if s["kind"] == "diff":
                        dve.wait_ge(sem("diff_rstd"), s["head"] + 1)
                        for i in range(2):
                            m = dve.scalar_tensor_tensor(od[:, s["head"] % 2, i, :],
                                                         ps[6 + s["d"] % 2][:, i * P:i * P + P], stat(ORS + i),
                                                         g_sub[:, :], ALU.mult, ALU.mult)
                        m.then_inc(sem("diff_normed"), 1)
                    dve.wait_ge(sem(T + "_out_hi"), s["d"] + 1)
                    o = srcs_of(s)["o"]
                    dve.tensor_tensor(A.X[1][:, o, :], ps[6 + s["d"] % 2][:, out_cols(s)],
                                      A.X[0][:, o, :].bitcast(F32), ALU.subtract).then_inc(sem(T + "_out_lo"), 1)

        A1 = Attn("att", STEPS, 4, kT, qT, probs, probsT, XA)
        A2 = Attn("att2", STEPS2, 2, kT2, qT2, probs2, probsT2, XB)

        def ffn_base(U, i, gated):
            per = 3 if gated else 2
            return U // 4 + (per - 1) + (i - 1) * per

        def ffn_pe(pe, T, U, n, gated):
            def body(i, head=True, tail=True):
                g0 = U // 4 if isinstance(i, int) and i == 0 else ffn_base(U, i, gated)
                k = 0
                first = isinstance(i, int) and i == 0
                if head and gated:
                    if not first:
                        wait(pe, T + "_gated", i)
                        for q in range(4):
                            unit(pe, g0, q, ps[0:2], XA, 4 * q, q == 0, q == 3)
                    k = 1
                for q in range(4):
                    if head and (gated or not first):
                        if q == 0:
                            wait(pe, T + "_act", i)
                        unit(pe, g0 + k, q, ps[2:4], XA, 4 * q, q == 0, q == 3)
                    if q == 1 and tail:
                        pe.wait_ge(sem(T + "_act"), i)
                        wait(pe, T + "_y", 4 * i - 4)
                        for tk in range(2):
                            for j in range(4):
                                m = pe.transpose(ps[4 + tk][:, j * P:j * P + P],
                                                 act_a[:, tk, j * P:j * P + P], ident[:, :])
                        m.then_inc(sem(T + "_turned"), 1)
                k += head
                if tail:
                    pe.wait_ge(sem(T + "_xlo"), i)
                    for q in range(4):
                        wait(pe, T + "_y", 4 * i - 4 + q - 1)
                        b = 6 if q % 2 == 0 else 4
                        unit(pe, g0 + k, q, ps[b:b + 2], XF, 0, True, True)

            body(0, tail=False)
            body(1)
            with pe.Fori(2, n) as i:
                body(i)
            body_tail(pe, n, body, U, gated)

        def body_tail(eng, n, body, U, gated):
            body(n, head=False)

        def ffn_act(act, T, U, n, gated):
            def body(i, head=True, tail=True):
                g0 = U // 4 if isinstance(i, int) and i == 0 else ffn_base(U, i, gated)
                k = 0
                first = isinstance(i, int) and i == 0
                if head and gated:
                    if not first:
                        for q in range(4):
                            hi(act, g0, q)
                    k = 1
                up = head and (gated or not first)
                if up:
                    hi(act, g0 + k, 0)
                    hi(act, g0 + k, 1)
                if head and gated:
                    used(act, 4 * g0 + 4)
                    wait(act, T + "_act", i)
                    for tk in range(2):
                        m = act.activation(act_g[:, tk, :], ps[tk][:, :], ACT.Silu)
                    m.then_inc(sem(T + "_gated"), 1)
                if up:
                    hi(act, g0 + k, 2)
                if tail:
                    act.wait_ge(sem(T + "_turned"), i)
                    for tk in range(2):
                        m = act.activation(XF[0][:, :, tk * P:tk * P + P],
                                           ps[4 + tk][:, :].rearrange("p (j t) -> p j t", j=4), ACT.Copy)
                    m.then_inc(sem(T + "_xhi"), 1)
                if up:
                    hi(act, g0 + k, 3)
                k += head
                if tail:
                    hi(act, g0 + k, 0)
                    hi(act, g0 + k, 1)
                if head and not gated:
                    used(act, 4 * (g0 + k))
                    wait(act, T + "_act", i)
                    for tk in range(2):
                        m = act.activation(act_g[:, tk, :], ps[2 + tk][:, :], ACT.Relu)
                    m.then_inc(sem(T + "_gated"), 1)
                if tail:
                    hi(act, g0 + k, 2)
                    hi(act, g0 + k, 3)

            body(0, tail=False)
            body(1)
            with act.Fori(2, n) as i:
                body(i)
            body(n, head=False)

        def ffn_dve(dve, T, U, n, gated, finish, U_next):
            def add_y(i, q, g):
                used(dve, 4 * g + q + 1)
                b = 6 if q % 2 == 0 else 4
                for tk in range(2):
                    y = ybuf[:, tk, q * NCH:(q + 1) * NCH]
                    if isinstance(i, int) and i == 1:
                        m = dve.tensor_copy(y, ps[b + tk][:, :])
                    else:
                        m = dve.tensor_tensor(y, y, ps[b + tk][:, :], ALU.add)
                m.then_inc(sem(T + "_y"), 1)
                if isinstance(i, int) and i == n:
                    dve.drain()
                    finish(q)

            def body(i, head=True, tail=True, pending=True):
                g0 = U // 4 if isinstance(i, int) and i == 0 else ffn_base(U, i, gated)
                k = 0
                first = isinstance(i, int) and i == 0
                if head and gated:
                    if not first:
                        lo(dve, g0, 0)
                        lo(dve, g0, 1)
                        if pending:
                            add_y(i - 1, 3, g0 - 1)
                        lo(dve, g0, 2)
                        lo(dve, g0, 3)
                    k = 1
                up = head and (gated or not first)
                if up:
                    lo(dve, g0 + k, 0)
                    lo(dve, g0 + k, 1)
                if pending and not (head and gated):
                    add_y(i - 1, 3, g0 - 1)
                if up:
                    lo(dve, g0 + k, 2)
                if tail:
                    dve.wait_ge(sem(T + "_xhi"), i)
                    for tk in range(2):
                        m = dve.tensor_tensor(XF[1][:, :, tk * P:tk * P + P],
                                              ps[4 + tk][:, :].rearrange("p (j t) -> p j t", j=4),
                                              XF[0][:, :, tk * P:tk * P + P].bitcast(F32), ALU.subtract)
                    m.then_inc(sem(T + "_xlo"), 1)
                if up:
                    lo(dve, g0 + k, 3)
                k += head
                if tail:
                    lo(dve, g0 + k, 0)
                    lo(dve, g0 + k, 1)
                    add_y(i, 0, g0 + k)
                if head:
                    dve.wait_ge(sem(T + "_gated"), i + 1)
                    if gated:
                        used(dve, 4 * (g0 + k))
                    if tail:
                        dve.wait_ge(sem(T + "_turned"), i)
                    for tk in range(2):
                        m = dve.tensor_tensor(act_a[:, tk, :], act_g[:, tk, :],
                                              ps[2 + tk][:, :] if gated else act_g[:, tk, :], ALU.mult)
                    m.then_inc(sem(T + "_act"), 1)
                if tail:
                    for q in (2, 3):
                        lo(dve, g0 + k, q)
                        add_y(i, q - 1, g0 + k)

            body(0, tail=False, pending=False)
            body(1, pending=False)
            body(2)
            with dve.Fori(3, n) as i:
                body(i)
            body(n, head=False)
            if U_next is not None:
                lo(dve, U_next // 4, 0)
            add_y(n, 3, ffn_base(U, n, gated))
            if U_next is not None:
                lo(dve, U_next // 4, 1)

        def ffn_sp(sp, U, n, gated, gate_v, up_v, down_flat):
            def body(i, head=True, tail=True):
                g0 = U // 4 if isinstance(i, int) and i == 0 else ffn_base(U, i, gated)
                k = 0
                for v in ([gate_v, up_v] if gated else [up_v]) if head else []:
                    for q in range(4):
                        load(sp, g0 + k, q, at_col(v[:, q], i * NCH))
                    k += 1
                if tail:
                    for q in range(4):
                        v = down_flat[:, :, q * NCH:(q + 1) * NCH]
                        if isinstance(i, int):
                            load(sp, g0 + k, q, v[:, (i - 1) * KQ:i * KQ, :])
                        else:
                            load(sp, g0 + k, q, (v, i * KQ - KQ, "k"))

            body(0, tail=False)
            body(1)
            with sp.Fori(2, n) as i:
                body(i)
            body(n, head=False)

        wd_k = t["ffn_wd"][0].rearrange("(k p) n -> p k n", p=P)
        w_down_k = t["w_down_2"].rearrange("(k p) n -> p k n", p=P)

        def out_sp(sp, U, v):
            for c in range(4):
                for q in range(4):
                    load(sp, U // 4 + c, q, v[:, q, :, c * NCH:(c + 1) * NCH])

        def out_pe(pe, T, U, first):
            for c in range(first, 4):
                wait(pe, T, c - 1)
                for q in range(4):
                    unit(pe, U // 4 + c, q, ps[2 * (c % 2):2 * (c % 2) + 2], XA, 4 * q, q == 0, q == 3)

        def out_act(act, U, T, U_next, first):
            for c in range(first, 4):
                for q in range(4):
                    hi(act, U // 4 + c, q)
                if c:
                    squares_of(act, T, c - 1, T + "_chunk", xres, SQ1)
            hi(act, U_next // 4, 0)
            hi(act, U_next // 4, 1)
            squares_of(act, T, 3, T + "_chunk", xres, SQ1)

        def out_dve(dve, T, U, gate, U_next, first):
            def add(c):
                used(dve, U + 4 * c + 4)
                cc = slice(c * NCH, (c + 1) * NCH)
                src = [ps[2 * (c % 2) + tk][:, :] for tk in range(2)]
                if gate is not None:
                    for tk in range(2):
                        dve.tensor_tensor(tmp[:, tk, :], src[tk], gate[:, cc], ALU.mult)
                    dve.drain()
                    src = [tmp[:, tk, :] for tk in range(2)]
                for tk in range(2):
                    m = dve.tensor_tensor(xres[:, tk, cc], xres[:, tk, cc], src[tk], ALU.add)
                m.then_inc(sem(T + "_chunk"), 1)
                dve.drain()
                if gate is not None:
                    for tk in range(2):
                        dve.tensor_tensor(ybuf[:, tk, cc], xres[:, tk, cc], sc_f[:, cc], ALU.mult)
            for c in range(first, 4):
                lo(dve, U // 4 + c, 0)
                lo(dve, U // 4 + c, 1)
                if c == 1:
                    dve.wait_ge(sem(T + "_chunk_loaded"), 16 * (6 if gate is not None else 1))
                    if gate is not None:
                        dve.scalar_tensor_tensor(sc_f[:, :], sc_f[:, :], 1.0, gvec[:, :], ALU.add, ALU.mult)
                        dve.drain()
                if c:
                    add(c - 1)
                lo(dve, U // 4 + c, 2)
                lo(dve, U // 4 + c, 3)
            lo(dve, U_next // 4, 0)
            add(3)
            lo(dve, U_next // 4, 1)
            sum_squares(dve, T, 4, [(SQ1, SS)])

        def rstd_pool(pool, T, tiles, done):
            pool.wait_ge(sem(T + done), 1)
            pool_rstd(pool, stat(RSTD, tiles), stat(SS, tiles), tiles, D).then_inc(sem(T + "_rstd"), 1)

        block = ctx.enter_context(nc.Block())

        @block.sync
        def _(sp):
            sp.dma_start(crow[0:16, :], t["c"].rearrange("a (k p) -> (a k) p", p=P)).then_inc(sem("c_loaded"), 16)
            sp.dma_start(crow[16:32, :], t["c_ctx"].rearrange("(k p) -> k p", p=P)).then_inc(sem("c_loaded"), 16)
            sp.dma_start(ident[:, :], t["identity"]).then_inc(sem("ident_loaded"), 16)
            sp.dma_start(esel[:, :], t["row_select"]).then_inc(sem("ident_loaded"), 16)
            sp.dma_start(spread[:, :, :], t["row_spread"]).then_inc(sem("ident_loaded"), 16)

            for i in range(4):
                sp.dma_start(xin[:, i, :], (x_v, ctx_v)[i // 2][:, i % 2, :]).then_inc(sem(f"x_loaded{i}"), 16)

            def ada_cols(c):
                col = (c * NCH + D) % (2 * D) if c < N_ADA_1 else c * NCH
                return slice(col, col + NCH)

            def b_piece(c):
                wait(sp, "ada_combined", c - 1)
                sp.dma_start(rows_of(c, c % 2)[4:5, :], t["b_ada"][:, ada_cols(c)]).then_inc(sem(f"b_loaded{c % 2}"), 16)

            for c in range(N_ADA_1):
                for q in range(4):
                    load(sp, c, q, w_ada_v[:, q, :, ada_cols(c)])
                b_piece(c)

            def store(c):
                sp.wait_ge(sem("mod_row"), c + 1)
                sp.dma_start(mod_d[:, c * NCH - 2 * D:(c + 1) * NCH - 2 * D], late_row(c % 2))\
                    .then_inc(sem(f"late_mod_stored{c % 2}"), 16)
            for n, (kind, c, k) in enumerate(MIX):
                u = U_MIX + n
                if kind == "ada":
                    load(sp, u // 4, u % 4, w_ada_v[:, k, :, ada_cols(c)])
                    if k == 3:
                        if c == N_ADA_1:
                            sp.wait_ge(sem("x_squares"), 1)
                        b_piece(c)
                else:
                    col, w, _ = WIN[c]
                    load(sp, u // 4, u % 4, w_in_v[:, k, :, col:col + w], w=w)
                for c in range(N_ADA_1, N_ADA):
                    if n == LAST["ada", c] + 5:
                        store(c)
            load(sp, U_MLA // 4, 0, wuq_v[:, :, 0:512])
            load(sp, U_MLA // 4, 1, wuq_v[:, :, 512:768], w=256)
            load(sp, U_MLA // 4, 2, wukv_v[:, :, 0:512], k=2)
            load(sp, U_MLA // 4, 3, wukv_v[:, :, 512:1024], k=2)
            out_sp(sp, U_OUT, w_out_v)
            ffn_sp(sp, U_FFN, N_FF, True, wg_v, wu_v, wd_k)

            def qkv2(i):
                for b in range(2):
                    for q in range(4):
                        load(sp, U_WIN2 // 4 + 2 * i + b, q, at_col(w_in2_v[:, q], i * (2 * NCH) + b * NCH))
            with sp.Fori(0, N_QKV2 // 2) as i:
                qkv2(i)

            def merge(n):
                for b, first in enumerate((6152, 8200)):
                    for q in range(4):
                        load(sp, U_MRG // 4 + 3 * n + b, q, at_col(w_in2_v[:, q], n * NCH + first))
                for q in range(4):
                    v = wpa_v if q < 2 else wpb_v
                    load(sp, U_MRG // 4 + 3 * n + 2, q, at_col(v[:, q % 2], n * NCH))
            for n in range(4):
                merge(n)
            out_sp(sp, U_OUT2, w_out2_v)
            ffn_sp(sp, U_FFN2, N_FF2, False, None, w_up_v, w_down_k)
            for q in range(4):
                sp.wait_ge(sem("out_ready"), 2 * q + 2)
                cc = slice(q * NCH, (q + 1) * NCH)
                sp.dma_start(out_v[:, :, cc], ybuf[:, :, cc]).then_inc(sem("stored"), 16)
            sp.wait_ge(sem("stored"), 64)

        @block.scalar
        def _(act):
            act.wait_ge(sem("c_loaded"), 32)
            act.activation(csig[:, :], crow[:, :], ACT.Silu).then_inc(sem("c_silu"), 1)
            act.wait_ge(sem("c_turned"), 1)
            for v in range(2):
                m = act.activation(cst[:, :, 2 * v], ccol[:, 16 * v:16 * v + 16], ACT.Copy)
            m.then_inc(sem("c_hi"), 1)

            for i in range(4):
                act.wait_ge(sem(f"x_loaded{i}"), 16)
                act.drain()
                m = act.activation(junk[:, :], xin[:, i, :], ACT.Square, accum_out=stat(SS + i))
            m.then_inc(sem("x_squares"), 1)

            def copy_rows(c, b, units, bank):
                used(act, units)
                wait(act, "ada_combined", c - 1)
                act.activation(rows_of(c, b)[0:4, :], ps[bank][0:4, :], ACT.Copy).then_inc(sem("ada_rows"), 1)

            for c in range(N_ADA_1):
                hi(act, c, 0)
                hi(act, c, 1)
                if c:
                    copy_rows(c - 1, (c - 1) % 2, 4 * c, 2 + (c - 1) % 2)
                hi(act, c, 2)
                hi(act, c, 3)
                if c == 0:
                    act.wait_ge(sem("na_rpb_loaded"), 128)
                    act.wait_ge(sem("na_band_loaded"), 16)
                    act.activation(bandr[:, :], band[:, :], ACT.Copy)
                    act.activation(narpbr[:, :], narpb[:, :], ACT.Copy).then_inc(sem("na_rpb_hi"), 1)
                    act.wait_ge(sem("x_rstd"), 1)
                    for i in range(4):
                        m = act.activation(xin[:, i, :], xin[:, i, :], ACT.Copy, scale=stat(RSTD + i))
                    m.then_inc(sem("x_scaled"), 1)
                if c >= 5:
                    turn_h_act(act, c - 5)

            def win_copy(c):
                col, w, cx = WIN[c]
                used(act, U_MIX + LAST["win", c] + 1)
                b = 4 * (c % 2)
                if c == len(WIN) - 1:
                    act.wait_ge(sem("ada_combined"), N_ADA)
                    for i in range(2):
                        act.wait_ge(sem(f"late_mod_stored{i}"), 8 * (N_ADA - N_ADA_1))
                m = act.activation(PL[:, 0, col:col + w], ps[b][:, 0:w], ACT.Copy)
                if cx is not None:
                    m = act.activation(PC[:, 0, cx:cx + w], ps[b + 2][:, 0:w], ACT.Copy)
                m.then_inc(sem("win_copied_a"), 1)
                if c in WIN_SQ:
                    first, width, n, tiles = WIN_SQ[c]
                    act.wait_ge(sem("win_copied_d"), c + 1)
                    for i in range(tiles):
                        for h in range(n):
                            act.drain()
                            src = PL[:, i, col + h * width:col + (h + 1) * width] if i < 2 else \
                                PC[:, i - 2, cx + h * width:cx + (h + 1) * width]
                            m = act.activation(psq[:, 0:width], src, ACT.Square, accum_out=stat(first + n * i + h))
                    m.then_inc(sem("win_squared"), 1)
            for n, (kind, c, _) in enumerate(MIX):
                u = U_MIX + n
                hi(act, u // 4, u % 4, w=NCH if kind == "ada" else WIN[c][1])
                if n == 1:
                    copy_rows(N_ADA_1 - 1, 1, U_MIX, 3)
                if n == 3:
                    turn_h_act(act, 3)
                if n >= 2 and MIX[n - 2][2] == 3:
                    kind, c, _ = MIX[n - 2]
                    if kind == "ada":
                        copy_rows(c, c % 2, u - 1, ada_banks(c)[0])
                    else:
                        win_copy(c)
            hi(act, U_MLA // 4, 0)
            win_copy(len(WIN) - 1)
            hi(act, U_MLA // 4, 1, w=256)

            act.wait_ge(sem("mla_turned"), 1)
            for i in range(2):
                act.activation(XQ[0][:, :, i * P:i * P + P], ps[i][:, :].rearrange("p (j t) -> p j t", j=4), ACT.Copy)
            for i in range(4):
                m = act.activation(XKV[0][:, :, i * P:i * P + P],
                                   ps[2 + i // 2][:, (i % 2) * 256:(i % 2) * 256 + 256].rearrange("p (j t) -> p j t", j=2),
                                   ACT.Copy)
            m.then_inc(sem("mla_hi"), 1)
            act.activation(kpeT[:, :], ps[4][0:64, :], ACT.Copy).then_inc(sem("kpe_copied"), 1)
            hi(act, U_MLA // 4, 2, k=2)
            hi(act, U_MLA // 4, 3, k=2)
            used(act, U_MLA + 1)
            act.activation(PL[:, 0, ML_Q:ML_Q + 512], ps[0][:, :], ACT.Copy)
            used(act, U_MLA + 2)
            act.activation(PL[:, 0, ML_Q + 512:ML_Q + 768], ps[2][:, 0:256], ACT.Copy).then_inc(sem("mla_copied_a"), 1)
            used(act, U_MLA + 3)
            for i in (0, 1):
                m = act.activation(mkv[:, i, 0:512], ps[4 + i][:, :], ACT.Copy)
            used(act, U_MLA + 4)
            for i in (0, 1):
                m = act.activation(mkv[:, i, 512:1024], ps[i][:, :], ACT.Copy)
            m.then_inc(sem("mla_copied_a"), 1)
            act.wait_ge(sem("lam_dots"), 1)
            act.activation(stat(LAMW, 2), stat(LAMW, 2), ACT.Exp).then_inc(sem("lam_exp"), 1)

            act.wait_ge(sem("rotated_pe"), 1)
            attn_act(act, A1, 0, len(STEPS))
            out_act(act, U_OUT, "x1", U_FFN, 0)

            start_act(act, "h2", U_FFN, 0)
            ffn_act(act, "ff1", U_FFN, N_FF, True)

            def squares_2(c):
                squares_of(act, "xf", c, "xf_chunk", xres, SQ1)
                squares_of(act, "xf", c, "xg_chunk", ybuf, SQ2)
            squares_2(0)
            hi(act, U_WIN2 // 4, 0)
            squares_2(1)
            hi(act, U_WIN2 // 4, 1)
            squares_2(2)
            squares_2(3)
            start_act(act, "h3", U_WIN2, 0)
            act.wait_ge(sem("wf_loaded"), 32)
            act.activation(wfh[:, :, :], wf[:, :, :], ACT.Copy).then_inc(sem("wf_hi"), 1)

            def qkv2(i, first=False):
                for b in range(2):
                    g = U_WIN2 // 4 + 2 * i + b
                    if first and b == 0:
                        continue
                    hi(act, g, 0)
                    hi(act, g, 1)
                    qkv2_copy(i * 2 + (b - 1), 1 - b)
                    hi(act, g, 2)
                    hi(act, g, 3)

            def qkv2_copy(c, b):
                used(act, c * 4 + (U_WIN2 + 4))
                act.activation(P2[:, 0, bass.ds(c * NCH, NCH)], ps[2 * b][:, :], ACT.Copy).then_inc(sem("qkv2_a"), 1)
            qkv2(0, True)
            with act.Fori(1, N_QKV2 // 2) as i:
                qkv2(i)
            qkv2_copy(N_QKV2 - 1, 1)
            act.wait_ge(sem("fz_abs"), 1)
            act.activation(fz[:, 2], fz[:, 1], ACT.Exp, scale=-1.0).then_inc(sem("fz_exp"), 1)
            act.wait_ge(sem("fz_one"), 1)
            act.activation(fz[:, 4], fz[:, 3], ACT.Ln).then_inc(sem("fz_log"), 1)
            act.wait_ge(sem("x2_stored"), 16)
            attn_act(act, A2, 0, len(STEPS2))

            def sigm(n, b):
                used(act, n * 12 + (U_MRG + 4 * b + 4))
                wait(act, "merged_chunk", n)
                for tk in range(2):
                    m = act.activation(sig[:, 2 * b + tk, :], ps[2 * b + tk][:, :], ACT.Sigmoid)
                m.then_inc(sem("gate_sigmoid"), 1)

            def merge(n):
                g = 3 * n + U_MRG // 4
                for q in range(4):
                    hi(act, g, q)
                hi(act, g + 1, 0)
                hi(act, g + 1, 1)
                sigm(n, 0)
                hi(act, g + 1, 2)
                hi(act, g + 1, 3)
                hi(act, g + 2, 0)
                hi(act, g + 2, 1)
                sigm(n, 1)
                hi(act, g + 2, 2)
                hi(act, g + 2, 3)
            merge(0)
            with act.Fori(1, 4) as n:
                merge(n)
            hi(act, U_OUT2 // 4, 0)
            hi(act, U_OUT2 // 4, 1)
            start_act(act, "mrg", U_OUT2, 0)
            out_act(act, U_OUT2, "x3", U_FFN2, 1)
            start_act(act, "h4", U_FFN2, 2)
            ffn_act(act, "ff2", U_FFN2, N_FF2, False)
            for c in range(4):
                squares_of(act, "x4", c, "x4_chunk", xres, SQ1)

        @block.vector
        def _(dve):
            dve.memset(pstat[:, 16:24], -0.5).then_inc(sem("halves"), 1)
            dve.memset(narpb[:, :], 0.0).then_inc(sem("na_rpb_zero"), 1)
            dve.wait_ge(sem("c_cols"), 1)
            dve.tensor_copy(ccol[:, :], ps[7][:, 0:32]).then_inc(sem("c_turned"), 1)
            dve.wait_ge(sem("c_hi"), 1)
            for v in range(2):
                m = dve.tensor_tensor(cst[:, :, 2 * v + 1], ccol[:, 16 * v:16 * v + 16],
                                      cst[:, :, 2 * v].bitcast(F32), ALU.subtract)
            m.then_inc(sem("c_lo"), 1)

            def make_na_bias():
                dve.wait_ge(sem("na_mask_loaded"), 16)
                dve.wait_ge(sem("na_bands"), 1)
                for i in range(2):
                    for half in range(2):
                        pp = slice(64 * half, 64 * half + 64)
                        d0 = 3 - (2 * i + half)
                        for jb in range(4):
                            bands = ps[4 + jb][pp, 0:448].rearrange("p (j h d) -> p h d j", h=4, d=7)[:, :, d0:d0 + 4, :]
                            mask = namask[pp, jb * 16:jb * 16 + 16].rearrange("p (a b j) -> p a b j", a=1, b=1)
                            m = dve.tensor_tensor(
                                nab_1[pp, :, i, :].rearrange("p h (k j) -> p h k j", k=4)[:, :, :, jb * 16:jb * 16 + 16],
                                bands, mask.to_broadcast([64, 4, 4, 16]), ALU.add)
                m.then_inc(sem("na_bias_made"), 1)

            def take(c):
                q = c % 4
                cc = slice(q * NCH, (q + 1) * NCH)
                dve.wait_ge(sem("ada_combined"), c + 1)
                if c == 0:
                    dve.wait_ge(sem("g_attn_loaded"), 16)
                if c == 4:
                    dve.wait_ge(sem("x_modulated"), 4)
                if c < 4:
                    wait(dve, "x_modulated", c)
                    for v in range(2):
                        m = dve.scalar_tensor_tensor(scale_g[:, v, :], ps[v][:, :], 1.0, gvec[:, cc], ALU.add, ALU.mult)
                    m.then_inc(sem("mod_row"), 1)
                else:
                    for i in range(4):
                        dve.tensor_tensor(xin[:, i, cc], xin[:, i, cc], ps[i // 2][:, :], ALU.add)\
                            .then_inc(sem("h_ready"), 1)
                    dve.drain().then_inc(sem("mod_row"), 1)

            def move_row(c, b, bank):
                dve.wait_ge(sem("ada_combined"), c + 1)
                wait(dve, f"late_mod_stored{b}", 16 * ((c - N_ADA_1) // 2))
                dve.tensor_copy(late_row(b), ps[bank][0:1, :]).then_inc(sem("mod_row"), 1)

            for c in range(N_ADA_1):
                lo(dve, c, 0)
                lo(dve, c, 1)
                lo(dve, c, 2)
                if c:
                    take(c - 1)
                lo(dve, c, 3)
                if c == 0:
                    dve.wait_ge(sem("na_rpb_hi"), 1)
                    dve.tensor_tensor(narpbr[32:63, :], narpb[32:63, :], narpbr[32:63, :].bitcast(F32),
                                      ALU.subtract).then_inc(sem("na_rpb_lo"), 1)
                if c == 1:
                    make_na_bias()
                if c >= 5:
                    turn_h_dve(dve, c - 5)

            def win_copy(c):
                col, w, cx = WIN[c]
                used(dve, U_MIX + LAST["win", c] + 1)
                b = 4 * (c % 2)
                if c == len(WIN) - 1:
                    dve.wait_ge(sem("ada_combined"), N_ADA)
                    for i in range(2):
                        dve.wait_ge(sem(f"late_mod_stored{i}"), 8 * (N_ADA - N_ADA_1))
                m = dve.tensor_copy(PL[:, 1, col:col + w], ps[b + 1][:, 0:w])
                if cx is not None:
                    m = dve.tensor_copy(PC[:, 1, cx:cx + w], ps[b + 3][:, 0:w])
                m.then_inc(sem("win_copied_d"), 1)
            for n, (kind, c, _) in enumerate(MIX):
                u = U_MIX + n
                lo(dve, u // 4, u % 4, w=NCH if kind == "ada" else WIN[c][1])
                if n == 2:
                    take(N_ADA_1 - 1)
                    turn_h_dve(dve, 3)
                if n >= 2 and MIX[n - 2][2] == 3:
                    kind, c, _ = MIX[n - 2]
                    if kind == "ada":
                        move_row(c, c % 2, ada_banks(c)[1])
                    else:
                        win_copy(c)
            lo(dve, U_MLA // 4, 0)
            win_copy(len(WIN) - 1)
            lo(dve, U_MLA // 4, 1, w=256)
            dve.wait_ge(sem("mla_hi"), 1)
            for i in range(2):
                dve.tensor_tensor(XQ[1][:, :, i * P:i * P + P], ps[i][:, :].rearrange("p (j t) -> p j t", j=4),
                                  XQ[0][:, :, i * P:i * P + P].bitcast(F32), ALU.subtract)
            for i in range(4):
                m = dve.tensor_tensor(XKV[1][:, :, i * P:i * P + P],
                                      ps[2 + i // 2][:, (i % 2) * 256:(i % 2) * 256 + 256].rearrange("p (j t) -> p j t", j=2),
                                      XKV[0][:, :, i * P:i * P + P].bitcast(F32), ALU.subtract)
            m.then_inc(sem("mla_lo"), 1)
            lo(dve, U_MLA // 4, 2, k=2)
            lo(dve, U_MLA // 4, 3, k=2)
            used(dve, U_MLA + 1)
            dve.tensor_copy(PL[:, 1, ML_Q:ML_Q + 512], ps[1][:, :])
            used(dve, U_MLA + 2)
            dve.tensor_copy(PL[:, 1, ML_Q + 512:ML_Q + 768], ps[3][:, 0:256]).then_inc(sem("mla_copied_d"), 1)
            used(dve, U_MLA + 3)
            for i in (2, 3):
                m = dve.tensor_copy(mkv[:, i, 0:512], ps[4 + i][:, :])
            used(dve, U_MLA + 4)
            for i in (2, 3):
                m = dve.tensor_copy(mkv[:, i, 512:1024], ps[i][:, :])
            m.then_inc(sem("mla_copied_d"), 1)

            dve.wait_ge(sem("small_loaded"), 16 * 13)
            for v in range(2):
                dve.tensor_tensor(lamv[:, 2 * v, :], lamv[:, 2 * v, :], lamv[:, 2 * v + 1, :], ALU.mult)
                dve.drain()
                dve.tensor_reduce(stat(LAMW + v), lamv[:, 2 * v, :], AX.X, ALU.add)
            dve.drain().then_inc(sem("lam_dots"), 1)
            dve.wait_ge(sem("lam_exp"), 1)
            dve.tensor_tensor(stat(LAM), stat(LAMW + 1), stat(LAMW), ALU.subtract)
            dve.drain()
            dve.tensor_scalar(stat(LAM), stat(LAM), -LAM0, None, ALU.add)
            dve.tensor_scalar(g_sub[:, :], g_sub[:, :], 1.0 - LAM0, None, ALU.mult).then_inc(sem("lam_used"), 1)
            dve.drain()

            attn_dve(dve, A1, 0, len(STEPS))
            out_dve(dve, "x1", U_OUT, gt_a, U_FFN, 0)

            def scaled(T, out, x, g, shift=False):
                def make(q):
                    cc = slice(q * NCH, (q + 1) * NCH)
                    for i in range(2):
                        dve.scalar_tensor_tensor(out[:, i, cc], x[:, i, cc], stat(RSTD + i), g[:, cc], ALU.mult,
                                                 ALU.add if shift else ALU.mult).then_inc(sem(T + "_ready"), 1)
                return make

            dve.wait_ge(sem("x1_rstd"), 1)
            start_dve(dve, "h2", U_FFN, 0, scaled("h2", ybuf, ybuf, sh_f, True))

            def finish_1(q):
                cc = slice(q * NCH, (q + 1) * NCH)
                for i in range(2):
                    dve.tensor_tensor(ybuf[:, i, cc], ybuf[:, i, cc], gt_f[:, cc], ALU.mult)
                dve.drain()
                for i in range(2):
                    m = dve.tensor_tensor(xres[:, i, cc], xres[:, i, cc], ybuf[:, i, cc], ALU.add)
                m.then_inc(sem("xf_chunk"), 1)
            ffn_dve(dve, "ff1", U_FFN, N_FF, True, finish_1, U_WIN2)
            sum_squares(dve, "xf", 8, [(SQ1, SS), (SQ2, SS + 2)])
            dve.wait_ge(sem("g_mix_loaded"), 16)
            dve.wait_ge(sem("xf_rstd"), 1)
            start_dve(dve, "h3", U_WIN2, 0, scaled("h3", h3, ybuf, gvec))
            dve.wait_ge(sem("wf_hi"), 1)
            dve.tensor_tensor(wfl[:, :, :], wf[:, :, :], wfh[:, :, :].bitcast(F32), ALU.subtract).then_inc(sem("wf_lo"), 1)
            def qkv2_copy(c, b):
                used(dve, c * 4 + (U_WIN2 + 4))
                dve.tensor_copy(P2[:, 1, bass.ds(c * NCH, NCH)], ps[2 * b + 1][:, :]).then_inc(sem("qkv2_d"), 1)

            def qkv2(i, first=False):
                for b in range(2):
                    g = U_WIN2 // 4 + 2 * i + b
                    if first and b == 0:
                        continue
                    lo(dve, g, 0)
                    lo(dve, g, 1)
                    if first:
                        dve.wait_ge(sem("f_acc"), 1)
                        dve.tensor_copy(zT[:, :], ps[4][0:8, 0:SEQ]).then_inc(sem("z_copied"), 1)
                    qkv2_copy(i * 2 + (b - 1), 1 - b)
                    lo(dve, g, 2)
                    lo(dve, g, 3)
            dve.wait_ge(sem("x2_made"), 1)
            qkv2(0, True)
            dve.wait_ge(sem("z_turned"), 1)
            dve.tensor_tensor(fz[:, 0], ps[5][:, 0:16].rearrange("p (i h) -> p i h", i=2),
                              bf[:, :].rearrange("p (i h) -> p i h", i=1).to_broadcast([P, 2, 8]), ALU.add)
            dve.drain()
            dve.scalar_tensor_tensor(fz[:, 1], fz[:, 0], -1.0, fz[:, 0], ALU.mult, ALU.max)
            dve.tensor_scalar(fz[:, 5], fz[:, 0], 0.0, None, ALU.min)
            dve.drain().then_inc(sem("fz_abs"), 1)
            with dve.Fori(1, N_QKV2 // 2) as i:
                qkv2(i)
            qkv2_copy(N_QKV2 - 1, 1)
            dve.wait_ge(sem("fz_exp"), 1)
            dve.tensor_scalar(fz[:, 3], fz[:, 2], 1.0, None, ALU.add).then_inc(sem("fz_one"), 1)
            dve.wait_ge(sem("fz_log"), 1)
            dve.tensor_tensor(fz[:, 4], fz[:, 4], fz[:, 5], ALU.subtract)
            dve.drain()
            dve.tensor_scalar(nlf[:, :, :], fz[:, 4], float(HD) ** 0.5, None, ALU.mult).then_inc(sem("nlf_made"), 1)
            dve.wait_ge(sem("masks_loaded"), 48)
            dve.wait_ge(sem("x2_stored"), 16)
            attn_dve(dve, A2, 0, len(STEPS2))

            def gate_mul(n):
                cc = bass.ds(n * NCH, NCH)
                used(dve, n * 12 + (U_MRG + 12))
                dve.wait_ge(sem("gate_sigmoid"), n * 2 + 2)
                for s in range(4):
                    dve.tensor_tensor(sig[:, s, :], sig[:, s, :], ps[4 + s][:, :], ALU.mult)
                dve.drain()
                for tk in range(2):
                    m = dve.tensor_tensor(mrg[:, tk, cc], sig[:, tk, :], sig[:, 2 + tk, :], ALU.add)
                m.then_inc(sem("merged_chunk"), 1)

            def merge(n, first=False):
                g = 3 * n + U_MRG // 4
                lo(dve, g, 0)
                lo(dve, g, 1)
                if not first:
                    gate_mul(n - 1)
                lo(dve, g, 2)
                lo(dve, g, 3)
                for q in range(4):
                    lo(dve, g + 1, q)
                for q in range(4):
                    lo(dve, g + 2, q)
            merge(0, True)
            with dve.Fori(1, 4) as n:
                merge(n)
            lo(dve, U_OUT2 // 4, 0)
            lo(dve, U_OUT2 // 4, 1)
            start_dve(dve, "mrg", U_OUT2, 0, lambda g: gate_mul(3) if g == 2 else None)
            out_dve(dve, "x3", U_OUT2, None, U_FFN2, 1)
            dve.wait_ge(sem("g_mlp_loaded"), 16)
            dve.wait_ge(sem("x3_rstd"), 1)
            start_dve(dve, "h4", U_FFN2, 2, scaled("h4", ybuf, xres, gvec))

            def finish_2(q):
                cc = slice(q * NCH, (q + 1) * NCH)
                for i in range(2):
                    m = dve.tensor_tensor(xres[:, i, cc], xres[:, i, cc], ybuf[:, i, cc], ALU.add)
                m.then_inc(sem("x4_chunk"), 1)
            ffn_dve(dve, "ff2", U_FFN2, N_FF2, False, finish_2, None)
            sum_squares(dve, "x4", 4, [(SQ1, SS)])
            dve.wait_ge(sem("g_final_loaded"), 16)
            dve.wait_ge(sem("x4_rstd"), 1)
            for q in range(4):
                scaled("out", ybuf, xres, gvec)(q)

        @block.tensor
        def _(pe):
            pe.wait_ge(sem("ident_loaded"), 48)
            pe.wait_ge(sem("c_silu"), 1)
            pe.transpose(ps[7][:, 0:32], csig[:, :], ident[0:32, 0:32]).then_inc(sem("c_cols"), 1)
            pe.wait_ge(sem("c_lo"), 1)

            def rows_complete(c, b):
                pe.wait_ge(sem("ada_rows"), c + 1)
                pe.wait_ge(sem(f"b_loaded{b}"), 8 * (c - b) + 16)

            def combine(c, b, bank):
                pe.matmul(ps[bank][0:1, :], esel[:, 0:1], rows_of(c, b), start=True, stop=True)\
                    .then_inc(sem("ada_combined"), 1)

            def ada_unit(u4, q, k0, bank):
                for j in range(KQ):
                    if j % 2 == 0:
                        pe.wait_ge(sem("lo_made"), 8 * u4 + (2 * q + 1 + j // 2))
                    k = k0 + j
                    pe.matmul(ps[bank][0:4, :], cst[:, k, :], whi[:, q % 2, j, :], start=k == 0, stop=False)
                    m = pe.matmul(ps[bank][0:4, :], cst[:, k, :], wlo[:, q % 2, j, :], start=False, stop=k == 15)
                    if j % 2 == 1:
                        m.then_inc(sem("unit_used"), 1)

            def spread_row(c):
                rows_complete(c, c % 2)
                wait(pe, "mod_row", c)
                for v in range(2):
                    m = pe.matmul(ps[v][:, :], spread[:, v, :], rows_of(c, c % 2), start=True, stop=True)
                m.then_inc(sem("ada_combined"), 1)

            for c in range(N_ADA_1):
                wait(pe, "ada_rows", c - 1)
                for q in range(4):
                    ada_unit(c, q, 4 * q, 2 + c % 2)
                    if q == 1 and c:
                        spread_row(c - 1)
                    if q == 2 and c >= 5:
                        if c == 5:
                            pe.wait_ge(sem("na_bias_made"), 1)
                        turn_h_pe(pe, c - 5)
                if c == 0:
                    pe.wait_ge(sem("na_rpb_lo"), 1)
                    for j in range(64):
                        m = pe.matmul(ps[4 + j // 16][:, (j % 16) * 28:(j % 16) * 28 + 28], bandr[:, 63 - j:191 - j],
                                      narpbr[:, :], start=True, stop=True)
                    m.then_inc(sem("na_bands"), 1)

            for n, (kind, c, k) in enumerate(MIX):
                u = U_MIX + n
                if n == 2:
                    spread_row(N_ADA_1 - 1)
                    turn_h_pe(pe, 3)
                    pe.wait_ge(sem("h_lo"), 16)
                if n >= 2 and MIX[n - 2][0] == "ada" and MIX[n - 2][2] == 3:
                    done = MIX[n - 2][1]
                    rows_complete(done, done % 2)
                    pe.wait_ge(sem("mod_row"), done)
                    combine(done, done % 2, ada_banks(done)[1])
                if kind == "ada":
                    if k == 0:
                        pe.wait_ge(sem("ada_rows"), c)
                        if ada_banks(c) != ada_banks(c - 1):
                            pe.wait_ge(sem("win_copied_a"), 4)
                            pe.wait_ge(sem("win_copied_d"), 4)
                    ada_unit(u // 4, u % 4, 4 * k, ada_banks(c)[0])
                    continue
                col, w, cx = WIN[c]
                if k == 0:
                    wait(pe, "win_copied_a", c - 1)
                    wait(pe, "win_copied_d", c - 1)
                    if c in (4, 9):
                        pe.wait_ge(sem("mod_row"), N_ADA_1 + (8 if c == 4 else 16))
                toks = (0, 1) if cx is None else (0, 1, 2, 3)
                b = 4 * (c % 2)
                unit(pe, u // 4, u % 4, ps[b:b + len(toks)], [XA, XB], 4 * k, k == 0, k == 3, w=w, toks=toks)

            pe.wait_ge(sem("mla_normed"), 1)
            pe.wait_ge(sem("win_copied_a"), len(WIN))
            pe.wait_ge(sem("win_copied_d"), len(WIN))
            for i in range(2):
                for j in range(4):
                    pe.transpose(ps[i][:, j * P:j * P + P], PL[:, i, ML_Q + j * P:ML_Q + j * P + P], ident[:, :])
            for i in range(4):
                ckv = PL[:, i, ML_KV:ML_KV + 320] if i < 2 else PC[:, i - 2, CX_ML:CX_ML + 320]
                for j in range(2):
                    b = (i % 2) * 256 + j * P
                    pe.transpose(ps[2 + i // 2][:, b:b + P], ckv[:, j * P:j * P + P], ident[:, :])
                m = pe.transpose(ps[4][0:64, i * P:i * P + P], ckv[:, 256:320], ident[:, :])
            m.then_inc(sem("mla_turned"), 1)
            g = U_MLA // 4
            pe.wait_ge(sem("mla_lo"), 1)
            pe.wait_ge(sem("kpe_copied"), 1)
            unit(pe, g, 0, ps[0:2], XQ, 0, True, True)
            unit(pe, g, 1, ps[2:4], XQ, 0, True, True, w=256)
            unit(pe, g, 2, ps[4:8], XKV, 0, True, True, k=2, toks=(0, 1, 2, 3))
            pe.wait_ge(sem("mla_copied_a"), 1)
            pe.wait_ge(sem("mla_copied_d"), 1)
            unit(pe, g, 3, ps[0:4], XKV, 0, True, True, k=2, toks=(0, 1, 2, 3))
            pe.wait_ge(sem("mla_copied_a"), 2)
            pe.wait_ge(sem("mla_copied_d"), 2)
            pe.wait_ge(sem("rotated_pe"), 1)
            attn_pe(pe, A1, 0, len(STEPS))
            pe.wait_ge(sem("att_out_lo"), 16)
            out_pe(pe, "x1_chunk", U_OUT, 0)

            def made(T):
                return lambda g, i: pe.wait_ge(sem(T + "_ready"), 2 * g + i + 1)
            tiles_y = [ybuf[:, i, :] for i in range(2)]
            start_pe(pe, "h2", tiles_y, U_FFN, 0, made("h2"))
            ffn_pe(pe, "ff1", U_FFN, N_FF, True)
            start_pe(pe, "h3", [h3[:, i, :] for i in range(2)], U_WIN2, 0, made("h3"))
            pe.wait_ge(sem("wf_lo"), 1)
            for k in range(16):
                pe.matmul(ps[4][0:8, 0:SEQ], wfh[:, k, :], XA[0][:, k, :], start=k == 0, stop=False)
                pe.matmul(ps[4][0:8, 0:SEQ], wfh[:, k, :], XA[1][:, k, :], start=False, stop=False)
                m = pe.matmul(ps[4][0:8, 0:SEQ], wfl[:, k, :], XA[0][:, k, :], start=False, stop=k == 15)
            m.then_inc(sem("f_acc"), 1)

            def qkv2(i, first=False):
                for b in range(2):
                    if first and b == 0:
                        continue
                    wait(pe, "qkv2_a", 2 * i + (b - 1))
                    wait(pe, "qkv2_d", 2 * i + (b - 1))
                    for q in range(4):
                        unit(pe, U_WIN2 // 4 + 2 * i + b, q, ps[2 * b:2 * b + 2], XA, 4 * q, q == 0, q == 3)
            qkv2(0, True)
            pe.wait_ge(sem("z_copied"), 1)
            for i in range(2):
                m = pe.transpose(ps[5][:, 8 * i:8 * i + 8], zT[:, i * P:i * P + P], ident[0:8, 0:8])
            m.then_inc(sem("z_turned"), 1)
            with pe.Fori(1, N_QKV2 // 2) as i:
                qkv2(i)
            pe.wait_ge(sem("qkv2_a"), N_QKV2)
            pe.wait_ge(sem("qkv2_d"), N_QKV2)
            pe.wait_ge(sem("nlf_made"), 1)
            pe.wait_ge(sem("masks_loaded"), 48)
            attn_pe(pe, A2, 0, len(STEPS2))
            pe.wait_ge(sem("att2_out_lo"), 16)

            def merge(n):
                g = 3 * n + U_MRG // 4
                wait(pe, "gate_sigmoid", n * 2)
                for b in range(2):
                    for q in range(4):
                        unit(pe, g + b, q, ps[2 * b:2 * b + 2], XA, 4 * q, q == 0, q == 3)
                wait(pe, "merged_chunk", n)
                for q in range(4):
                    b = 4 if q < 2 else 6
                    unit(pe, g + 2, q, ps[b:b + 2], XB, 4 * q, q % 2 == 0, q % 2 == 1)
            merge(0)
            with pe.Fori(1, 4) as n:
                merge(n)

            def merged(g, i):
                pe.wait_ge(sem("gate_sigmoid"), 8)
                pe.wait_ge(sem("merged_chunk"), g + 1 if g < 2 else 4)
            start_pe(pe, "mrg", [mrg[:, i, :] for i in range(2)], U_OUT2, 0, merged)
            out_pe(pe, "x3_chunk", U_OUT2, 1)
            start_pe(pe, "h4", tiles_y, U_FFN2, 2, made("h4"))
            ffn_pe(pe, "ff2", U_FFN2, N_FF2, False)

        @block.gpsimd
        def _(pool):
            for dst, src in ((cos128, t["cos128"]), (sin128, t["sin128"]), (cos64, t["cos64"]), (sin64, t["sin64"])):
                pool.dma_start(dst[:, :, :], src).then_inc(sem("small_loaded"), 16)
            for dst, src, n in ((g_gq, t["gqa_gq"], 128), (g_gk, t["gqa_gk"], 128), (g_sub, t["diff_gsub"], 128),
                                (g_mq, t["mla_gq"], 512), (g_mkv, t["mla_gkv"], 256)):
                pool.dma_start(dst[:, :], bcast(src, n)).then_inc(sem("small_loaded"), 16)
            pool.dma_start(gvec[:, :], bcast(t["g_attn"], D)).then_inc(sem("g_attn_loaded"), 16)

            with nc.allow_non_contiguous_dma(reason="31 x 28 table, once"):
                pool.wait_ge(sem("na_rpb_zero"), 1)
                for h in range(4):
                    for p in (0, 32):
                        pool.dma_start(narpb[p:p + 31, h * 7:h * 7 + 7], t["na_rpb"][0, h, 4:11, :].rearrange("r m -> m r"))\
                            .then_inc(sem("na_rpb_loaded"), 16)
            pool.dma_start(band[:, :], t["na_band"]).then_inc(sem("na_band_loaded"), 16)
            pool.dma_start(namask[:, :], t["na_mask"]).then_inc(sem("na_mask_loaded"), 16)
            pool.wait_ge(sem("halves"), 1)
            rstd_pool(pool, "x", 4, "_squares")

            def modulate(q):
                cc = slice(q * NCH, (q + 1) * NCH)
                pool.wait_ge(sem("mod_row"), q + 1)
                for i in range(4):
                    m = pool.tensor_tensor(xin[:, i, cc], xin[:, i, cc], scale_g[:, i // 2, :], ALU.mult)
                m.then_inc(sem("x_modulated"), 1)
            pool.wait_ge(sem("x_scaled"), 1)
            modulate(0)
            pool.wait_ge(sem("na_bias_made"), 1)
            pool.dma_start(nab_d, nab_1[:, :, :, :]).then_inc(sem("na_bias_stored"), 16)
            for q in range(1, 4):
                modulate(q)

            def norm(x, g, width, n, col):
                pool_rstd(pool, stat(col, n), stat(col, n), n, width)
                pool.drain()
                pool.tensor_tensor(x, x, stat(col, n).rearrange("p (a b) -> p a b", b=1)
                                   .to_broadcast([P, n, width]), ALU.mult)
                pool.drain()
                pool.tensor_tensor(x, x, g[:, 0:width].rearrange("p (a b) -> p a b", a=1)
                                   .to_broadcast([P, n, width]), ALU.mult)
                pool.drain()

            def rope(x, cos, sin, half, n):
                a = ropeA[:, 0:2 * n * half].rearrange("p (n s h) -> p n s h", n=n, s=2)
                b = ropeB[:, 0:2 * n * half].rearrange("p (n s h) -> p n s h", n=n, s=2)
                for s in range(2):
                    c3 = cos.rearrange("p (a h) -> p a h", a=1).to_broadcast([P, n, half])
                    s3 = sin.rearrange("p (a h) -> p a h", a=1).to_broadcast([P, n, half])
                    pool.tensor_tensor(a[:, :, s, :], x[:, :, s, :], c3, ALU.mult)
                    pool.tensor_tensor(b[:, :, s, :], x[:, :, s, :], s3, ALU.mult)
                pool.drain()
                pool.tensor_tensor(x[:, :, 0, :], a[:, :, 0, :], b[:, :, 1, :], ALU.subtract)
                m = pool.tensor_tensor(x[:, :, 1, :], b[:, :, 0, :], a[:, :, 1, :], ALU.add)
                pool.drain()
                return m

            def copied(c):
                if c in WIN_SQ:
                    pool.wait_ge(sem("win_squared"), sorted(WIN_SQ).index(c) + 1)
                pool.wait_ge(sem("win_copied_a"), c + 1)
                pool.wait_ge(sem("win_copied_d"), c + 1)

            pool.wait_ge(sem("h_ready"), 16)
            for i, name in enumerate(("diff_lq1", "diff_lk1", "diff_lq2", "diff_lk2")):
                pool.dma_start(lamv[:, i, :], bcast(t[name], 64)).then_inc(sem("small_loaded"), 16)
            pool.wait_ge(sem("small_loaded"), 16 * 13)
            copied(0)
            for i in range(2):
                norm(PL[:, i:i + 1, ML_Q:ML_Q + 512], g_mq, 512, 1, NCQ + i)
            copied(1)
            for i in range(2):
                norm(PL[:, i:i + 1, ML_KV:ML_KV + 256], g_mkv, 256, 1, NCKV + i)
                norm(PC[:, i:i + 1, CX_ML:CX_ML + 256], g_mkv, 256, 1, NCKV + 2 + i)
                rope(PL[:, i, ML_PE:ML_PE + 64].rearrange("p (n s h) -> p n s h", n=1, s=2), cos64[:, i, :],
                     sin64[:, i, :], 32, 1)
            pool.drain().then_inc(sem("mla_normed"), 1)
            for c, col in ((2, DF_Q), (3, DF_K)):
                copied(c)
                for i in range(2):
                    rope(PL[:, i, col:col + 512].rearrange("p (n s h) -> p n s h", s=2, h=32), cos64[:, i, :],
                         sin64[:, i, :], 32, 8)
            copied(5)
            for i in range(2):
                norm(PL[:, i, GQ_Q:GQ_Q + 512].rearrange("p (n d) -> p n d", d=HD), g_gq, HD, 4, NGQ + 4 * i)
                rope(PL[:, i, GQ_Q:GQ_Q + 512].rearrange("p (n s h) -> p n s h", s=2, h=64), cos128[:, i, :],
                     sin128[:, i, :], 64, 4)
            copied(6)
            for i in range(2):
                norm(PL[:, i, GQ_K:GQ_K + 256].rearrange("p (n d) -> p n d", d=HD), g_gk, HD, 2, NGK + 2 * i)
                norm(PC[:, i, CX_GK:CX_GK + 256].rearrange("p (n d) -> p n d", d=HD), g_gk, HD, 2, NGK + 4 + 2 * i)
                rope(PL[:, i, GQ_K:GQ_K + 256].rearrange("p (n s h) -> p n s h", s=2, h=64), cos128[:, i, :],
                     sin128[:, i, :], 64, 2)
            pool.wait_ge(sem("mla_copied_a"), 1)
            pool.wait_ge(sem("mla_copied_d"), 1)
            for i in range(2):
                q = PL[:, i, ML_Q:ML_Q + 768].rearrange("p (n d) -> p n d", d=192)[:, :, 128:192]
                rope(q.rearrange("p n (s h) -> p n s h", s=2), cos64[:, i, :], sin64[:, i, :], 32, 4)
            pool.drain().then_inc(sem("rotated_pe"), 1)

            pool.wait_ge(sem("att_out"), 4)
            pool.wait_ge(sem("na_bias_stored"), 16)
            pool.dma_start(nabias[:, :, :, :], nab_d).then_inc(sem("na_bias_loaded"), 16)
            for h in range(4):
                pool.wait_ge(sem("diff_squares"), h + 1)
                pool_rstd(pool, stat(ORS, 2), stat(OSS, 2), 2, HD).then_inc(sem("diff_rstd"), 1)

            pool.wait_ge(sem("att_out_lo"), 16)
            for b in range(2):
                pool.wait_ge(sem(f"late_mod_stored{b}"), 8 * (N_ADA - N_ADA_1))
            pool.dma_start(xres[:, :, :], x_v).then_inc(sem("x1_chunk_loaded"), 16)
            for dst, n in ((gt_a, 2), (sh_f, 3), (sc_f, 4), (gt_f, 5)):
                pool.dma_start(dst[:, :], bcast(mod_d[:, (n - 2) * D:(n - 1) * D], D)).then_inc(sem("x1_chunk_loaded"), 16)
            pool.dma_start(gvec[:, :], bcast(t["g_ffn"], D)).then_inc(sem("x1_chunk_loaded"), 16)
            rstd_pool(pool, "x1", 2, "_summed")
            pool.wait_ge(sem("x1_chunk"), 4)
            pool.dma_start(gt_a[:, :], bcast(t["g_final"].rearrange("(a n) -> a n", a=1), D))\
                .then_inc(sem("g_first_loaded"), 16)
            pool.wait_ge(sem("h2_ready"), 8)
            pool.dma_start(gvec[:, :], bcast(t["norm_mix_g_2"].rearrange("(a n) -> a n", a=1), D))\
                .then_inc(sem("g_mix_loaded"), 16)
            with nc.allow_non_contiguous_dma(reason="eight columns of w_in_2"):
                pool.dma_start(wf[:, :, :], t["w_in_2"].rearrange("(k p) n -> p k n", p=P)[:, :, 6144:6152])\
                    .then_inc(sem("wf_loaded"), 16)
            pool.dma_start(bf[:, :], bcast(t["b_forget_2"].rearrange("(a n) -> a n", a=1), 8)).then_inc(sem("wf_loaded"), 16)
            for dst, src in ((distm, t["distance"]), (causal, t["causal"]), (tri, t["triangle"])):
                pool.dma_start(dst[:, :, :], src).then_inc(sem("masks_loaded"), 16)
            pool.wait_ge(sem("g_first_loaded"), 16)
            for q in range(4):
                pool.wait_ge(sem("xf_chunk"), q + 1)
                cc = slice(q * NCH, (q + 1) * NCH)
                for i in range(2):
                    m = pool.tensor_tensor(ybuf[:, i, cc], xres[:, i, cc], gt_a[:, cc], ALU.mult)
                m.then_inc(sem("xg_chunk"), 1)
            pool.wait_ge(sem("xf_summed"), 1)
            r1, r2, r12 = stat(RSTD + 2, 2), stat(SS + 2, 2), stat(RSTD, 2)
            pool_rstd(pool, r1, stat(SS, 2), 2, D)
            for k in range(2):
                pool.drain()
                pool.tensor_tensor(r2, r2, r1, ALU.mult)
            pool.drain()
            pool_rstd(pool, r2, r2, 2, D)
            pool.drain()
            pool.tensor_tensor(r12, r1, r2, ALU.mult).then_inc(sem("xf_rstd"), 1)
            pool.drain()
            for i in range(2):
                pool.tensor_tensor(xres[:, i, :], ybuf[:, i, :], stat(RSTD + 2 + i).to_broadcast([P, D]), ALU.mult)
            pool.drain().then_inc(sem("x2_made"), 1)
            pool.dma_start(x2_d, xres[:, :, :]).then_inc(sem("x2_stored"), 16)
            pool.wait_ge(sem("h3_ready"), 8)
            pool.dma_start(gvec[:, :], bcast(t["norm_mlp_g_2"].rearrange("(a n) -> a n", a=1), D))\
                .then_inc(sem("g_mlp_loaded"), 16)
            pool.wait_ge(sem("x2_stored"), 16)
            pool.wait_ge(sem("att2_out_lo"), 16)
            pool.dma_start(xres[:, :, :], x2_d).then_inc(sem("x3_chunk_loaded"), 16)
            rstd_pool(pool, "x3", 2, "_summed")
            pool.wait_ge(sem("h4_ready"), 8)
            pool.dma_start(gvec[:, :], bcast(t["norm_final_g_2"].rearrange("(a n) -> a n", a=1), D))\
                .then_inc(sem("g_final_loaded"), 16)
            rstd_pool(pool, "x4", 2, "_summed")


_INS = ["x", "c", "ctx", "c_ctx", "w_ada", "b_ada", "g_attn", "g_ffn", "w_in", "w_out", "na_rpb", "gqa_gq",
        "gqa_gk", "mla_gq", "mla_gkv", "mla_wuq", "mla_wukv", "diff_lq1", "diff_lk1", "diff_lq2", "diff_lk2",
        "diff_gsub", "ffn_wg", "ffn_wu", "ffn_wd", "g_final", "norm_mix_g_2", "w_in_2", "b_forget_2", "w_proj_a_2",
        "w_proj_b_2", "w_out_2", "norm_mlp_g_2", "w_up_2", "w_down_2", "norm_final_g_2"]


def constants():
    tok = np.arange(SEQ)
    row, col = (tok // 64).astype(np.float32), (tok % 64).astype(np.float32)

    def rope(dim):
        axis = dim // 2
        inv = (1.0 / (np.float32(10000.0) ** (np.arange(0, axis, 2, dtype=np.float32) / np.float32(axis)))).astype(np.float32)
        ang = np.concatenate([row[:, None] * inv, col[:, None] * inv], axis=-1).astype(np.float32)
        tile = lambda a: np.ascontiguousarray(a.reshape(2, P, -1).transpose(1, 0, 2).astype(np.float32))
        return tile(np.cos(ang)), tile(np.sin(ang))
    cos128, sin128 = rope(128)
    cos64, sin64 = rope(64)
    select = np.zeros((5, 2), np.float32)
    select[[0, 1, 4], 0] = 1
    select[[2, 3, 4], 1] = 1
    spread = np.ascontiguousarray(np.repeat(select[:, :, None], P, axis=2))
    c, j = np.arange(P) % 64, np.arange(64)
    start = np.clip(c - 8, 0, 48)
    inside = (j[None] >= start[:, None]) & (j[None] < start[:, None] + 16)
    na_mask = np.where(inside, 0.0, -1e30).astype(np.float32)
    m, y = np.arange(31)[:, None], np.arange(191)[None] - 63
    na_band = np.zeros((63, 191), np.float32)
    na_band[0:31] = na_band[32:63] = (m == 15 - y) | (m == 79 - y)
    q = np.arange(SEQ)
    dist = (q[:, None] - q[None, :]).astype(np.float32)
    tiles = lambda a: np.ascontiguousarray(a.astype(np.float32).reshape(2, P, SEQ).transpose(1, 0, 2))
    return {"identity": np.eye(P, dtype=np.float32), "row_select": select, "row_spread": spread, "cos128": cos128, "sin128": sin128,
            "cos64": cos64, "sin64": sin64, "na_mask": na_mask, "na_band": na_band,
            "distance": tiles(np.where(dist >= 0, dist, 1e30)), "causal": tiles(np.where(dist >= 0, 0.0, -1e30)),
            "triangle": tiles(q[:, None] <= q[None, :])}


def kernel(**inputs):
    import concourse.bacc as bacc
    from concourse.bass_utils import run_bass_kernel_spmd

    nc = bacc.Bacc("TRN2", target_bir_lowering=False, num_devices=1)
    arrays, t = {}, {}
    for name, a in [(n, inputs[n]) for n in _INS] + list(constants().items()):
        a = np.ascontiguousarray(a)
        arrays[f"in_{name}"] = a
        t[name] = nc.dram_tensor(f"in_{name}", a.shape, mybir.dt.from_np(a.dtype), kind="ExternalInput").ap()
    t["out"] = nc.dram_tensor("out_x", (1, SEQ, D), F32, kind="ExternalOutput").ap()
    build(nc, t)
    r = run_bass_kernel_spmd(nc, [arrays], core_ids=[0])
    return r.results[0]["out_x"]
```

```python
from contextlib import ExitStack
import math

import numpy as np

import concourse.bass as bass
from concourse import mybir
from concourse.alu_op_type import AluOpType as ALU

F32 = mybir.dt.float32
F32R = mybir.dt.float32r
ACT = mybir.ActivationFunctionType
AX = mybir.AxisListType

P = 128
D = 2048
SEQ = 256
NCH = 512
KQ = 4
HD = 128
EPS = 1e-6
D_IN = 4928
D_FF = 5632
D_IN_2 = 10248
D_FF_2 = 8192
KB = 1024
BASE = 16512

NA_Q, NA_K, NA_V, GQ_Q, GQ_K, GQ_V = 0, 512, 1024, 1536, 2048, 2304
ML_Q, ML_KV, ML_PE, DF_Q, DF_K, DF_V = 2560, 3072, 3328, 3392, 3904, 4416
CX_ML, CX_DK, CX_DV, CX_GK, CX_NK, CX_NV, CX_W = 0, 320, 832, 1344, 1856, 2368, 2880
WIN = [(ML_Q, 512, None), (ML_KV, 320, CX_ML), (DF_Q, 512, None), (DF_K, 512, CX_DK), (DF_V, 512, CX_DV),
       (GQ_Q, 512, None), (GQ_K, 512, CX_GK), (NA_Q, 512, None), (NA_K, 512, CX_NK), (NA_V, 512, CX_NV)]

N_ADA = 6 * D // NCH
N_ADA_1 = 2 * D // NCH
U_MIX = 4 * N_ADA_1
U_MLA = U_MIX + 4 * len(WIN) + 4 * (N_ADA - N_ADA_1)
U_OUT = U_MLA + 4
U_FFN = U_OUT + 4 * (D // NCH)
N_FF = D_FF // NCH
U_WIN2 = U_FFN + 12 * N_FF
N_QKV2 = 12
U_MRG = U_WIN2 + 4 * N_QKV2
U_OUT2 = U_MRG + 12 * (D // NCH)
U_FFN2 = U_OUT2 + 4 * (D // NCH)
N_FF2 = D_FF_2 // NCH
LAM0 = 0.8 - 0.6 * math.exp(-0.3 * 0)


def mixed_units():
    per = [1, 2, 1, 2, 3, 1, 2, 1, 3, 0]
    units, a = [], 4 * N_ADA_1
    for c in range(len(WIN)):
        for q in range(4):
            units.append(("win", c, q))
            for _ in range(per[c]):
                units.append(("ada", a // 4, a % 4))
                a += 1
    assert a == 4 * N_ADA
    return units


MIX = mixed_units()
LAST = {(kind, c): n for n, (kind, c, q) in enumerate(MIX) if q == 3}
W = [n for n, m in enumerate(MIX) if m[0] == "win"]
FOLLOW = [(W + [len(MIX)])[i + 1] - W[i] - 1 for i in range(len(W))]
ADD_UP = {c: min(i for i, n in enumerate(W) if n > LAST["ada", c] and MIX[n][2] >= 1)
          for c in range(N_ADA_1, N_ADA)}


def sum_bank(c):
    return 4 * ((MIX[W[ADD_UP[c]]][1] + 1) % 2) + 2 + c % 2


def head_steps():
    steps, a, d = [], 0, 0
    for kind, n in (("mla", 4), ("diff", 8), ("gqa", 4), ("na", 4)):
        for m in range(n):
            half = m % 2 if kind == "diff" else 0
            head = m // 2 if kind == "diff" else m
            turn, value = half == 0, kind != "diff" or half == 1
            steps.append(dict(kind=kind, head=head, half=half, a=a if turn else a - 1, turn=turn,
                              d=d if value else None))
            a += turn
            d += value
    return steps


def head_steps_2():
    return [dict(kind=k, head=h, half=0, a=n, turn=True, d=n)
            for n, (k, h) in enumerate([("moba", h) for h in range(8)] + [("fox", h) for h in range(8)])]


def build(nc, t):
    ctx = ExitStack()
    with ctx:
        sems = {}

        def sem(name):
            if name not in sems:
                sems[name] = ctx.enter_context(nc.semaphore(name))
            return sems[name]

        def at(name, shape, dt, kb):
            return nc.alloc_sbuf_tensor_at(name, shape, dt, offset=BASE + int(kb * KB))

        def wait(eng, name, value):
            if isinstance(value, int) and value <= 0:
                return
            eng.wait_ge(sem(name), value)

        ps = [ctx.enter_context(nc.psum_tensor(f"bank{b}", [P, 512], F32)) for b in range(8)]

        raw = at("w_raw", [P, 4, KQ, NCH], F32, 0)
        whi = at("w_hi", [P, 2, KQ, NCH], F32R, 32)
        wlo = at("w_lo", [P, 2, KQ, NCH], F32R, 48)
        XA = (at("xa_hi", [P, 16, SEQ], F32R, 64), at("xa_lo", [P, 16, SEQ], F32R, 80))
        XB = (at("xb_hi", [P, 16, SEQ], F32R, 96), at("xb_lo", [P, 16, SEQ], F32R, 112))
        cst = at("c_stationary", [P, 16, 4], F32R, 198.75)
        rows_1 = at("ada_rows", [5, 2, NCH], F32, 160)
        scale_g = at("scale_g", [P, 2, NCH], F32, 164)
        spread = at("row_spread", [5, 2, 128], F32, 180)
        nab_1 = at("na_bias_early", [P, 4, 2, 256], F32, 64)
        band = at("na_band", [63, 191], F32, 72)
        bandr = at("na_band_r", [63, 191], F32R, 73)
        narpbr = at("na_rpb_hi_lo", [63, 28], F32R, 74)
        namask = at("na_mask", [P, 64], F32, 104)
        narpb = at("na_rpb_T", [63, 28], F32, 104.25)
        xin = at("x_in", [P, 4, D], F32, 128)
        crow = at("c_rows", [32, 128], F32, 178)
        csig = at("c_silu", [32, 128], F32, 178.5)
        ccol = at("c_cols", [P, 32], F32, 199.25)
        ones = at("ones", [P, 1], F32, 199.5)
        junk = at("squares", [P, D], F32, 168)
        PL = at("proj_x", [P, 2, D_IN], F32, 128)
        PC = at("proj_ctx", [P, 2, CX_W], F32, 128 + 38.5)
        kpeT = at("mla_kpe_T", [64, 512], F32, 128 + 61)
        def rows_of(b):
            return rows_1[:, b, :]

        def late_sums(b):
            return PC[:, b, CX_NV:CX_NV + NCH]

        def late_row(b):
            return PL[0:1, b, NA_V:NA_V + NCH]

        late_b = (at("late_b_0", [1, NCH], F32, 205.75), at("late_b_1", [1, NCH], F32, 189))
        XQ = (at("mla_cq_hi", [P, 4, SEQ], F32R, 96), at("mla_cq_lo", [P, 4, SEQ], F32R, 100))
        XKV = (at("mla_ckv_hi", [P, 2, 512], F32R, 104), at("mla_ckv_lo", [P, 2, 512], F32R, 108))
        mkv = at("mla_kv", [P, 4, 1024], F32, 112)
        kT = at("k_T", [P, 2, 512], F32, 96)
        qT = at("q_T", [P, 2, 512], F32, 100)
        probs = at("probs", [P, 2, 2, 512], F32, 104)
        probsT = at("probs_T", [P, 2, 4, SEQ], F32, 192 + 7.75)
        nabias = at("na_bias", [P, 4, 2, 256], F32, 112)
        od = at("diff_out", [P, 2, 2, 128], F32, 120)
        ident = at("identity", [P, P], F32, 192)
        small = at("small", [P, 64], F32, 192.5)
        cos128 = at("cos128", [P, 2, 64], F32, 192.75)
        sin128 = at("sin128", [P, 2, 64], F32, 193.25)
        cos64 = at("cos64", [P, 2, 32], F32, 193.75)
        sin64 = at("sin64", [P, 2, 32], F32, 194)
        g_gq = at("gqa_gq_row", [P, 128], F32, 194.25)
        g_gk = at("gqa_gk_row", [P, 128], F32, 194.75)
        g_sub = at("diff_gsub_row", [P, 128], F32, 195.25)
        g_mq = at("mla_gq_row", [P, 512], F32, 195.75)
        g_mkv = at("mla_gkv_row", [P, 256], F32, 197.75)
        lamv = at("diff_lambdas", [P, 4, 64], F32, 191)
        gvec = at("g_row", [P, D], F32, 192 + 7.75)
        ropeA = at("rope_a", [P, 512], F32, 192 + 7.75)
        ropeB = at("rope_b", [P, 512], F32, 192 + 9.75)
        psq = at("win_squares", [P, 512], F32, 192 + 11.75)
        pstat = at("pool_stats", [P, 24], F32, 192 + 15.75)
        x_one = at("x_one", [P, 2, D_IN], F32, 128)[:, :, 0:D]
        gt_a = at("gt_a", [P, D], F32, 138.25)
        sc_f = at("sc_f", [P, D], F32, 157.5)
        gt_f = at("gt_f", [P, D], F32, 166)
        sh_f = at("sh_f", [P, D], F32, 108)
        ybuf = at("y_sum", [P, 2, D], F32, 176)
        tmp = at("gated", [P, 2, NCH], F32, 116)
        xres = at("x_res", [P, 2, D], F32, 128)
        squared = at("squared", [P, 2, NCH], F32, 104)
        squared_3 = at("squared_3", [P, 2, NCH], F32, 168)
        act_g = at("ffn_gate", [P, 2, NCH], F32, 116)
        act_a = at("ffn_act", [P, 2, NCH], F32, 120)
        XF = (at("ffn_act_hi", [P, 4, SEQ], F32R, 96), at("ffn_act_lo", [P, 4, SEQ], F32R, 100))
        h3 = (at("h_mix_0", [P, D], F32, 157.5), at("h_mix_1", [P, D], F32, 108))
        P2 = at("proj_2", [P, 2, 6144], F32, 144)
        wf = at("w_forget", [P, 16, 8], F32, 124)
        wfh = at("w_forget_hi", [P, 16, 8], F32R, 124.5)
        wfl = at("w_forget_lo", [P, 16, 8], F32R, 125)
        bf = at("b_forget", [P, 8], F32, 125.5)
        fz = at("forget_work", [P, 6, 2, 8], F32, 126)
        zT = at("forget_z_T", [8, SEQ], F32, 116)
        nlf = at("neg_log_forget", [P, 2, 8], F32, 192 + 15.75)
        distm = at("distance", [P, 2, 256], F32, 192.75)
        causal = at("causal_mask", [P, 2, 256], F32, 194.75)
        tri = at("triangle", [P, 2, 256], F32, 196.75)
        kT2 = at("k_T_2", [P, 2, 256], F32, 128)
        qT2 = at("q_T_2", [P, 2, 256], F32, 130)
        probs2 = at("probs_2", [P, 2, 2, 256], F32, 132)
        probsT2 = at("probs_T_2", [P, 2, 2, SEQ], F32, 136)
        sig = at("gate_sig", [P, 4, NCH], F32, 160)
        mrg = at("merged", [P, 2, D], F32, 144)

        def stat(n, w=1):
            return small[:, n:n + w]

        SS, RSTD = 0, 4
        MX, NM, SUM, RIN = 8, 12, 16, 20
        OSS, ORS = 24, 28
        LAM, LAMW = 32, 34
        NCQ, NCKV, NGQ, NGK = 36, 38, 42, 50
        RSTD3 = 52
        SQ1, SQ2 = 36, 44
        WIN_SQ = {0: (NCQ, 512, 1, 2), 1: (NCKV, 256, 1, 4), 5: (NGQ, HD, 4, 2), 6: (NGK, HD, 2, 4)}

        w_in_v = t["w_in"][0].rearrange("(q k p) n -> p q k n", p=P, k=KQ)
        w_ada_v = t["w_ada"][0].rearrange("(q k p) n -> p q k n", p=P, k=KQ)
        w_out_v = t["w_out"][0].rearrange("(q k p) n -> p q k n", p=P, k=KQ)
        wg_v = t["ffn_wg"][0].rearrange("(q k p) n -> p q k n", p=P, k=KQ)
        wu_v = t["ffn_wu"][0].rearrange("(q k p) n -> p q k n", p=P, k=KQ)
        wd_v = t["ffn_wd"][0].rearrange("(q k p) n -> p q k n", p=P, k=KQ)
        wuq_v = t["mla_wuq"][0].rearrange("(k p) n -> p k n", p=P)
        wukv_v = t["mla_wukv"][0].rearrange("(k p) n -> p k n", p=P)
        w_in2_v = t["w_in_2"].rearrange("(q k p) n -> p q k n", p=P, k=KQ)
        wpa_v = t["w_proj_a_2"].rearrange("(q k p) n -> p q k n", p=P, k=KQ)
        wpb_v = t["w_proj_b_2"].rearrange("(q k p) n -> p q k n", p=P, k=KQ)
        w_out2_v = t["w_out_2"].rearrange("(q k p) n -> p q k n", p=P, k=KQ)
        w_up_v = t["w_up_2"].rearrange("(q k p) n -> p q k n", p=P, k=KQ)
        w_down_v = t["w_down_2"].rearrange("(q k p) n -> p q k n", p=P, k=KQ)
        x_v = t["x"][0].rearrange("(t p) n -> p t n", p=P)
        ctx_v = t["ctx"][0].rearrange("(t p) n -> p t n", p=P)
        out_v = t["out"][0].rearrange("(t p) n -> p t n", p=P)
        mod_d = nc.dram_tensor("mods_scratch", (1, 4 * D), F32).ap()
        nab_d = nc.dram_tensor("na_bias_scratch", (P, 4, 2, 256), F32).ap()
        x2_d = nc.dram_tensor("x2_scratch", (P, 2, D), F32).ap()

        def bcast(row, n):
            return row.to_broadcast([P, n])

        STEPS, STEPS2 = head_steps(), head_steps_2()

        def load(sp, u4, q, src, k=KQ, w=NCH):
            if isinstance(src, tuple):
                v, off, axis = src
                off = sp.snap(off)
                src = v[:, :, bass.ds(off, NCH)] if axis == "col" else v[:, bass.ds(off, KQ), :]
            wait(sp, "lo_made", 8 * u4 + (2 * q - 6))
            sp.dma_start(raw[:, q, 0:k, 0:w], src).then_inc(sem(f"landed{q}"), 16)

        def at_col(v, col):
            return v[:, :, col:col + NCH] if isinstance(col, int) else (v, col, "col")

        def used(eng, units):
            eng.wait_ge(sem("unit_used"), units * 2)

        def hi(act, u4, q, k=KQ, w=NCH, slot=None, before=None, follow=0):
            slot = q % 2 if slot is None else slot
            act.wait_ge(sem(f"landed{q}"), 16 * u4 + 16)
            for h in range(2):
                ks = slice(h * k // 2, (h + 1) * k // 2)
                wait(act, "unit_used", 8 * u4 + (2 * q - 3 + h) if before is None else 2 * before + 1 + h)
                act.activation(whi[:, slot, ks, 0:w], raw[:, q, ks, 0:w], ACT.Copy)\
                    .then_inc(sem("hi_made"), 1 + 2 * follow * h)

        def lo(dve, u4, q, k=KQ, w=NCH, slot=None):
            slot = q % 2 if slot is None else slot
            for h in range(2):
                ks = slice(h * k // 2, (h + 1) * k // 2)
                dve.wait_ge(sem("hi_made"), 8 * u4 + (2 * q + 1 + h))
                dve.tensor_tensor(wlo[:, slot, ks, 0:w], raw[:, q, ks, 0:w],
                                  whi[:, slot, ks, 0:w].bitcast(F32), ALU.subtract).then_inc(sem("lo_made"), 1)

        def mm3(pe, out, xh, xl, wh, wl, first, last):
            pe.matmul(out, xh, wh, start=first, stop=False)
            pe.matmul(out, xh, wl, start=False, stop=False)
            return pe.matmul(out, xl, wh, start=False, stop=last)

        def unit(pe, u4, q, outs, X, k0, first, last, k=KQ, w=NCH, toks=(0, 1), slot=None, follow=0):
            slot = q % 2 if slot is None else slot
            for j in range(k):
                if j % (k // 2) == 0:
                    pe.wait_ge(sem("lo_made"), 8 * u4 + (2 * q + 1 + 2 * j // k))
                for out, tk in zip(outs, toks):
                    Xt = X[tk // 2] if isinstance(X, list) else X
                    c = slice((tk % 2) * P, (tk % 2) * P + P) if isinstance(X, list) else slice(tk * P, tk * P + P)
                    m = mm3(pe, out[:, 0:w], Xt[0][:, k0 + j, c], Xt[1][:, k0 + j, c],
                            whi[:, slot, j, 0:w], wlo[:, slot, j, 0:w],
                            first and j == 0, last and j == k - 1)
                if (j + 1) % (k // 2) == 0:
                    m.then_inc(sem("unit_used"), 1 + (2 * follow if j == k - 1 else 0))

        def turn_h_pe(pe, g):
            for i in range(4):
                pe.wait_ge(sem("h_ready"), 4 * g + i + 1)
                wait(pe, "h_lo", 4 * g + i - 3)
                for j in range(4):
                    m = pe.transpose(ps[4 + i][:, j * P:j * P + P], xin[:, i, (4 * g + j) * P:(4 * g + j + 1) * P],
                                     ident[:, :])
                m.then_inc(sem("h_turned"), 1)

        def turn_h_act(act, g):
            if g == 0:
                act.wait_ge(sem("na_bias_stored"), 16)
            for i in range(4):
                act.wait_ge(sem("h_turned"), 4 * g + i + 1)
                act.activation((XA, XB)[i // 2][0][:, 4 * g:4 * g + 4, (i % 2) * P:(i % 2) * P + P],
                               ps[4 + i][:, :].rearrange("p (j t) -> p j t", j=4), ACT.Copy).then_inc(sem("h_hi"), 1)

        def turn_h_dve(dve, g):
            for i in range(4):
                X, c = (XA, XB)[i // 2], (i % 2) * P
                dve.wait_ge(sem("h_hi"), 4 * g + i + 1)
                dve.tensor_tensor(X[1][:, 4 * g:4 * g + 4, c:c + P], ps[4 + i][:, :].rearrange("p (j t) -> p j t", j=4),
                                  X[0][:, 4 * g:4 * g + 4, c:c + P].bitcast(F32), ALU.subtract).then_inc(sem("h_lo"), 1)

        TURN = {"h2": range(8), "mrg": range(8), "h3": [2, 3] * 4, "h4": [4, 5, 6, 7] * 2}

        INTO = {"h2": XA, "h3": XA, "mrg": XB, "h4": XA}

        def turn_pe(pe, T, srcs, g, ready):
            for i, src in enumerate(srcs):
                n = 2 * g + i
                ready(g, i)
                before = [m for m in range(n) if TURN[T][m] == TURN[T][n]]
                if before:
                    pe.wait_ge(sem(T + "_lo"), before[-1] + 1)
                for j in range(4):
                    m = pe.transpose(ps[TURN[T][n]][:, j * P:j * P + P],
                                     src[:, (4 * g + j) * P:(4 * g + j + 1) * P], ident[:, :])
                m.then_inc(sem(T + "_turned"), 1)

        def turn_act(act, T, g):
            for i in range(2):
                n = 2 * g + i
                act.wait_ge(sem(T + "_turned"), n + 1)
                act.activation(INTO[T][0][:, 4 * g:4 * g + 4, i * P:i * P + P],
                               ps[TURN[T][n]][:, :].rearrange("p (j t) -> p j t", j=4),
                               ACT.Copy).then_inc(sem(T + "_hi"), 1)

        def turn_dve(dve, T, g):
            for i in range(2):
                n = 2 * g + i
                dve.wait_ge(sem(T + "_hi"), n + 1)
                dve.tensor_tensor(INTO[T][1][:, 4 * g:4 * g + 4, i * P:i * P + P],
                                  ps[TURN[T][n]][:, :].rearrange("p (j t) -> p j t", j=4),
                                  INTO[T][0][:, 4 * g:4 * g + 4, i * P:i * P + P].bitcast(F32),
                                  ALU.subtract).then_inc(sem(T + "_lo"), 1)

        def start_pe(pe, T, srcs, U, first, ready, groups):
            for q in range(4):
                for g in groups[q]:
                    turn_pe(pe, T, srcs, g, ready)
                pe.wait_ge(sem(T + "_lo"), 2 * q + 2)
                unit(pe, U // 4, q, ps[first:first + 2], INTO[T], 4 * q, q == 0, q == 3)

        def start_act(act, T, U):
            for g in range(4):
                turn_act(act, T, g)
                if g >= 2:
                    hi(act, U // 4, g)

        def start_dve(dve, T, U, make):
            make(0)
            make(1)
            turn_dve(dve, T, 0)
            make(2)
            turn_dve(dve, T, 1)
            make(3)
            turn_dve(dve, T, 2)
            lo(dve, U // 4, 2)
            turn_dve(dve, T, 3)
            lo(dve, U // 4, 3)

        def squares_of(act, T, c, done, x, col):
            act.wait_ge(sem(done), c + 1)
            act.drain()
            for i in range(2):
                m = act.activation((squared_3 if T == "x3" else squared)[:, i, :], x[:, i, c * NCH:(c + 1) * NCH], ACT.Square,
                                   accum_out=stat(col + 4 * i + c))
            m.then_inc(sem(T + "_squares"), 1)

        def sum_squares(dve, T, count, groups):
            dve.wait_ge(sem(T + "_squares"), count)
            for col, out in groups:
                m = dve.tensor_reduce(stat(out, 2), stat(col, 8).rearrange("p (i c) -> p i c", i=2), AX.X, ALU.add)
            m.then_inc(sem(T + "_summed"), 1)

        def pool_rstd(pool, out, sums, width, n):
            pool.tensor_scalar(out, sums, 1.0 / n, EPS, ALU.mult, ALU.add)
            pool.drain()
            return pool.tensor_tensor(out, out, pstat[:, 16:16 + width], ALU.pow)

        def srcs_of(s):
            h, kind = s["head"], s["kind"]
            c = h * HD

            def lc(lat, cx):
                return [PL[:, 0, lat:lat + HD], PL[:, 1, lat:lat + HD],
                        PC[:, 0, cx:cx + HD], PC[:, 1, cx:cx + HD]]
            if kind == "mla":
                q0 = ML_Q + h * 192
                return dict(q=[PL[:, i, q0:q0 + HD] for i in range(2)],
                            qpe=[PL[:, i, q0 + HD:q0 + 192] for i in range(2)],
                            k=[mkv[:, i, h * 256:h * 256 + HD] for i in range(4)],
                            v=[mkv[:, i, h * 256 + HD:h * 256 + 256] for i in range(4)],
                            o=8 + h, scale=192 ** -0.5)
            if kind == "diff":
                return dict(q=[PL[:, i, DF_Q + c:DF_Q + c + HD] for i in range(2)],
                            k=lc(DF_K + c, CX_DK + c), v=lc(DF_V + c, CX_DV + c), o=12 + h, scale=64 ** -0.5)
            if kind == "gqa":
                e = (h // 2) * HD
                return dict(q=[PL[:, i, GQ_Q + c:GQ_Q + c + HD] for i in range(2)],
                            k=lc(GQ_K + e, CX_GK + e), v=lc(GQ_V + e, CX_GK + 256 + e), o=4 + h, scale=HD ** -0.5)
            if kind == "na":
                return dict(q=[PL[:, i, NA_Q + c:NA_Q + c + HD] for i in range(2)],
                            k=lc(NA_K + c, CX_NK + c), v=lc(NA_V + c, CX_NV + c), o=h, scale=HD ** -0.5)
            o = 0 if kind == "moba" else 3072
            return dict(q=[P2[:, i, o + c:o + c + HD] for i in range(2)],
                        k=[P2[:, i, o + 1024 + c:o + 1024 + c + HD] for i in range(2)],
                        v=[P2[:, i, o + 2048 + c:o + 2048 + c + HD] for i in range(2)],
                        o=h + (0 if kind == "moba" else 8), scale=HD ** -0.5)

        class Attn:

            def __init__(self, tag, steps, nkt, kT, qT, pr, prT, X):
                self.tag, self.steps, self.nkt = tag, steps, nkt
                self.kT, self.qT, self.pr, self.prT, self.X = kT, qT, pr, prT, X

            def wide(self):
                return self.nkt == 4

            def k_bank(self, a):
                return ps[0][:, :] if self.wide() else ps[a % 2][:, 0:SEQ]

            def q_bank(self, a):
                return ps[1][:, :] if self.wide() else ps[a % 2][:, SEQ:2 * SEQ]

            def s_bank(self, n, i):
                return ps[2 + i][:, :] if self.wide() else ps[2 + n % 2][:, i * SEQ:(i + 1) * SEQ]

            def p_bank(self, d, i):
                return ps[4 + i][:, :] if self.wide() else ps[4 + d % 2][:, i * SEQ:(i + 1) * SEQ]

            def since(self, n):
                return n if self.wide() else n - 1

            def get(self, n, lo_, hi_):
                return self.steps[n] if lo_ <= n < hi_ else None

            def last_step_of_turn(self, a):
                return max(i for i, s in enumerate(self.steps) if s["a"] == a)

            def d_before(self, n):
                return sum(1 for s in self.steps[:max(n, 0)] if s["d"] is not None)

        def attn_pe(pe, A, lo_, hi_, U, k0s):
            T, nkt = A.tag, A.nkt
            for n in range(lo_, hi_ + 4):
                s = A.get(n, lo_, hi_)
                if s and s["turn"]:
                    src = srcs_of(s)
                    wait(pe, T + "_qk_copied", A.since(s["a"]))
                    for i, k in enumerate(src["k"]):
                        pe.transpose(A.k_bank(s["a"])[:, i * P:i * P + P], k, ident[:, :])
                    for i, q in enumerate(src["q"]):
                        m = pe.transpose(A.q_bank(s["a"])[:, i * P:i * P + P], q, ident[:, :])
                    for i, q in enumerate(src.get("qpe", ())):
                        m = pe.transpose(ps[1][0:64, 256 + i * P:256 + i * P + P], q, ident[:, :])
                    m.then_inc(sem(T + "_qk_turned"), 1)
                s = A.get(n - 1, lo_, hi_)
                if s:
                    pe.wait_ge(sem(T + "_qk_copied"), s["a"] + 1)
                    wait(pe, T + "_exp_done", A.since(n - 1))
                    r, w = s["a"] % 2, nkt * P
                    rs = slice(64 * s["half"], 64 * s["half"] + 64) if s["kind"] == "diff" else slice(0, P)
                    for i in range(2):
                        extra = s["kind"] in ("mla", "fox")
                        m = pe.matmul(A.s_bank(n - 1, i), A.qT[rs, r, i * P:i * P + P], A.kT[rs, r, 0:w],
                                      start=True, stop=not extra)
                        if s["kind"] == "mla":
                            m = pe.matmul(A.s_bank(n - 1, i), A.qT[0:64, r, 256 + i * P:256 + i * P + P],
                                          kpeT[:, :], start=False, stop=True)
                        if s["kind"] == "fox":
                            for j in range(2):
                                m = pe.matmul(A.s_bank(n - 1, i),
                                              nlf[:, j, s["head"]:s["head"] + 1].to_broadcast([P, P]),
                                              tri[:, j, :], start=False, stop=j == 1)
                    m.then_inc(sem(T + "_scores"), 1)
                s = A.get(n - 2, lo_, hi_)
                if s and s["d"] is not None:
                    pe.wait_ge(sem(T + "_probs"), n - 1)
                    wait(pe, T + "_pt_copied", A.since(s["d"]))
                    for i in range(2):
                        for j in range(nkt):
                            m = pe.transpose(A.p_bank(s["d"], i)[:, j * P:j * P + P],
                                             A.pr[:, (n - 2) % 2, i, j * P:j * P + P], ident[:, :])
                    m.then_inc(sem(T + "_probs_turned"), 1)
                s = A.get(n - 3, lo_, hi_)
                if s and s["d"] is not None:
                    src, d = srcs_of(s), s["d"]
                    pe.wait_ge(sem(T + "_pt_copied"), d + 1)
                    wait(pe, T + "_out_lo", d - 1)
                    o = ps[6 + d % 2]
                    if s["kind"] == "diff":
                        for i in range(2):
                            for j in range(nkt):
                                m = pe.matmul(o[:, i * P:i * P + P], A.prT[:, d % 2, j, i * P:i * P + P],
                                              src["v"][j], start=j == 0, stop=j == nkt - 1)
                    else:
                        for j in range(nkt):
                            m = pe.matmul(o[:, 0:SEQ], src["v"][j], A.prT[:, d % 2, j, :],
                                          start=j == 0, stop=j == nkt - 1)
                    m.then_inc(sem(T + "_out"), 1)
                s = A.get(n - 4, lo_, hi_)
                if s and s["d"] is not None and s["kind"] == "diff":
                    pe.wait_ge(sem("diff_normed"), s["head"] + 1)
                    for i in range(2):
                        m = pe.transpose(ps[6 + s["d"] % 2][:, 256 + i * P:256 + i * P + P],
                                         od[:, s["head"] % 2, i, :], ident[:, :])
                    m.then_inc(sem("diff_turned"), 1)
                q = n - hi_
                if 0 <= q < 3:
                    if q == 0:
                        pe.wait_ge(sem(T + "_qk_copied"), A.steps[-1]["a"] + 1)
                    pe_next(pe, A, U, k0s, q)
            pe.wait_ge(sem(T + "_out_lo"), 16)
            pe_next(pe, A, U, k0s, 3)

        def pe_next(pe, A, U, k0s, q):
            if A.X is XA:
                pe.wait_ge(sem(A.tag + "_out_lo"), 4 * q + 4)
            unit(pe, U // 4, q, ps[0:2], XA, k0s[q], q == 0, q == 3)

        def next_unit(n, hi_):
            return {-2: 0, -1: 1, 1: 2, 2: 3}.get(n - hi_)

        def outputs_of(A, n, lo_, hi_):
            for lag in (5, 4):
                s = A.get(n - lag, lo_, hi_)
                if s and s["d"] is not None and (s["kind"] == "diff") == (lag == 5):
                    yield s

        def out_cols(s):
            return slice(256, 512) if s["kind"] == "diff" else slice(0, 256)

        def probs_free(eng, A, n):
            wait(eng, A.tag + "_probs_turned", A.d_before(n - 1))
            if n >= 1 and A.steps[n - 1]["half"] == 1:
                eng.wait_ge(sem(A.tag + "_probs"), n)

        def attn_act(act, A, lo_, hi_, U):
            T, nkt = A.tag, A.nkt
            for n in range(lo_, hi_ + 4):
                for s in outputs_of(A, n, lo_, hi_):
                    if s["kind"] == "diff":
                        act.wait_ge(sem("diff_turned"), s["head"] + 1)
                    else:
                        act.wait_ge(sem(T + "_out"), s["d"] + 1)
                    act.activation(A.X[0][:, srcs_of(s)["o"], :], ps[6 + s["d"] % 2][:, out_cols(s)],
                                   ACT.Copy).then_inc(sem(T + "_out_hi"), 1)
                s = A.get(n, lo_, hi_)
                if s and s["turn"]:
                    act.wait_ge(sem(T + "_qk_turned"), s["a"] + 1)
                    if s["a"] >= 2:
                        act.wait_ge(sem(T + "_scores"), A.last_step_of_turn(s["a"] - 2) + 1)
                    r = s["a"] % 2
                    act.activation(A.kT[:, r, 0:nkt * P], A.k_bank(s["a"]), ACT.Copy)
                    m = act.activation(A.qT[:, r, 0:SEQ], A.q_bank(s["a"])[:, 0:SEQ], ACT.Copy)
                    if s["kind"] == "mla":
                        m = act.activation(A.qT[0:64, r, 256:512], ps[1][0:64, 256:512], ACT.Copy)
                    m.then_inc(sem(T + "_qk_copied"), 1)
                s = A.get(n - 1, lo_, hi_)
                if s:
                    par = (n - 1) % 2
                    probs_free(act, A, n - 1)
                    act.wait_ge(sem(T + "_negmax"), n)
                    biased = s["kind"] in ("na", "moba", "fox")
                    for i in range(2):
                        src = A.pr[:, par, i, :] if biased else A.s_bank(n - 1, i)
                        scale = srcs_of(s)["scale"]
                        m = act.activation(A.pr[:, par, i, :], src, ACT.Exp, bias=stat(NM + 2 * par + i),
                                           scale=1.0 if s["kind"] == "na" else scale,
                                           accum_out=stat(SUM + 2 * par + i))
                    m.then_inc(sem(T + "_exp_done"), 1)
                s = A.get(n - 3, lo_, hi_)
                if s and s["d"] is not None and s["kind"] == "diff":
                    act.wait_ge(sem(T + "_out"), s["d"] + 1)
                    wait(act, "diff_normed", s["head"])
                    for i in range(2):
                        m = act.activation(od[:, s["head"] % 2, i, :], ps[6 + s["d"] % 2][:, i * P:i * P + P],
                                           ACT.Square, accum_out=stat(OSS + i))
                    m.then_inc(sem("diff_squares"), 1)
                q = next_unit(n, hi_)
                if q is not None:
                    hi(act, U // 4, q)

        def attn_dve(dve, A, lo_, hi_, U):
            T, nkt = A.tag, A.nkt
            w = nkt * P
            for n in range(lo_, hi_ + 4):
                s = A.get(n - 3, lo_, hi_)
                if s and s["d"] is not None:
                    d = s["d"]
                    dve.wait_ge(sem(T + "_probs_turned"), d + 1)
                    wait(dve, T + "_out", d - 1)
                    for i in range(2):
                        m = dve.tensor_copy(A.prT[:, d % 2, :, i * P:i * P + P],
                                            A.p_bank(d, i).rearrange("p (j t) -> p j t", j=nkt))
                    m.then_inc(sem(T + "_pt_copied"), 1)
                s = A.get(n - 2, lo_, hi_)
                if s:
                    par = (n - 2) % 2
                    dve.wait_ge(sem(T + "_exp_done"), n - 1)
                    dve.reciprocal(stat(RIN + 2 * par, 2), stat(SUM + 2 * par, 2))
                    dve.drain()
                    if s["half"] == 1:
                        dve.tensor_scalar(stat(RIN + 2 * par, 2), stat(RIN + 2 * par, 2), stat(LAM), None, ALU.mult)
                        dve.drain()
                    for i in range(2):
                        p = A.pr[:, par, i, :]
                        if s["half"] == 1:
                            m = dve.scalar_tensor_tensor(p, p, stat(RIN + 2 * par + i), A.pr[:, 1 - par, i, :],
                                                         ALU.mult, ALU.add)
                        else:
                            m = dve.tensor_scalar(p, p, stat(RIN + 2 * par + i), None, ALU.mult)
                    m.then_inc(sem(T + "_probs"), 1)
                for s in outputs_of(A, n, lo_, hi_):
                    dve.wait_ge(sem(T + "_out_hi"), s["d"] + 1)
                    o = srcs_of(s)["o"]
                    dve.tensor_tensor(A.X[1][:, o, :], ps[6 + s["d"] % 2][:, out_cols(s)],
                                      A.X[0][:, o, :].bitcast(F32), ALU.subtract).then_inc(sem(T + "_out_lo"), 1)
                s = A.get(n - 1, lo_, hi_)
                if s:
                    par = (n - 1) % 2
                    src = srcs_of(s)
                    dve.wait_ge(sem(T + "_scores"), n)
                    if s["kind"] in ("na", "moba", "fox"):
                        probs_free(dve, A, n - 1)
                        if s["kind"] == "na" and s["head"] == 0:
                            dve.wait_ge(sem("na_bias_loaded"), 16)
                        for i in range(2) if s["kind"] == "na" else ():
                            p = A.pr[:, par, i, :]
                            if s["kind"] == "na":
                                dve.scalar_tensor_tensor(p[:, 0:256], ps[2 + i][:, 0:256], src["scale"],
                                                         nabias[:, s["head"], i, :], ALU.mult, ALU.add)
                                dve.tensor_scalar(p[:, 256:512], ps[2 + i][:, 256:512], src["scale"], None, ALU.mult)
                        if s["kind"] != "na":
                            both = ps[2 + (n - 1) % 2][:, :].rearrange("p (i k) -> p i k", i=2)
                            if s["kind"] == "moba":
                                slope = 2.0 ** -(s["head"] + 1)
                                dve.scalar_tensor_tensor(A.pr[:, par], distm[:, :, :], -slope / src["scale"], both,
                                                         ALU.mult, ALU.add)
                            else:
                                dve.scalar_tensor_tensor(A.pr[:, par], causal[:, :, :], 1.0, both, ALU.mult, ALU.add)
                        dve.drain()
                    if A.wide():
                        for i in range(2):
                            x = A.pr[:, par, i, :] if s["kind"] == "na" else A.s_bank(n - 1, i)
                            dve.tensor_reduce(stat(MX + 2 * par + i), x, AX.X, ALU.max)
                    else:
                        dve.tensor_reduce(stat(MX + 2 * par, 2), A.pr[:, par], AX.X, ALU.max)
                    dve.drain()
                    dve.tensor_scalar(stat(NM + 2 * par, 2), stat(MX + 2 * par, 2),
                                      -1.0 if s["kind"] == "na" else -src["scale"], None,
                                      ALU.mult).then_inc(sem(T + "_negmax"), 1)
                s = A.get(n - 4, lo_, hi_)
                if s and s["d"] is not None:
                    if s["kind"] == "diff":
                        dve.wait_ge(sem("diff_rstd"), s["head"] + 1)
                        for i in range(2):
                            m = dve.scalar_tensor_tensor(od[:, s["head"] % 2, i, :],
                                                         ps[6 + s["d"] % 2][:, i * P:i * P + P], stat(ORS + i),
                                                         g_sub[:, :], ALU.mult, ALU.mult)
                        m.then_inc(sem("diff_normed"), 1)
                q = next_unit(n, hi_)
                if q is not None:
                    lo(dve, U // 4, q)

        A1 = Attn("att", STEPS, 4, kT, qT, probs, probsT, XA)
        A2 = Attn("att2", STEPS2, 2, kT2, qT2, probs2, probsT2, XB)

        def ffn_base(U, i, gated):
            per = 3 if gated else 2
            return U // 4 + (per - 1) + (i - 1) * per

        def ffn_pe(pe, T, U, n, gated, turn=lambda q: None):
            def body(i, head=True, tail=True):
                g0 = U // 4 if isinstance(i, int) and i == 0 else ffn_base(U, i, gated)
                k = 0
                first = isinstance(i, int) and i == 0
                if head and gated:
                    if not first:
                        wait(pe, T + "_gated", i)
                        for q in range(4):
                            unit(pe, g0, q, ps[0:2], XA, 4 * q, q == 0, q == 3)
                    k = 1
                for q in range(4):
                    if head and (gated or not first):
                        if q == 0:
                            wait(pe, T + "_act", i)
                        unit(pe, g0 + k, q, ps[2:4], XA, 4 * q, q == 0, q == 3)
                    if q == 1 and tail:
                        pe.wait_ge(sem(T + "_act"), i)
                        wait(pe, T + "_y", 4 * i - 4)
                        for tk in range(2):
                            for j in range(4):
                                m = pe.transpose(ps[4 + tk][:, j * P:j * P + P],
                                                 act_a[:, tk, j * P:j * P + P], ident[:, :])
                        m.then_inc(sem(T + "_turned"), 1)
                k += head
                if tail:
                    pe.wait_ge(sem(T + "_xlo"), i)
                    for q in range(4):
                        wait(pe, T + "_y", 4 * i - 4 + q - 1)
                        b = 6 if q % 2 == 0 else 4
                        unit(pe, g0 + k, q, ps[b:b + 2], XF, 0, True, True)
                        if not head:
                            turn(q)

            body(0, tail=False)
            body(1)
            with pe.Fori(2, n) as i:
                body(i)
            body_tail(pe, n, body, U, gated)

        def body_tail(eng, n, body, U, gated):
            body(n, head=False)

        def ffn_act(act, T, U, n, gated):
            def body(i, head=True, tail=True):
                g0 = U // 4 if isinstance(i, int) and i == 0 else ffn_base(U, i, gated)
                k = 0
                first = isinstance(i, int) and i == 0
                if head and gated:
                    if not first:
                        for q in range(4):
                            hi(act, g0, q)
                    k = 1
                up = head and (gated or not first)
                if up:
                    hi(act, g0 + k, 0)
                    hi(act, g0 + k, 1)
                if head and gated:
                    used(act, 4 * g0 + 4)
                    wait(act, T + "_act", i)
                    for tk in range(2):
                        m = act.activation(act_g[:, tk, :], ps[tk][:, :], ACT.Silu)
                    m.then_inc(sem(T + "_gated"), 1)
                if up:
                    hi(act, g0 + k, 2)
                if tail:
                    act.wait_ge(sem(T + "_turned"), i)
                    for tk in range(2):
                        m = act.activation(XF[0][:, :, tk * P:tk * P + P],
                                           ps[4 + tk][:, :].rearrange("p (j t) -> p j t", j=4), ACT.Copy)
                    m.then_inc(sem(T + "_xhi"), 1)
                if up:
                    hi(act, g0 + k, 3)
                k += head
                if tail:
                    hi(act, g0 + k, 0)
                    hi(act, g0 + k, 1)
                if head and not gated:
                    used(act, 4 * (g0 + k))
                    wait(act, T + "_act", i)
                    for tk in range(2):
                        m = act.activation(act_g[:, tk, :], ps[2 + tk][:, :], ACT.Relu, scale=stat(RSTD3 + tk))
                    m.then_inc(sem(T + "_gated"), 1)
                if tail:
                    hi(act, g0 + k, 2)
                    hi(act, g0 + k, 3)

            body(0, tail=False)
            body(1)
            with act.Fori(2, n) as i:
                body(i)
            body(n, head=False)

        def ffn_dve(dve, T, U, n, gated, finish, U_next):
            def add_y(i, q, g):
                used(dve, 4 * g + q + 1)
                b = 6 if q % 2 == 0 else 4
                for tk in range(2):
                    y = ybuf[:, tk, q * NCH:(q + 1) * NCH]
                    if isinstance(i, int) and i == 1:
                        m = dve.tensor_copy(y, ps[b + tk][:, :])
                    else:
                        m = dve.tensor_tensor(y, y, ps[b + tk][:, :], ALU.add)
                m.then_inc(sem(T + "_y"), 1)
                if isinstance(i, int) and i == n:
                    dve.drain()
                    finish(q)

            def body(i, head=True, tail=True, pending=True):
                g0 = U // 4 if isinstance(i, int) and i == 0 else ffn_base(U, i, gated)
                k = 0
                first = isinstance(i, int) and i == 0
                if head and gated:
                    if not first:
                        lo(dve, g0, 0)
                        lo(dve, g0, 1)
                        if pending:
                            add_y(i - 1, 3, g0 - 1)
                        lo(dve, g0, 2)
                        lo(dve, g0, 3)
                    k = 1
                up = head and (gated or not first)
                if up:
                    lo(dve, g0 + k, 0)
                    lo(dve, g0 + k, 1)
                if pending and not (head and gated):
                    add_y(i - 1, 3, g0 - 1)
                if up:
                    lo(dve, g0 + k, 2)
                if tail:
                    dve.wait_ge(sem(T + "_xhi"), i)
                    for tk in range(2):
                        m = dve.tensor_tensor(XF[1][:, :, tk * P:tk * P + P],
                                              ps[4 + tk][:, :].rearrange("p (j t) -> p j t", j=4),
                                              XF[0][:, :, tk * P:tk * P + P].bitcast(F32), ALU.subtract)
                    m.then_inc(sem(T + "_xlo"), 1)
                if up:
                    lo(dve, g0 + k, 3)
                k += head
                if tail:
                    lo(dve, g0 + k, 0)
                    lo(dve, g0 + k, 1)
                    if not head:
                        lo(dve, g0 + k, 2)
                    add_y(i, 0, g0 + k)
                if head:
                    dve.wait_ge(sem(T + "_gated"), i + 1)
                    if gated:
                        used(dve, 4 * (g0 + k))
                    if tail:
                        dve.wait_ge(sem(T + "_turned"), i)
                    for tk in range(2):
                        m = dve.tensor_tensor(act_a[:, tk, :], act_g[:, tk, :],
                                              ps[2 + tk][:, :] if gated else act_g[:, tk, :], ALU.mult)
                    m.then_inc(sem(T + "_act"), 1)
                if tail:
                    for q in (2, 3):
                        if head or q == 3:
                            lo(dve, g0 + k, q)
                        add_y(i, q - 1, g0 + k)

            body(0, tail=False, pending=False)
            body(1, pending=False)
            body(2)
            with dve.Fori(3, n) as i:
                body(i)
            body(n, head=False)
            if U_next is not None:
                lo(dve, U_next // 4, 0)
                turn_dve(dve, "h3", 0)
            add_y(n, 3, ffn_base(U, n, gated))

        def ffn_sp(sp, U, n, gated, gate_v, up_v, down_flat):
            def body(i, head=True, tail=True):
                g0 = U // 4 if isinstance(i, int) and i == 0 else ffn_base(U, i, gated)
                k = 0
                for v in ([gate_v, up_v] if gated else [up_v]) if head else []:
                    for q in range(4):
                        load(sp, g0 + k, q, at_col(v[:, q], i * NCH))
                    k += 1
                if tail:
                    for q in range(4):
                        v = down_flat[:, :, q * NCH:(q + 1) * NCH]
                        if isinstance(i, int):
                            load(sp, g0 + k, q, v[:, (i - 1) * KQ:i * KQ, :])
                        else:
                            load(sp, g0 + k, q, (v, i * KQ - KQ, "k"))

            body(0, tail=False)
            body(1)
            with sp.Fori(2, n) as i:
                body(i)
            body(n, head=False)

        wd_k = t["ffn_wd"][0].rearrange("(k p) n -> p k n", p=P)
        w_down_k = t["w_down_2"].rearrange("(k p) n -> p k n", p=P)

        IN_ORDER, BY_HEADS = (0, 1, 2, 3), (2, 3, 1, 0)
        def out_sp(sp, U, v, order):
            for c in range(4):
                for q in range(4):
                    load(sp, U // 4 + c, q, v[:, order[q], :, c * NCH:(c + 1) * NCH])

        def out_pe(pe, T, U, X, order, turn=lambda c: None):
            for c in range(1, 4):
                wait(pe, T, c - 1)
                for q in range(4):
                    unit(pe, U // 4 + c, q, ps[2 * (c % 2):2 * (c % 2) + 2], X, 4 * order[q], q == 0, q == 3)
                    if q == 2:
                        turn(c - 1)

        def out_act(act, U, T, U_next, x, turn=lambda c: None):
            for c in range(1, 4):
                for q in range(4):
                    hi(act, U // 4 + c, q)
                squares_of(act, T, c - 1, T + "_chunk", x, SQ1)
                turn(c - 1)
            hi(act, U_next // 4, 0)
            hi(act, U_next // 4, 1)
            squares_of(act, T, 3, T + "_chunk", x, SQ1)

        def out_dve(dve, T, U, U_next, ready, add, turn=lambda c: None):
            for c in range(1, 4):
                lo(dve, U // 4 + c, 0)
                lo(dve, U // 4 + c, 1)
                if c == 1:
                    ready()
                used(dve, U + 4 * c)
                add(c - 1, [ps[2 * ((c - 1) % 2) + tk][:, :] for tk in range(2)])
                lo(dve, U // 4 + c, 2)
                lo(dve, U // 4 + c, 3)
                turn(c - 1)
            lo(dve, U_next // 4, 0)
            used(dve, U + 16)
            add(3, [ps[2 + tk][:, :] for tk in range(2)])
            lo(dve, U_next // 4, 1)
            sum_squares(dve, T, 4, [(SQ1, SS)])

        def rstd_pool(pool, T, tiles, done, col=RSTD):
            pool.wait_ge(sem(T + done), 1)
            pool_rstd(pool, stat(col, tiles), stat(SS, tiles), tiles, D).then_inc(sem(T + "_rstd"), 1)

        block = ctx.enter_context(nc.Block())

        @block.sync
        def _(sp):
            sp.dma_start(crow[0:16, :], t["c"].rearrange("a (k p) -> (a k) p", p=P)).then_inc(sem("c_loaded"), 16)
            sp.dma_start(crow[16:32, :], t["c_ctx"].rearrange("(k p) -> k p", p=P)).then_inc(sem("c_loaded"), 16)
            sp.dma_start(ident[:, :], t["identity"]).then_inc(sem("ident_loaded"), 16)
            sp.dma_start(spread[:, :, :], t["row_spread"]).then_inc(sem("ident_loaded"), 16)

            for i in range(4):
                sp.dma_start(xin[:, i, :], (x_v, ctx_v)[i // 2][:, i % 2, :]).then_inc(sem(f"x_loaded{i // 2}"), 16)

            def ada_cols(c):
                col = (c * NCH + D) % (2 * D) if c < N_ADA_1 else c * NCH
                return slice(col, col + NCH)

            def b_piece(c):
                wait(sp, "ada_combined", c - 1)
                sp.dma_start(rows_of(c % 2)[4:5, :], t["b_ada"][:, ada_cols(c)]).then_inc(sem(f"b_loaded{c % 2}"), 16)

            for c in range(N_ADA_1):
                for q in range(4):
                    load(sp, c, q, w_ada_v[:, q, :, ada_cols(c)])
                b_piece(c)

            def late_b_piece(c):
                wait(sp, "mod_row", c - 1)
                sp.dma_start(late_b[c % 2][:, :], t["b_ada"][:, ada_cols(c)]).then_inc(sem(f"b_loaded{c % 2}"), 16)

            def store(c):
                sp.wait_ge(sem("mod_row"), c + 1)
                sp.dma_start(mod_d[:, c * NCH - 2 * D:(c + 1) * NCH - 2 * D], late_row(c % 2))\
                    .then_inc(sem(f"late_mod_stored{c % 2}"), 16)
                if c + 2 < N_ADA:
                    late_b_piece(c + 2)
            stored = N_ADA_1
            for n, (kind, c, k) in enumerate(MIX):
                u = U_MIX + n
                if kind == "ada":
                    load(sp, u // 4, u % 4, w_ada_v[:, k, :, ada_cols(c)])
                else:
                    col, w, _ = WIN[c]
                    load(sp, u // 4, u % 4, w_in_v[:, k, :, col:col + w], w=w)
                if n == 3:
                    late_b_piece(N_ADA_1)
                    late_b_piece(N_ADA_1 + 1)
                if stored < N_ADA and ADD_UP[stored] + 1 < len(W) and n == W[ADD_UP[stored] + 1] + 4:
                    store(stored)
                    stored += 1
            load(sp, U_MLA // 4, 0, wuq_v[:, :, 0:512])
            load(sp, U_MLA // 4, 1, wuq_v[:, :, 512:768], w=256)
            load(sp, U_MLA // 4, 2, wukv_v[:, :, 0:512], k=2)
            load(sp, U_MLA // 4, 3, wukv_v[:, :, 512:1024], k=2)
            for c in range(stored, N_ADA):
                store(c)
            out_sp(sp, U_OUT, w_out_v, BY_HEADS)
            ffn_sp(sp, U_FFN, N_FF, True, wg_v, wu_v, wd_k)

            def qkv2(i):
                for b in range(2):
                    for q in range(4):
                        load(sp, U_WIN2 // 4 + 2 * i + b, q, at_col(w_in2_v[:, q], i * (2 * NCH) + b * NCH))
            with sp.Fori(0, N_QKV2 // 2) as i:
                qkv2(i)

            def merge(n):
                for b, first in enumerate((6152, 8200)):
                    for q in range(4):
                        load(sp, U_MRG // 4 + 3 * n + b, q, at_col(w_in2_v[:, q], n * NCH + first))
                for q in range(4):
                    v = wpa_v if q < 2 else wpb_v
                    load(sp, U_MRG // 4 + 3 * n + 2, q, at_col(v[:, q % 2], n * NCH))
            for n in range(4):
                merge(n)
            out_sp(sp, U_OUT2, w_out2_v, IN_ORDER)
            ffn_sp(sp, U_FFN2, N_FF2, False, None, w_up_v, w_down_k)
            for q in range(4):
                sp.wait_ge(sem("out_ready"), q + 1)
                cc = slice(q * NCH, (q + 1) * NCH)
                sp.dma_start(out_v[:, :, cc], ybuf[:, :, cc]).then_inc(sem("stored"), 16)
            sp.wait_ge(sem("stored"), 64)

        @block.scalar
        def _(act):
            act.wait_ge(sem("c_loaded"), 32)
            act.activation(csig[:, :], crow[:, :], ACT.Silu).then_inc(sem("c_silu"), 1)
            act.wait_ge(sem("c_turned"), 1)
            for v in range(2):
                m = act.activation(cst[:, :, 2 * v], ccol[:, 16 * v:16 * v + 16], ACT.Copy)
            m.then_inc(sem("c_hi"), 1)

            for i in range(4):
                act.wait_ge(sem(f"x_loaded{i // 2}"), 32)
                act.drain()
                m = act.activation(junk[:, :], xin[:, i, :], ACT.Square, accum_out=stat(SS + i))
            m.then_inc(sem("x_squares"), 1)

            def copy_rows(c, b, units, bank):
                used(act, units)
                wait(act, "ada_combined", c - 1)
                act.activation(rows_of(b)[0:4, :], ps[bank][0:4, :], ACT.Copy).then_inc(sem("ada_rows"), 1)

            for c in range(N_ADA_1):
                hi(act, c, 0)
                hi(act, c, 1)
                if c:
                    copy_rows(c - 1, (c - 1) % 2, 4 * c, 2 + (c - 1) % 2)
                hi(act, c, 2)
                hi(act, c, 3)
                if c == 0:
                    act.wait_ge(sem("na_tables_loaded"), 160)
                    act.activation(bandr[:, :], band[:, :], ACT.Copy)
                    act.activation(narpbr[:, :], narpb[:, :], ACT.Copy).then_inc(sem("na_rpb_hi"), 1)
                    act.wait_ge(sem("x_rstd"), 1)
                    for i in range(4):
                        m = act.activation(xin[:, i, :], xin[:, i, :], ACT.Copy, scale=stat(RSTD + i))
                    m.then_inc(sem("x_scaled"), 1)
                if c >= 5:
                    turn_h_act(act, c - 5)

            def win_copy(c):
                col, w, cx = WIN[c]
                used(act, U_MIX + LAST["win", c] + 1)
                b = 4 * (c % 2)
                if c == len(WIN) - 1:
                    act.wait_ge(sem("ada_combined"), N_ADA)
                    for i in range(2):
                        act.wait_ge(sem(f"late_mod_stored{i}"), 8 * (N_ADA - N_ADA_1))
                m = act.activation(PL[:, 0, col:col + w], ps[b][:, 0:w], ACT.Copy)
                if cx is not None:
                    m = act.activation(PC[:, 0, cx:cx + w], ps[b + 2][:, 0:w], ACT.Copy)
                m.then_inc(sem("win_copied_a"), 1)
                if c in WIN_SQ:
                    first, width, n, tiles = WIN_SQ[c]
                    act.wait_ge(sem("win_copied_d"), c + 1)
                    for i in range(tiles):
                        for h in range(n):
                            act.drain()
                            src = PL[:, i, col + h * width:col + (h + 1) * width] if i < 2 else \
                                PC[:, i - 2, cx + h * width:cx + (h + 1) * width]
                            m = act.activation(psq[:, 0:width], src, ACT.Square, accum_out=stat(first + n * i + h))
                    m.then_inc(sem("win_squared"), 1)
            def slot_before(i):
                return U_MIX + (W[i - 2] if i >= 2 else i - 2)
            for i, n in enumerate(W):
                u, c = U_MIX + n, MIX[n][1]
                if i >= 2 and MIX[W[i - 2]][2] == 3:
                    win_copy(MIX[W[i - 2]][1])
                hi(act, u // 4, u % 4, w=WIN[c][1], slot=i % 2, before=slot_before(i), follow=FOLLOW[i])
                if i == 0:
                    copy_rows(N_ADA_1 - 1, 1, U_MIX, 3)
                    turn_h_act(act, 3)
            hi(act, U_MLA // 4, 0)
            win_copy(len(WIN) - 1)
            hi(act, U_MLA // 4, 1, w=256)

            act.wait_ge(sem("mla_turned"), 1)
            for i in range(2):
                act.activation(XQ[0][:, :, i * P:i * P + P], ps[i][:, :].rearrange("p (j t) -> p j t", j=4), ACT.Copy)
            for i in range(4):
                m = act.activation(XKV[0][:, :, i * P:i * P + P],
                                   ps[2 + i // 2][:, (i % 2) * 256:(i % 2) * 256 + 256].rearrange("p (j t) -> p j t", j=2),
                                   ACT.Copy)
            m.then_inc(sem("mla_hi"), 1)
            act.activation(kpeT[:, :], ps[4][0:64, :], ACT.Copy).then_inc(sem("kpe_copied"), 1)
            hi(act, U_MLA // 4, 2, k=2)
            hi(act, U_MLA // 4, 3, k=2)
            used(act, U_MLA + 1)
            act.activation(PL[:, 0, ML_Q:ML_Q + 512], ps[0][:, :], ACT.Copy)
            used(act, U_MLA + 2)
            act.activation(PL[:, 0, ML_Q + 512:ML_Q + 768], ps[2][:, 0:256], ACT.Copy).then_inc(sem("mla_copied_a"), 1)
            used(act, U_MLA + 3)
            for i in (0, 1):
                m = act.activation(mkv[:, i, 0:512], ps[4 + i][:, :], ACT.Copy)
            used(act, U_MLA + 4)
            for i in (0, 1):
                m = act.activation(mkv[:, i, 512:1024], ps[i][:, :], ACT.Copy)
            m.then_inc(sem("mla_copied_a"), 1)
            act.wait_ge(sem("lam_dots"), 1)
            act.activation(stat(LAMW, 2), stat(LAMW, 2), ACT.Exp).then_inc(sem("lam_exp"), 1)

            act.wait_ge(sem("rotated_pe"), 1)
            attn_act(act, A1, 0, len(STEPS), U_OUT)
            out_act(act, U_OUT, "x1", U_FFN, x_one)

            start_act(act, "h2", U_FFN)
            ffn_act(act, "ff1", U_FFN, N_FF, True)

            def squares_2(c):
                squares_of(act, "xf", c, "xf_chunk", x_one, SQ1)
                squares_of(act, "xf", c, "xg_chunk", ybuf, SQ2)
            hi(act, U_WIN2 // 4, 0)
            turn_act(act, "h3", 0)
            squares_2(0)
            hi(act, U_WIN2 // 4, 1)
            turn_act(act, "h3", 1)
            squares_2(1)
            hi(act, U_WIN2 // 4, 2)
            turn_act(act, "h3", 2)
            squares_2(2)
            hi(act, U_WIN2 // 4, 3)
            turn_act(act, "h3", 3)
            squares_2(3)
            act.wait_ge(sem("wf_loaded"), 32)
            act.activation(wfh[:, :, :], wf[:, :, :], ACT.Copy).then_inc(sem("wf_hi"), 1)

            def qkv2(i, first=False):
                for b in range(2):
                    g = U_WIN2 // 4 + 2 * i + b
                    if first and b == 0:
                        continue
                    hi(act, g, 0)
                    hi(act, g, 1)
                    qkv2_copy(i * 2 + (b - 1), 1 - b)
                    hi(act, g, 2)
                    hi(act, g, 3)

            def qkv2_copy(c, b):
                used(act, c * 4 + (U_WIN2 + 4))
                act.activation(P2[:, 0, bass.ds(c * NCH, NCH)], ps[2 * b][:, :], ACT.Copy,
                               scale=stat(RSTD)).then_inc(sem("qkv2_a"), 1)
            act.wait_ge(sem("xf_rstd"), 1)
            qkv2(0, True)
            with act.Fori(1, N_QKV2 // 2) as i:
                qkv2(i)
            qkv2_copy(N_QKV2 - 1, 1)
            act.wait_ge(sem("fz_abs"), 1)
            act.activation(fz[:, 2], fz[:, 1], ACT.Exp, scale=-1.0).then_inc(sem("fz_exp"), 1)
            act.wait_ge(sem("fz_one"), 1)
            act.activation(fz[:, 4], fz[:, 3], ACT.Ln).then_inc(sem("fz_log"), 1)
            act.wait_ge(sem("x2_stored"), 16)
            attn_act(act, A2, 0, len(STEPS2), U_MRG)

            def sigm(n, b):
                used(act, n * 12 + (U_MRG + 4 * b + 4))
                wait(act, "merged_chunk", n)
                for tk in range(2):
                    m = act.activation(sig[:, 2 * b + tk, :], ps[2 * b + tk][:, :], ACT.Sigmoid,
                                       scale=stat(RSTD + tk))
                m.then_inc(sem("gate_sigmoid"), 1)

            def merge(n, first=False):
                g = 3 * n + U_MRG // 4
                for q in () if first else range(4):
                    hi(act, g, q)
                hi(act, g + 1, 0)
                hi(act, g + 1, 1)
                sigm(n, 0)
                hi(act, g + 1, 2)
                hi(act, g + 1, 3)
                hi(act, g + 2, 0)
                hi(act, g + 2, 1)
                sigm(n, 1)
                hi(act, g + 2, 2)
                hi(act, g + 2, 3)
            merge(0, True)
            with act.Fori(1, 4) as n:
                merge(n)
            hi(act, U_OUT2 // 4, 0)
            hi(act, U_OUT2 // 4, 1)
            start_act(act, "mrg", U_OUT2)
            out_act(act, U_OUT2, "x3", U_FFN2, xres, lambda c: turn_act(act, "h4", c))
            hi(act, U_FFN2 // 4, 2)
            turn_act(act, "h4", 3)
            hi(act, U_FFN2 // 4, 3)
            act.wait_ge(sem("x3_rstd"), 1)
            ffn_act(act, "ff2", U_FFN2, N_FF2, False)
            for c in range(4):
                squares_of(act, "x4", c, "x4_chunk", xres, SQ1)

        @block.vector
        def _(dve):
            dve.memset(pstat[:, 16:24], -0.5).then_inc(sem("memsets"), 1)
            dve.memset(narpb[:, :], 0.0).then_inc(sem("memsets"), 1)
            dve.memset(ones[:, :], 1.0).then_inc(sem("memsets"), 1)
            dve.wait_ge(sem("c_cols"), 1)
            dve.tensor_copy(ccol[:, :], ps[7][:, 0:32]).then_inc(sem("c_turned"), 1)
            dve.wait_ge(sem("c_hi"), 1)
            for v in range(2):
                m = dve.tensor_tensor(cst[:, :, 2 * v + 1], ccol[:, 16 * v:16 * v + 16],
                                      cst[:, :, 2 * v].bitcast(F32), ALU.subtract)
            m.then_inc(sem("c_lo"), 1)

            def make_na_bias():
                dve.wait_ge(sem("na_tables_loaded"), 160)
                dve.wait_ge(sem("na_bands"), 1)
                for i in range(2):
                    for half in range(2):
                        pp = slice(64 * half, 64 * half + 64)
                        d0 = 3 - (2 * i + half)
                        for jb in range(4):
                            bands = ps[4 + jb][pp, 0:448].rearrange("p (j h d) -> p h d j", h=4, d=7)[:, :, d0:d0 + 4, :]
                            mask = namask[pp, jb * 16:jb * 16 + 16].rearrange("p (a b j) -> p a b j", a=1, b=1)
                            m = dve.tensor_tensor(
                                nab_1[pp, :, i, :].rearrange("p h (k j) -> p h k j", k=4)[:, :, :, jb * 16:jb * 16 + 16],
                                bands, mask.to_broadcast([64, 4, 4, 16]), ALU.add)
                m.then_inc(sem("na_bias_made"), 1)

            def take(c):
                q = c % 4
                cc = slice(q * NCH, (q + 1) * NCH)
                dve.wait_ge(sem("ada_combined"), c + 1)
                if c == 0:
                    dve.wait_ge(sem("g_attn_loaded"), 16)
                if c == 4:
                    dve.wait_ge(sem("x_modulated"), 4)
                if c < 4:
                    wait(dve, "x_modulated", c)
                    for v in range(2):
                        m = dve.scalar_tensor_tensor(scale_g[:, v, :], ps[v][:, :], 1.0, gvec[:, cc], ALU.add, ALU.mult)
                    m.then_inc(sem("mod_row"), 1)
                else:
                    for i in range(4):
                        dve.tensor_tensor(xin[:, i, cc], xin[:, i, cc], ps[i // 2][:, :], ALU.add)\
                            .then_inc(sem("h_ready"), 1)
                    dve.drain().then_inc(sem("mod_row"), 1)

            def multiply(n):
                _, c, k = MIX[n]
                u = U_MIX + n
                acc = late_sums(c % 2)
                dve.wait_ge(sem(f"landed{u % 4}"), 16 * (u // 4) + 16)
                if k == 0 and c >= N_ADA_1 + 2:
                    dve.wait_ge(sem("ada_combined"), c - 1)
                for j in range(KQ):
                    w, cj = raw[:, u % 4, j, :], ccol[:, 4 * k + j:4 * k + j + 1]
                    if k == 0 and j == 0:
                        m = dve.tensor_scalar(acc, w, cj, None, ALU.mult)
                    else:
                        dve.drain()
                        m = dve.scalar_tensor_tensor(acc, w, cj, acc, ALU.mult, ALU.add)
                m.then_inc(sem("lo_made"), 2)
                if k == 3:
                    dve.drain().then_inc(sem("late_summed"), 1)

            def move_row(c):
                b = c % 2
                dve.wait_ge(sem("ada_combined"), c + 1)
                dve.wait_ge(sem(f"b_loaded{b}"), 8 * (c - b) + 16)
                wait(dve, f"late_mod_stored{b}", 16 * ((c - N_ADA_1) // 2))
                dve.tensor_tensor(late_row(b), ps[sum_bank(c)][0:1, :], late_b[b][:, :], ALU.add)\
                    .then_inc(sem("mod_row"), 1)

            for c in range(N_ADA_1):
                lo(dve, c, 0)
                lo(dve, c, 1)
                lo(dve, c, 2)
                if c:
                    take(c - 1)
                lo(dve, c, 3)
                if c == 0:
                    dve.wait_ge(sem("na_rpb_hi"), 1)
                    dve.tensor_tensor(narpbr[32:63, :], narpb[32:63, :], narpbr[32:63, :].bitcast(F32),
                                      ALU.subtract).then_inc(sem("na_rpb_lo"), 1)
                if c == 1:
                    make_na_bias()
                if c >= 5:
                    turn_h_dve(dve, c - 5)

            def win_copy(c):
                col, w, cx = WIN[c]
                used(dve, U_MIX + LAST["win", c] + 1)
                b = 4 * (c % 2)
                if c == len(WIN) - 1:
                    dve.wait_ge(sem("ada_combined"), N_ADA)
                    for i in range(2):
                        dve.wait_ge(sem(f"late_mod_stored{i}"), 8 * (N_ADA - N_ADA_1))
                m = dve.tensor_copy(PL[:, 1, col:col + w], ps[b + 1][:, 0:w])
                if cx is not None:
                    m = dve.tensor_copy(PC[:, 1, cx:cx + w], ps[b + 3][:, 0:w])
                m.then_inc(sem("win_copied_d"), 1)
            moved = N_ADA_1
            for i, n in enumerate(W):
                u, c = U_MIX + n, MIX[n][1]
                if i >= 2 and MIX[W[i - 2]][2] == 3:
                    win_copy(MIX[W[i - 2]][1])
                while moved < N_ADA and ADD_UP[moved] + 1 <= i:
                    move_row(moved)
                    moved += 1
                lo(dve, u // 4, u % 4, w=WIN[c][1], slot=i % 2)
                if i == 0:
                    take(N_ADA_1 - 1)
                    turn_h_dve(dve, 3)
                for k in range(FOLLOW[i]):
                    multiply(n + 1 + k)
            for c in range(moved, N_ADA):
                move_row(c)
            lo(dve, U_MLA // 4, 0)
            win_copy(len(WIN) - 1)
            lo(dve, U_MLA // 4, 1, w=256)
            dve.wait_ge(sem("mla_hi"), 1)
            for i in range(2):
                dve.tensor_tensor(XQ[1][:, :, i * P:i * P + P], ps[i][:, :].rearrange("p (j t) -> p j t", j=4),
                                  XQ[0][:, :, i * P:i * P + P].bitcast(F32), ALU.subtract)
            for i in range(4):
                m = dve.tensor_tensor(XKV[1][:, :, i * P:i * P + P],
                                      ps[2 + i // 2][:, (i % 2) * 256:(i % 2) * 256 + 256].rearrange("p (j t) -> p j t", j=2),
                                      XKV[0][:, :, i * P:i * P + P].bitcast(F32), ALU.subtract)
            m.then_inc(sem("mla_lo"), 1)
            lo(dve, U_MLA // 4, 2, k=2)
            lo(dve, U_MLA // 4, 3, k=2)
            used(dve, U_MLA + 1)
            dve.tensor_copy(PL[:, 1, ML_Q:ML_Q + 512], ps[1][:, :])
            used(dve, U_MLA + 2)
            dve.tensor_copy(PL[:, 1, ML_Q + 512:ML_Q + 768], ps[3][:, 0:256]).then_inc(sem("mla_copied_d"), 1)
            used(dve, U_MLA + 3)
            for i in (2, 3):
                m = dve.tensor_copy(mkv[:, i, 0:512], ps[4 + i][:, :])
            used(dve, U_MLA + 4)
            for i in (2, 3):
                m = dve.tensor_copy(mkv[:, i, 512:1024], ps[i][:, :])
            m.then_inc(sem("mla_copied_d"), 1)

            dve.wait_ge(sem("small_loaded"), 16 * 13)
            for v in range(2):
                dve.tensor_tensor(lamv[:, 2 * v, :], lamv[:, 2 * v, :], lamv[:, 2 * v + 1, :], ALU.mult)
                dve.drain()
                dve.tensor_reduce(stat(LAMW + v), lamv[:, 2 * v, :], AX.X, ALU.add)
            dve.drain().then_inc(sem("lam_dots"), 1)
            dve.wait_ge(sem("lam_exp"), 1)
            dve.tensor_tensor(stat(LAM), stat(LAMW + 1), stat(LAMW), ALU.subtract)
            dve.drain()
            dve.tensor_scalar(stat(LAM), stat(LAM), -LAM0, None, ALU.add)
            dve.tensor_scalar(g_sub[:, :], g_sub[:, :], 1.0 - LAM0, None, ALU.mult).then_inc(sem("lam_used"), 1)
            dve.drain()

            attn_dve(dve, A1, 0, len(STEPS), U_OUT)
            def x1_ready():
                dve.wait_ge(sem("x1_loaded"), 64)
                dve.scalar_tensor_tensor(sc_f[:, :], sc_f[:, :], 1.0, gvec[:, :], ALU.add, ALU.mult)
                dve.drain()

            def add_1(c, src):
                cc = slice(c * NCH, (c + 1) * NCH)
                for tk in range(2):
                    dve.tensor_tensor(tmp[:, tk, :], src[tk], gt_a[:, cc], ALU.mult)
                dve.drain()
                for tk in range(2):
                    m = dve.tensor_tensor(x_one[:, tk, cc], x_one[:, tk, cc], tmp[:, tk, :], ALU.add)
                m.then_inc(sem("x1_chunk"), 1)
                dve.drain()
                for tk in range(2):
                    dve.tensor_tensor(ybuf[:, tk, cc], x_one[:, tk, cc], sc_f[:, cc], ALU.mult)
            out_dve(dve, "x1", U_OUT, U_FFN, x1_ready, add_1)

            def make_h2(q):
                cc = slice(q * NCH, (q + 1) * NCH)
                for i in range(2):
                    dve.scalar_tensor_tensor(ybuf[:, i, cc], ybuf[:, i, cc], stat(RSTD + i), sh_f[:, cc], ALU.mult,
                                             ALU.add).then_inc(sem("h2_ready"), 1)
            dve.wait_ge(sem("x1_gates_loaded"), 32)
            dve.wait_ge(sem("x1_rstd"), 1)
            start_dve(dve, "h2", U_FFN, make_h2)

            def finish_1(q):
                cc = slice(q * NCH, (q + 1) * NCH)
                for i in range(2):
                    m = dve.tensor_tensor(ybuf[:, i, cc], ybuf[:, i, cc], gt_f[:, cc], ALU.mult)
                m.then_inc(sem("y_gated"), 1)
            ffn_dve(dve, "ff1", U_FFN, N_FF, True, finish_1, U_WIN2)
            lo(dve, U_WIN2 // 4, 1)
            turn_dve(dve, "h3", 1)
            lo(dve, U_WIN2 // 4, 2)
            turn_dve(dve, "h3", 2)
            lo(dve, U_WIN2 // 4, 3)
            turn_dve(dve, "h3", 3)
            sum_squares(dve, "xf", 8, [(SQ1, SS), (SQ2, SS + 2)])
            dve.wait_ge(sem("wf_hi"), 1)
            dve.tensor_tensor(wfl[:, :, :], wf[:, :, :], wfh[:, :, :].bitcast(F32), ALU.subtract).then_inc(sem("wf_lo"), 1)
            def qkv2_copy(c, b):
                used(dve, c * 4 + (U_WIN2 + 4))
                dve.tensor_scalar(P2[:, 1, bass.ds(c * NCH, NCH)], ps[2 * b + 1][:, :], stat(RSTD + 1), None,
                                  ALU.mult).then_inc(sem("qkv2_d"), 1)

            def qkv2(i, first=False):
                for b in range(2):
                    g = U_WIN2 // 4 + 2 * i + b
                    if first and b == 0:
                        continue
                    lo(dve, g, 0)
                    lo(dve, g, 1)
                    if first:
                        dve.wait_ge(sem("f_acc"), 1)
                        dve.tensor_copy(zT[:, :], ps[4][0:8, 0:SEQ]).then_inc(sem("z_copied"), 1)
                    qkv2_copy(i * 2 + (b - 1), 1 - b)
                    lo(dve, g, 2)
                    lo(dve, g, 3)
            dve.wait_ge(sem("x2_made"), 1)
            qkv2(0, True)
            dve.wait_ge(sem("z_turned"), 1)
            for i in range(2):
                dve.scalar_tensor_tensor(fz[:, 0, i], ps[5][:, 8 * i:8 * i + 8], stat(RSTD + i), bf[:, :],
                                         ALU.mult, ALU.add)
            dve.drain()
            dve.scalar_tensor_tensor(fz[:, 1], fz[:, 0], -1.0, fz[:, 0], ALU.mult, ALU.max)
            dve.tensor_scalar(fz[:, 5], fz[:, 0], 0.0, None, ALU.min)
            dve.drain().then_inc(sem("fz_abs"), 1)
            with dve.Fori(1, N_QKV2 // 2) as i:
                qkv2(i)
            qkv2_copy(N_QKV2 - 1, 1)
            dve.wait_ge(sem("fz_exp"), 1)
            dve.tensor_scalar(fz[:, 3], fz[:, 2], 1.0, None, ALU.add).then_inc(sem("fz_one"), 1)
            dve.wait_ge(sem("fz_log"), 1)
            dve.tensor_tensor(fz[:, 4], fz[:, 4], fz[:, 5], ALU.subtract)
            dve.drain()
            dve.tensor_scalar(nlf[:, :, :], fz[:, 4], float(HD) ** 0.5, None, ALU.mult).then_inc(sem("nlf_made"), 1)
            dve.wait_ge(sem("masks_loaded"), 48)
            dve.wait_ge(sem("x2_stored"), 16)
            attn_dve(dve, A2, 0, len(STEPS2), U_MRG)

            def gate_mul(n):
                cc = bass.ds(n * NCH, NCH)
                used(dve, n * 12 + (U_MRG + 12))
                dve.wait_ge(sem("gate_sigmoid"), n * 2 + 2)
                for s in range(4):
                    dve.tensor_tensor(sig[:, s, :], sig[:, s, :], ps[4 + s][:, :], ALU.mult)
                dve.drain()
                for tk in range(2):
                    m = dve.tensor_tensor(mrg[:, tk, cc], sig[:, tk, :], sig[:, 2 + tk, :], ALU.add)
                m.then_inc(sem("merged_chunk"), 1)

            def merge(n, first=False):
                g = 3 * n + U_MRG // 4
                if not first:
                    lo(dve, g, 0)
                    lo(dve, g, 1)
                    gate_mul(n - 1)
                    lo(dve, g, 2)
                    lo(dve, g, 3)
                for q in range(4):
                    lo(dve, g + 1, q)
                for q in range(4):
                    lo(dve, g + 2, q)
            merge(0, True)
            with dve.Fori(1, 4) as n:
                merge(n)
            lo(dve, U_OUT2 // 4, 0)
            lo(dve, U_OUT2 // 4, 1)
            start_dve(dve, "mrg", U_OUT2, lambda g: gate_mul(3) if g == 2 else None)

            def add_2(c, src):
                cc = slice(c * NCH, (c + 1) * NCH)
                for tk in range(2):
                    m = dve.tensor_tensor(xres[:, tk, cc], xres[:, tk, cc], src[tk], ALU.add)
                m.then_inc(sem("x3_chunk"), 1)
                dve.drain()
                for tk in range(2):
                    dve.tensor_tensor(ybuf[:, tk, cc], xres[:, tk, cc], gvec[:, cc], ALU.mult)\
                        .then_inc(sem("h4_ready"), 1)

            def x3_ready():
                dve.wait_ge(sem("x3_loaded"), 16)
                dve.wait_ge(sem("g_mlp_loaded"), 16)
            out_dve(dve, "x3", U_OUT2, U_FFN2, x3_ready, add_2, lambda c: turn_dve(dve, "h4", c))
            lo(dve, U_FFN2 // 4, 2)
            turn_dve(dve, "h4", 3)
            lo(dve, U_FFN2 // 4, 3)

            def finish_2(q):
                cc = slice(q * NCH, (q + 1) * NCH)
                for i in range(2):
                    m = dve.tensor_tensor(xres[:, i, cc], xres[:, i, cc], ybuf[:, i, cc], ALU.add)
                m.then_inc(sem("x4_chunk"), 1)
            ffn_dve(dve, "ff2", U_FFN2, N_FF2, False, finish_2, None)
            sum_squares(dve, "x4", 4, [(SQ1, SS)])
            dve.wait_ge(sem("g_final_loaded"), 16)
            dve.wait_ge(sem("x4_rstd"), 1)
            for q in range(4):
                cc = slice(q * NCH, (q + 1) * NCH)
                for i in range(2):
                    m = dve.scalar_tensor_tensor(ybuf[:, i, cc], xres[:, i, cc], stat(RSTD + i), gvec[:, cc],
                                                 ALU.mult, ALU.mult)
                m.then_inc(sem("out_ready"), 1)

        @block.tensor
        def _(pe):
            pe.wait_ge(sem("ident_loaded"), 32)
            pe.wait_ge(sem("c_silu"), 1)
            pe.transpose(ps[7][:, 0:32], csig[:, :], ident[0:32, 0:32]).then_inc(sem("c_cols"), 1)
            pe.wait_ge(sem("c_lo"), 1)

            def rows_complete(c, b):
                pe.wait_ge(sem("ada_rows"), c + 1)
                pe.wait_ge(sem(f"b_loaded{b}"), 8 * (c - b) + 16)

            def add_up(c):
                pe.wait_ge(sem("late_summed"), c - N_ADA_1 + 1)
                pe.wait_ge(sem("mod_row"), c - 1)
                win = MIX[W[ADD_UP[c]]][1]
                wait(pe, "win_copied_a", win)
                wait(pe, "win_copied_d", win)
                pe.matmul(ps[sum_bank(c)][0:1, :], ones[:, :], late_sums(c % 2), start=True, stop=True)\
                    .then_inc(sem("ada_combined"), 1)

            def ada_unit(u4, q, k0, bank):
                for j in range(KQ):
                    if j % 2 == 0:
                        pe.wait_ge(sem("lo_made"), 8 * u4 + (2 * q + 1 + j // 2))
                    k = k0 + j
                    pe.matmul(ps[bank][0:4, :], cst[:, k, :], whi[:, q % 2, j, :], start=k == 0, stop=False)
                    m = pe.matmul(ps[bank][0:4, :], cst[:, k, :], wlo[:, q % 2, j, :], start=False, stop=k == 15)
                    if j % 2 == 1:
                        m.then_inc(sem("unit_used"), 1)

            def spread_row(c):
                rows_complete(c, c % 2)
                wait(pe, "mod_row", c)
                for v in range(2):
                    m = pe.matmul(ps[v][:, :], spread[:, v, :], rows_of(c % 2), start=True, stop=True)
                m.then_inc(sem("ada_combined"), 1)

            for c in range(N_ADA_1):
                wait(pe, "ada_rows", c - 1)
                for q in range(4):
                    ada_unit(c, q, 4 * q, 2 + c % 2)
                    if q == 1 and c:
                        spread_row(c - 1)
                    if q == 2 and c >= 5:
                        if c == 5:
                            pe.wait_ge(sem("na_bias_made"), 1)
                        turn_h_pe(pe, c - 5)
                if c == 0:
                    pe.wait_ge(sem("na_rpb_lo"), 1)
                    for j in range(64):
                        m = pe.matmul(ps[4 + j // 16][:, (j % 16) * 28:(j % 16) * 28 + 28], bandr[:, 63 - j:191 - j],
                                      narpbr[:, :], start=True, stop=True)
                    m.then_inc(sem("na_bands"), 1)

            spread_row(N_ADA_1 - 1)
            turn_h_pe(pe, 3)
            pe.wait_ge(sem("h_lo"), 16)
            pe.wait_ge(sem("memsets"), 3)
            for i, n in enumerate(W):
                u, (_, c, k) = U_MIX + n, MIX[n]
                for a in range(N_ADA_1, N_ADA):
                    if ADD_UP[a] == i:
                        add_up(a)
                col, w, cx = WIN[c]
                if k == 0:
                    wait(pe, "win_copied_a", c - 1)
                    wait(pe, "win_copied_d", c - 1)
                    if cx is not None:
                        wait(pe, "mod_row", N_ADA_1 + sum(ADD_UP[a] < i for a in ADD_UP))
                toks = (0, 1) if cx is None else (0, 1, 2, 3)
                b = 4 * (c % 2)
                unit(pe, u // 4, u % 4, ps[b:b + len(toks)], [XA, XB], 4 * k, k == 0, k == 3, w=w, toks=toks,
                     slot=i % 2, follow=FOLLOW[i])
            pe.wait_ge(sem("mod_row"), N_ADA)

            pe.wait_ge(sem("mla_normed"), 1)
            pe.wait_ge(sem("win_copied_a"), len(WIN))
            pe.wait_ge(sem("win_copied_d"), len(WIN))
            for i in range(2):
                for j in range(4):
                    pe.transpose(ps[i][:, j * P:j * P + P], PL[:, i, ML_Q + j * P:ML_Q + j * P + P], ident[:, :])
            for i in range(4):
                ckv = PL[:, i, ML_KV:ML_KV + 320] if i < 2 else PC[:, i - 2, CX_ML:CX_ML + 320]
                for j in range(2):
                    b = (i % 2) * 256 + j * P
                    pe.transpose(ps[2 + i // 2][:, b:b + P], ckv[:, j * P:j * P + P], ident[:, :])
                m = pe.transpose(ps[4][0:64, i * P:i * P + P], ckv[:, 256:320], ident[:, :])
            m.then_inc(sem("mla_turned"), 1)
            g = U_MLA // 4
            pe.wait_ge(sem("mla_lo"), 1)
            pe.wait_ge(sem("kpe_copied"), 1)
            unit(pe, g, 0, ps[0:2], XQ, 0, True, True)
            unit(pe, g, 1, ps[2:4], XQ, 0, True, True, w=256)
            unit(pe, g, 2, ps[4:8], XKV, 0, True, True, k=2, toks=(0, 1, 2, 3))
            pe.wait_ge(sem("mla_copied_a"), 1)
            pe.wait_ge(sem("mla_copied_d"), 1)
            unit(pe, g, 3, ps[0:4], XKV, 0, True, True, k=2, toks=(0, 1, 2, 3))
            pe.wait_ge(sem("mla_copied_a"), 2)
            pe.wait_ge(sem("mla_copied_d"), 2)
            pe.wait_ge(sem("rotated_pe"), 1)
            attn_pe(pe, A1, 0, len(STEPS), U_OUT, [4 * g for g in BY_HEADS])
            out_pe(pe, "x1_chunk", U_OUT, XA, BY_HEADS)

            def made(T):
                return lambda g, i: pe.wait_ge(sem(T + "_ready"), 2 * g + i + 1)
            tiles_y = [ybuf[:, i, :] for i in range(2)]
            start_pe(pe, "h2", tiles_y, U_FFN, 0, made("h2"), [(0, 1, 2), (3,), (), ()])

            def turn_3(q):
                if q >= 2:
                    turn_pe(pe, "h3", h3, q - 2, made("h3"))
            ffn_pe(pe, "ff1", U_FFN, N_FF, True, turn_3)
            start_pe(pe, "h3", h3, U_WIN2, 0, made("h3"), [(), (2,), (3,), ()])
            pe.wait_ge(sem("wf_lo"), 1)
            for k in range(16):
                pe.matmul(ps[4][0:8, 0:SEQ], wfh[:, k, :], XA[0][:, k, :], start=k == 0, stop=False)
                pe.matmul(ps[4][0:8, 0:SEQ], wfh[:, k, :], XA[1][:, k, :], start=False, stop=False)
                m = pe.matmul(ps[4][0:8, 0:SEQ], wfl[:, k, :], XA[0][:, k, :], start=False, stop=k == 15)
            m.then_inc(sem("f_acc"), 1)

            def qkv2(i, first=False):
                for b in range(2):
                    if first and b == 0:
                        continue
                    wait(pe, "qkv2_a", 2 * i + (b - 1))
                    wait(pe, "qkv2_d", 2 * i + (b - 1))
                    for q in range(4):
                        unit(pe, U_WIN2 // 4 + 2 * i + b, q, ps[2 * b:2 * b + 2], XA, 4 * q, q == 0, q == 3)
            qkv2(0, True)
            pe.wait_ge(sem("z_copied"), 1)
            for i in range(2):
                m = pe.transpose(ps[5][:, 8 * i:8 * i + 8], zT[:, i * P:i * P + P], ident[0:8, 0:8])
            m.then_inc(sem("z_turned"), 1)
            with pe.Fori(1, N_QKV2 // 2) as i:
                qkv2(i)
            pe.wait_ge(sem("qkv2_a"), N_QKV2)
            pe.wait_ge(sem("qkv2_d"), N_QKV2)
            pe.wait_ge(sem("nlf_made"), 1)
            pe.wait_ge(sem("masks_loaded"), 48)
            attn_pe(pe, A2, 0, len(STEPS2), U_MRG, [4 * g for g in IN_ORDER])

            def merge(n, first=False):
                g = 3 * n + U_MRG // 4
                wait(pe, "gate_sigmoid", n * 2)
                for b in range(first, 2):
                    for q in range(4):
                        unit(pe, g + b, q, ps[2 * b:2 * b + 2], XA, 4 * q, q == 0, q == 3)
                wait(pe, "merged_chunk", n)
                for q in range(4):
                    b = 4 if q < 2 else 6
                    unit(pe, g + 2, q, ps[b:b + 2], XB, 4 * q, q % 2 == 0, q % 2 == 1)
            merge(0, True)
            with pe.Fori(1, 4) as n:
                merge(n)

            def merged(g, i):
                pe.wait_ge(sem("gate_sigmoid"), 8)
                pe.wait_ge(sem("merged_chunk"), g + 1 if g < 2 else 4)
            start_pe(pe, "mrg", [mrg[:, i, :] for i in range(2)], U_OUT2, 0, merged, [(0, 1, 2), (3,), (), ()])
            out_pe(pe, "x3_chunk", U_OUT2, XB, IN_ORDER, lambda c: turn_pe(pe, "h4", tiles_y, c, made("h4")))
            pe.wait_ge(sem("x3_chunk"), 4)
            start_pe(pe, "h4", tiles_y, U_FFN2, 2, made("h4"), [(), (3,), (), ()])
            ffn_pe(pe, "ff2", U_FFN2, N_FF2, False)

        @block.gpsimd
        def _(pool):
            for dst, src in ((cos128, t["cos128"]), (sin128, t["sin128"]), (cos64, t["cos64"]), (sin64, t["sin64"])):
                pool.dma_start(dst[:, :, :], src).then_inc(sem("small_loaded"), 16)
            for dst, src, n in ((g_gq, t["gqa_gq"], 128), (g_gk, t["gqa_gk"], 128), (g_sub, t["diff_gsub"], 128),
                                (g_mq, t["mla_gq"], 512), (g_mkv, t["mla_gkv"], 256)):
                pool.dma_start(dst[:, :], bcast(src, n)).then_inc(sem("small_loaded"), 16)
            pool.dma_start(gvec[:, :], bcast(t["g_attn"], D)).then_inc(sem("g_attn_loaded"), 16)

            with nc.allow_non_contiguous_dma(reason="31 x 28 table, once"):
                pool.wait_ge(sem("memsets"), 2)
                for h in range(4):
                    for p in (0, 32):
                        pool.dma_start(narpb[p:p + 31, h * 7:h * 7 + 7], t["na_rpb"][0, h, 4:11, :].rearrange("r m -> m r"))\
                            .then_inc(sem("na_tables_loaded"), 16)
            pool.dma_start(band[:, :], t["na_band"]).then_inc(sem("na_tables_loaded"), 16)
            pool.dma_start(namask[:, :], t["na_mask"]).then_inc(sem("na_tables_loaded"), 16)
            rstd_pool(pool, "x", 4, "_squares")

            def modulate(q):
                cc = slice(q * NCH, (q + 1) * NCH)
                pool.wait_ge(sem("mod_row"), q + 1)
                for i in range(4):
                    m = pool.tensor_tensor(xin[:, i, cc], xin[:, i, cc], scale_g[:, i // 2, :], ALU.mult)
                m.then_inc(sem("x_modulated"), 1)
            pool.wait_ge(sem("x_scaled"), 1)
            modulate(0)
            pool.wait_ge(sem("na_bias_made"), 1)
            pool.dma_start(nab_d, nab_1[:, :, :, :]).then_inc(sem("na_bias_stored"), 16)
            for q in range(1, 4):
                modulate(q)

            def norm(x, g, width, n, col):
                pool_rstd(pool, stat(col, n), stat(col, n), n, width)
                pool.drain()
                pool.tensor_tensor(x, x, stat(col, n).rearrange("p (a b) -> p a b", b=1)
                                   .to_broadcast([P, n, width]), ALU.mult)
                pool.drain()
                pool.tensor_tensor(x, x, g[:, 0:width].rearrange("p (a b) -> p a b", a=1)
                                   .to_broadcast([P, n, width]), ALU.mult)
                pool.drain()

            def rope(x, cos, sin, half, n):
                a = ropeA[:, 0:2 * n * half].rearrange("p (n s h) -> p n s h", n=n, s=2)
                b = ropeB[:, 0:2 * n * half].rearrange("p (n s h) -> p n s h", n=n, s=2)
                for s in range(2):
                    c3 = cos.rearrange("p (a h) -> p a h", a=1).to_broadcast([P, n, half])
                    s3 = sin.rearrange("p (a h) -> p a h", a=1).to_broadcast([P, n, half])
                    pool.tensor_tensor(a[:, :, s, :], x[:, :, s, :], c3, ALU.mult)
                    pool.tensor_tensor(b[:, :, s, :], x[:, :, s, :], s3, ALU.mult)
                pool.drain()
                pool.tensor_tensor(x[:, :, 0, :], a[:, :, 0, :], b[:, :, 1, :], ALU.subtract)
                m = pool.tensor_tensor(x[:, :, 1, :], b[:, :, 0, :], a[:, :, 1, :], ALU.add)
                pool.drain()
                return m

            def copied(c):
                if c in WIN_SQ:
                    pool.wait_ge(sem("win_squared"), sorted(WIN_SQ).index(c) + 1)
                pool.wait_ge(sem("win_copied_a"), c + 1)
                pool.wait_ge(sem("win_copied_d"), c + 1)

            pool.wait_ge(sem("h_ready"), 16)
            for i, name in enumerate(("diff_lq1", "diff_lk1", "diff_lq2", "diff_lk2")):
                pool.dma_start(lamv[:, i, :], bcast(t[name], 64)).then_inc(sem("small_loaded"), 16)
            pool.wait_ge(sem("small_loaded"), 16 * 13)
            copied(0)
            for i in range(2):
                norm(PL[:, i:i + 1, ML_Q:ML_Q + 512], g_mq, 512, 1, NCQ + i)
            copied(1)
            for i in range(2):
                norm(PL[:, i:i + 1, ML_KV:ML_KV + 256], g_mkv, 256, 1, NCKV + i)
                norm(PC[:, i:i + 1, CX_ML:CX_ML + 256], g_mkv, 256, 1, NCKV + 2 + i)
                rope(PL[:, i, ML_PE:ML_PE + 64].rearrange("p (n s h) -> p n s h", n=1, s=2), cos64[:, i, :],
                     sin64[:, i, :], 32, 1)
            pool.drain().then_inc(sem("mla_normed"), 1)
            for c, col in ((2, DF_Q), (3, DF_K)):
                copied(c)
                for i in range(2):
                    rope(PL[:, i, col:col + 512].rearrange("p (n s h) -> p n s h", s=2, h=32), cos64[:, i, :],
                         sin64[:, i, :], 32, 8)
            copied(5)
            for i in range(2):
                norm(PL[:, i, GQ_Q:GQ_Q + 512].rearrange("p (n d) -> p n d", d=HD), g_gq, HD, 4, NGQ + 4 * i)
                rope(PL[:, i, GQ_Q:GQ_Q + 512].rearrange("p (n s h) -> p n s h", s=2, h=64), cos128[:, i, :],
                     sin128[:, i, :], 64, 4)
            copied(6)
            for i in range(2):
                norm(PL[:, i, GQ_K:GQ_K + 256].rearrange("p (n d) -> p n d", d=HD), g_gk, HD, 2, NGK + 2 * i)
                norm(PC[:, i, CX_GK:CX_GK + 256].rearrange("p (n d) -> p n d", d=HD), g_gk, HD, 2, NGK + 4 + 2 * i)
                rope(PL[:, i, GQ_K:GQ_K + 256].rearrange("p (n s h) -> p n s h", s=2, h=64), cos128[:, i, :],
                     sin128[:, i, :], 64, 2)
            pool.wait_ge(sem("mla_copied_a"), 1)
            pool.wait_ge(sem("mla_copied_d"), 1)
            for i in range(2):
                q = PL[:, i, ML_Q:ML_Q + 768].rearrange("p (n d) -> p n d", d=192)[:, :, 128:192]
                rope(q.rearrange("p n (s h) -> p n s h", s=2), cos64[:, i, :], sin64[:, i, :], 32, 4)
            pool.drain().then_inc(sem("rotated_pe"), 1)

            pool.wait_ge(sem("att_out"), 4)
            pool.wait_ge(sem("na_bias_stored"), 16)
            pool.dma_start(nabias[:, :, :, :], nab_d).then_inc(sem("na_bias_loaded"), 16)
            for h in range(4):
                pool.wait_ge(sem("diff_squares"), h + 1)
                pool_rstd(pool, stat(ORS, 2), stat(OSS, 2), 2, HD).then_inc(sem("diff_rstd"), 1)

            for b in range(2):
                pool.wait_ge(sem(f"late_mod_stored{b}"), 8 * (N_ADA - N_ADA_1))
            pool.wait_ge(sem("att_out"), 8)

            def row(dst, n, name):
                pool.dma_start(dst[:, :], bcast(mod_d[:, (n - 2) * D:(n - 1) * D], D)).then_inc(sem(name), 16)
            row(gt_a, 2, "x1_loaded")
            row(sc_f, 4, "x1_loaded")
            pool.wait_ge(sem("att_out_lo"), 16)
            pool.dma_start(x_one, x_v).then_inc(sem("x1_loaded"), 16)
            pool.dma_start(gvec[:, :], bcast(t["g_ffn"], D)).then_inc(sem("x1_loaded"), 16)
            row(sh_f, 3, "x1_gates_loaded")
            row(gt_f, 5, "x1_gates_loaded")
            rstd_pool(pool, "x1", 2, "_summed")
            pool.wait_ge(sem("x1_chunk"), 4)
            pool.dma_start(gt_a[:, :], bcast(t["g_final"].rearrange("(a n) -> a n", a=1), D))\
                .then_inc(sem("g_first_loaded"), 16)
            pool.wait_ge(sem("h2_ready"), 8)
            pool.dma_start(gvec[:, :], bcast(t["norm_mix_g_2"].rearrange("(a n) -> a n", a=1), D))\
                .then_inc(sem("g_mix_loaded"), 16)
            with nc.allow_non_contiguous_dma(reason="eight columns of w_in_2"):
                pool.dma_start(wf[:, :, :], t["w_in_2"].rearrange("(k p) n -> p k n", p=P)[:, :, 6144:6152])\
                    .then_inc(sem("wf_loaded"), 16)
            pool.dma_start(bf[:, :], bcast(t["b_forget_2"].rearrange("(a n) -> a n", a=1), 8)).then_inc(sem("wf_loaded"), 16)
            for dst, src in ((distm, t["distance"]), (causal, t["causal"]), (tri, t["triangle"])):
                pool.dma_start(dst[:, :, :], src).then_inc(sem("masks_loaded"), 16)
            pool.wait_ge(sem("g_first_loaded"), 16)
            pool.wait_ge(sem("g_mix_loaded"), 16)
            pool.tensor_tensor(gvec[:, :], gvec[:, :], gt_a[:, :], ALU.mult)
            pool.drain()
            for q in range(4):
                pool.wait_ge(sem("y_gated"), q + 1)
                cc = slice(q * NCH, (q + 1) * NCH)
                for i in range(2):
                    m = pool.tensor_tensor(x_one[:, i, cc], x_one[:, i, cc], ybuf[:, i, cc], ALU.add)
                m.then_inc(sem("xf_chunk"), 1)
                pool.drain()
                for i in range(2):
                    pool.tensor_tensor(h3[i][:, cc], x_one[:, i, cc], gvec[:, cc], ALU.mult).then_inc(sem("h3_ready"), 1)
                for i in range(2):
                    m = pool.tensor_tensor(ybuf[:, i, cc], x_one[:, i, cc], gt_a[:, cc], ALU.mult)
                m.then_inc(sem("xg_chunk"), 1)
            pool.wait_ge(sem("xf_summed"), 1)
            r1, r2, r12 = stat(RSTD + 2, 2), stat(SS + 2, 2), stat(RSTD, 2)
            pool_rstd(pool, r1, stat(SS, 2), 2, D)
            for k in range(2):
                pool.drain()
                pool.tensor_tensor(r2, r2, r1, ALU.mult)
            pool.drain()
            pool_rstd(pool, r2, r2, 2, D)
            pool.drain()
            pool.tensor_tensor(r12, r1, r2, ALU.mult).then_inc(sem("xf_rstd"), 1)
            pool.drain()
            for i in range(2):
                pool.tensor_tensor(xres[:, i, :], ybuf[:, i, :], stat(RSTD + 2 + i).to_broadcast([P, D]), ALU.mult)
            pool.drain().then_inc(sem("x2_made"), 1)
            pool.dma_start(x2_d, xres[:, :, :]).then_inc(sem("x2_stored"), 16)
            pool.wait_ge(sem("h3_ready"), 8)
            pool.dma_start(gvec[:, :], bcast(t["norm_mlp_g_2"].rearrange("(a n) -> a n", a=1), D))\
                .then_inc(sem("g_mlp_loaded"), 16)
            pool.wait_ge(sem("x2_stored"), 16)
            pool.wait_ge(sem("att2_out_lo"), 16)
            pool.dma_start(xres[:, :, :], x2_d).then_inc(sem("x3_loaded"), 16)
            rstd_pool(pool, "x3", 2, "_summed", RSTD3)
            pool.wait_ge(sem("h4_ready"), 8)
            pool.dma_start(gvec[:, :], bcast(t["norm_final_g_2"].rearrange("(a n) -> a n", a=1), D))\
                .then_inc(sem("g_final_loaded"), 16)
            rstd_pool(pool, "x4", 2, "_summed")


_INS = ["x", "c", "ctx", "c_ctx", "w_ada", "b_ada", "g_attn", "g_ffn", "w_in", "w_out", "na_rpb", "gqa_gq",
        "gqa_gk", "mla_gq", "mla_gkv", "mla_wuq", "mla_wukv", "diff_lq1", "diff_lk1", "diff_lq2", "diff_lk2",
        "diff_gsub", "ffn_wg", "ffn_wu", "ffn_wd", "g_final", "norm_mix_g_2", "w_in_2", "b_forget_2", "w_proj_a_2",
        "w_proj_b_2", "w_out_2", "norm_mlp_g_2", "w_up_2", "w_down_2", "norm_final_g_2"]


def constants():
    tok = np.arange(SEQ)
    row, col = (tok // 64).astype(np.float32), (tok % 64).astype(np.float32)

    def rope(dim):
        axis = dim // 2
        inv = (1.0 / (np.float32(10000.0) ** (np.arange(0, axis, 2, dtype=np.float32) / np.float32(axis)))).astype(np.float32)
        ang = np.concatenate([row[:, None] * inv, col[:, None] * inv], axis=-1).astype(np.float32)
        tile = lambda a: np.ascontiguousarray(a.reshape(2, P, -1).transpose(1, 0, 2).astype(np.float32))
        return tile(np.cos(ang)), tile(np.sin(ang))
    cos128, sin128 = rope(128)
    cos64, sin64 = rope(64)
    select = np.zeros((5, 2), np.float32)
    select[[0, 1, 4], 0] = 1
    select[[2, 3, 4], 1] = 1
    spread = np.ascontiguousarray(np.repeat(select[:, :, None], P, axis=2))
    c, j = np.arange(P) % 64, np.arange(64)
    start = np.clip(c - 8, 0, 48)
    inside = (j[None] >= start[:, None]) & (j[None] < start[:, None] + 16)
    na_mask = np.where(inside, 0.0, -1e30).astype(np.float32)
    m, y = np.arange(31)[:, None], np.arange(191)[None] - 63
    na_band = np.zeros((63, 191), np.float32)
    na_band[0:31] = na_band[32:63] = (m == 15 - y) | (m == 79 - y)
    q = np.arange(SEQ)
    dist = (q[:, None] - q[None, :]).astype(np.float32)
    tiles = lambda a: np.ascontiguousarray(a.astype(np.float32).reshape(2, P, SEQ).transpose(1, 0, 2))
    return {"identity": np.eye(P, dtype=np.float32), "row_spread": spread, "cos128": cos128, "sin128": sin128,
            "cos64": cos64, "sin64": sin64, "na_mask": na_mask, "na_band": na_band,
            "distance": tiles(np.where(dist >= 0, dist, 1e30)), "causal": tiles(np.where(dist >= 0, 0.0, -1e30)),
            "triangle": tiles(q[:, None] <= q[None, :])}


def kernel(**inputs):
    import concourse.bacc as bacc
    from concourse.bass_utils import run_bass_kernel_spmd

    nc = bacc.Bacc("TRN2", target_bir_lowering=False, num_devices=1)
    arrays, t = {}, {}
    for name, a in [(n, inputs[n]) for n in _INS] + list(constants().items()):
        a = np.ascontiguousarray(a)
        arrays[f"in_{name}"] = a
        t[name] = nc.dram_tensor(f"in_{name}", a.shape, mybir.dt.from_np(a.dtype), kind="ExternalInput").ap()
    t["out"] = nc.dram_tensor("out_x", (1, SEQ, D), F32, kind="ExternalOutput").ap()
    build(nc, t)
    r = run_bass_kernel_spmd(nc, [arrays], core_ids=[0])
    return r.results[0]["out_x"]
```
